# Optimizing a Trainium2 kernel written in Bass

```python
import jax, jax.numpy as jnp
from jax import lax
import numpy as np

D_MODEL = 1024
BATCH = 1
SEQ = 128
DEPTH = 1
DEC_BATCH = 1
DEC_SEQ = 256
PAST_LEN = 128

GRID_W = 64
EPS = 1e-6
GLA_HEADS = 4
GLA_DK = 64
GLA_DV = 128
GLA_GATE_RANK = 16
GLA_GATE_NORM = 16.0
GLA_CHUNK = 32
GLA_KEY_W = GLA_HEADS * GLA_DK
GLA_VAL_W = GLA_HEADS * GLA_DV
MLA_HEADS = 4
Q_LORA = 256
KV_LORA = 128
NOPE_DIM = 64
ROPE_DIM = 32
V_DIM = 128
QK_DIM = NOPE_DIM + ROPE_DIM
MLA_OUT_W = MLA_HEADS * V_DIM
ROPE_THETA = 10000.0
ATTN_BLOCK = 128
MIX_W = GLA_VAL_W + MLA_OUT_W
IN_WIDTHS = (GLA_KEY_W, GLA_KEY_W, GLA_VAL_W, GLA_VAL_W, GLA_GATE_RANK, GLA_GATE_RANK, Q_LORA, KV_LORA, ROPE_DIM)
D_IN = sum(IN_WIDTHS)
N_EXPERTS = 64
TOP_K = 8
N_GROUPS = 8
TOPK_GROUPS = 4
D_EXPERT = 256
ROUTED_SCALE = 2.5
MOE_BLOCK = 128

kernel_name = 'hybrid_gla_mla_moe_diffusion_step'

def rmsnorm(x, g):
    xf = x.astype(jnp.float32)
    xf = xf * lax.rsqrt(jnp.mean(xf * xf, axis=-1, keepdims=True) + EPS)
    return xf.astype(x.dtype) * g

def to_heads(x, n_heads):
    b, l, w = x.shape
    return x.reshape(b, l, n_heads, w // n_heads).transpose(0, 2, 1, 3)

def grid_positions(length):
    rows = length // GRID_W
    r = jnp.repeat(jnp.arange(rows, dtype=jnp.float32), GRID_W)
    col = jnp.tile(jnp.arange(GRID_W, dtype=jnp.float32), rows)
    return r, col

def rope1d(x, pos):
    half = x.shape[-1] // 2
    inv_freq = ROPE_THETA ** (-jnp.arange(half, dtype=jnp.float32) / half)
    ang = (pos[:, None] * inv_freq[None, :])[:, None, :]
    cos, sin = jnp.cos(ang).astype(x.dtype), jnp.sin(ang).astype(x.dtype)
    x1, x2 = x[..., :half], x[..., half:]
    return jnp.concatenate([x1 * cos - x2 * sin, x1 * sin + x2 * cos], axis=-1)

def axial_rope(x, rows, cols):
    nope, rot = x[..., :NOPE_DIM], x[..., NOPE_DIM:]
    a = ROPE_DIM // 2
    rot = jnp.concatenate([rope1d(rot[..., :a], rows), rope1d(rot[..., a:], cols)], axis=-1)
    return jnp.concatenate([nope, rot], axis=-1)

def gla_chunked(q, k, v, logg, s0):
    b_, h_, l_, dk = q.shape
    dv = v.shape[-1]
    n = l_ // GLA_CHUNK
    qc = q.reshape(b_, h_, n, GLA_CHUNK, dk)
    kc = k.reshape(b_, h_, n, GLA_CHUNK, dk)
    vc = v.reshape(b_, h_, n, GLA_CHUNK, dv)
    cum = jnp.cumsum(logg.astype(jnp.float32).reshape(b_, h_, n, GLA_CHUNK, dk), axis=3)
    causal = jnp.tril(jnp.ones((GLA_CHUNK, GLA_CHUNK), dtype=bool))[:, :, None]
    rel = cum[:, :, :, :, None, :] - cum[:, :, :, None, :, :]
    decay = jnp.exp(jnp.where(causal, rel, -jnp.inf))
    attn = jnp.einsum('bhnijd,bhnjd->bhnij', qc[:, :, :, :, None, :] * decay, kc)
    o_intra = jnp.einsum('bhnij,bhnjv->bhniv', attn, vc)
    cum_last = cum[:, :, :, -1:, :]
    u = jnp.einsum('bhncd,bhncv->bhndv', kc * jnp.exp(cum_last - cum), vc).astype(jnp.float32)
    chunk_decay = jnp.exp(cum_last[:, :, :, 0, :])

    def step(s, inp):
        dec, upd = inp
        return dec[..., None] * s + upd, s

    s_final, s_enter = lax.scan(step, s0.astype(jnp.float32),
                                (jnp.moveaxis(chunk_decay, 2, 0), jnp.moveaxis(u, 2, 0)))
    s_enter = jnp.moveaxis(s_enter, 0, 2)
    o_inter = jnp.einsum('bhncd,bhndv->bhncv', qc * jnp.exp(cum), s_enter)
    o = (o_intra + o_inter).reshape(b_, h_, l_, dv)
    return o.astype(v.dtype), s_final.astype(v.dtype)

def mla_keys_values(ckv_n, krope, lp):
    b_, l_, _ = ckv_n.shape
    kv = (ckv_n @ lp['w_ukv']).reshape(b_, l_, MLA_HEADS, NOPE_DIM + V_DIM)
    k_rope = jnp.broadcast_to(krope[:, :, None, :], (b_, l_, MLA_HEADS, ROPE_DIM))
    k = rmsnorm(jnp.concatenate([kv[..., :NOPE_DIM], k_rope], axis=-1), lp['g_qk_k'])
    return k, kv[..., NOPE_DIM:]

def block_attention(q, k, v):
    b_, l_, h_, dk = q.shape
    nb = l_ // ATTN_BLOCK
    qb = (q * dk ** -0.5).reshape(b_, nb, ATTN_BLOCK, h_, dk).transpose(1, 0, 3, 2, 4)

    def one_block(qblk):
        s = jnp.einsum('bhqd,bkhd->bhqk', qblk, k).astype(jnp.float32)
        p = jax.nn.softmax(s, axis=-1).astype(v.dtype)
        return jnp.einsum('bhqk,bkhd->bqhd', p, v)

    o = lax.map(one_block, qb)
    return o.transpose(1, 0, 2, 3, 4).reshape(b_, l_, h_, v.shape[-1])

def token_mixers(h, lp, s0_f, s0_b, ctx_ckv, ctx_krope):
    b_, l_, _ = h.shape
    split_idx = np.cumsum(IN_WIDTHS)[:-1].tolist()
    q_g, k_g, v_g, g_g, lr_f, lr_b, cq, ckv, krope = jnp.split(h @ lp['w_in'], split_idx, axis=-1)
    q_g = to_heads(q_g, GLA_HEADS) * GLA_DK ** -0.5
    k_g = to_heads(k_g, GLA_HEADS)
    v_g = to_heads(v_g, GLA_HEADS)
    logg_f = to_heads(jax.nn.log_sigmoid((lr_f @ lp['w_gk_fwd'] + lp['b_gk_fwd']).astype(jnp.float32)) / GLA_GATE_NORM, GLA_HEADS)
    logg_b = to_heads(jax.nn.log_sigmoid((lr_b @ lp['w_gk_bwd'] + lp['b_gk_bwd']).astype(jnp.float32)) / GLA_GATE_NORM, GLA_HEADS)
    o_f, s_f = gla_chunked(q_g, k_g, v_g, logg_f, s0_f)
    flip = lambda t: jnp.flip(t, axis=2)
    o_b, s_b = gla_chunked(flip(q_g), flip(k_g), flip(v_g), flip(logg_b), s0_b)
    o_g = (o_f + flip(o_b)).transpose(0, 2, 1, 3)
    o_g = rmsnorm(o_g, lp['g_gla_out']) * jax.nn.silu(g_g.reshape(b_, l_, GLA_HEADS, GLA_DV))
    ckv_n = rmsnorm(ckv, lp['g_kv_lora'])
    q_m = (rmsnorm(cq, lp['g_q_lora']) @ lp['w_uq']).reshape(b_, l_, MLA_HEADS, QK_DIM)
    q_m = rmsnorm(q_m, lp['g_qk_q'])
    k_m, v_m = mla_keys_values(ckv_n, krope, lp)
    if ctx_ckv is not None:
        rows, cols = grid_positions(l_)
        q_m = axial_rope(q_m, rows, cols)
        k_m = axial_rope(k_m, rows, cols)
        k_c, v_c = mla_keys_values(ctx_ckv, ctx_krope, lp)
        k_m = jnp.concatenate([k_m, k_c], axis=1)
        v_m = jnp.concatenate([v_m, v_c], axis=1)
    o_m = block_attention(q_m, k_m, v_m)
    mixed = jnp.concatenate([o_g.reshape(b_, l_, GLA_VAL_W), o_m.reshape(b_, l_, MLA_OUT_W)], axis=-1)
    return mixed @ lp['w_out'], s_f, s_b, ckv_n, krope

def moe(h, lp):
    b_, l_, d = h.shape
    t = h.reshape(-1, d)
    n_tok = t.shape[0]
    scores = jax.nn.sigmoid((t @ lp['w_router']).astype(jnp.float32))
    sel = scores + lp['b_router'].astype(jnp.float32)
    grp_score = lax.top_k(sel.reshape(n_tok, N_GROUPS, N_EXPERTS // N_GROUPS), 2)[0].sum(-1)
    _, top_g = lax.top_k(grp_score, TOPK_GROUPS)
    g_mask = jax.nn.one_hot(top_g, N_GROUPS, dtype=jnp.float32).sum(-2) > 0
    e_mask = jnp.repeat(g_mask, N_EXPERTS // N_GROUPS, axis=-1)
    _, top_e = lax.top_k(jnp.where(e_mask, sel, -jnp.inf), TOP_K)
    w = jnp.take_along_axis(scores, top_e, axis=-1)
    w = w / jnp.sum(w, axis=-1, keepdims=True) * ROUTED_SCALE
    gates = jnp.sum(jax.nn.one_hot(top_e, N_EXPERTS, dtype=jnp.float32) * w[..., None], axis=-2)
    nb = n_tok // MOE_BLOCK

    def block(args):
        tb, gb = args
        a = jax.nn.silu(jnp.einsum('td,edf->tef', tb, lp['w_exp_gate'])) * jnp.einsum('td,edf->tef', tb, lp['w_exp_up'])
        a = a * gb[:, :, None].astype(a.dtype)
        return jnp.einsum('tef,efd->td', a, lp['w_exp_down'])

    routed = lax.map(block, (t.reshape(nb, MOE_BLOCK, d), gates.reshape(nb, MOE_BLOCK, N_EXPERTS))).reshape(n_tok, d)
    shared = (jax.nn.silu(t @ lp['w_sh_gate']) * (t @ lp['w_sh_up'])) @ lp['w_sh_down']
    return (routed + shared).reshape(b_, l_, d)

def adaln_layer(x, mod, lp, s0_f, s0_b, ctx_ckv, ctx_krope):
    sh1, sc1, gt1, sh2, sc2, gt2 = jnp.split(mod, 6, axis=-1)
    h = rmsnorm(x, lp['g_norm1']) * (1 + sc1) + sh1
    mix, s_f, s_b, ckv_n, krope = token_mixers(h, lp, s0_f, s0_b, ctx_ckv, ctx_krope)
    x = x + gt1 * mix
    h = rmsnorm(x, lp['g_norm2']) * (1 + sc2) + sh2
    x = x + gt2 * moe(h, lp)
    return x, s_f, s_b, ckv_n, krope

def setup_inputs(seed: int = 0) -> dict:
    key = jax.random.key(seed)
    ks = iter(jax.random.split(key, 40))
    nrm = lambda shape, scale: jax.random.normal(next(ks), shape, jnp.float32) * scale
    gain = lambda shape: 1.0 + nrm(shape, 0.02)
    D, L = D_MODEL, DEPTH
    return {
        'x_prompt': nrm((BATCH, SEQ, D), 1.0),
        'x_sample': nrm((DEC_BATCH, DEC_SEQ, D), 1.0),
        'c': nrm((DEC_BATCH, D), 1.0),
        'state_gla_fwd': nrm((DEC_BATCH, L, GLA_HEADS, GLA_DK, GLA_DV), 0.5),
        'state_gla_bwd': nrm((DEC_BATCH, L, GLA_HEADS, GLA_DK, GLA_DV), 0.5),
        'cache_mla_ckv': nrm((DEC_BATCH, L, PAST_LEN, KV_LORA), 1.0),
        'cache_mla_krope': nrm((DEC_BATCH, L, PAST_LEN, ROPE_DIM), 1.0),
        'c_ctx': nrm((D,), 1.0),
        'w_ada': nrm((L, D, 6 * D), 0.5 * D ** -0.5),
        'b_ada': nrm((L, 6 * D), 0.02),
        'g_norm1': gain((L, D)),
        'g_norm2': gain((L, D)),
        'w_in': nrm((L, D, D_IN), D ** -0.5),
        'w_gk_fwd': nrm((L, GLA_GATE_RANK, GLA_KEY_W), GLA_GATE_RANK ** -0.5),
        'b_gk_fwd': nrm((L, GLA_KEY_W), 0.1),
        'w_gk_bwd': nrm((L, GLA_GATE_RANK, GLA_KEY_W), GLA_GATE_RANK ** -0.5),
        'b_gk_bwd': nrm((L, GLA_KEY_W), 0.1),
        'g_gla_out': gain((L, GLA_DV)),
        'g_q_lora': gain((L, Q_LORA)),
        'w_uq': nrm((L, Q_LORA, MLA_HEADS * QK_DIM), Q_LORA ** -0.5),
        'g_kv_lora': gain((L, KV_LORA)),
        'w_ukv': nrm((L, KV_LORA, MLA_HEADS * (NOPE_DIM + V_DIM)), KV_LORA ** -0.5),
        'g_qk_q': gain((L, QK_DIM)),
        'g_qk_k': gain((L, QK_DIM)),
        'w_out': nrm((L, MIX_W, D), MIX_W ** -0.5),
        'w_router': nrm((L, D, N_EXPERTS), D ** -0.5),
        'b_router': nrm((L, N_EXPERTS), 0.01),
        'w_exp_gate': nrm((L, N_EXPERTS, D, D_EXPERT), D ** -0.5),
        'w_exp_up': nrm((L, N_EXPERTS, D, D_EXPERT), D ** -0.5),
        'w_exp_down': nrm((L, N_EXPERTS, D_EXPERT, D), D_EXPERT ** -0.5),
        'w_sh_gate': nrm((L, D, D_EXPERT), D ** -0.5),
        'w_sh_up': nrm((L, D, D_EXPERT), D ** -0.5),
        'w_sh_down': nrm((L, D_EXPERT, D), D_EXPERT ** -0.5),
    }

def reference(x_prompt, x_sample, c, state_gla_fwd, state_gla_bwd, cache_mla_ckv, cache_mla_krope,
              c_ctx, w_ada, b_ada, g_norm1, g_norm2, w_in, w_gk_fwd, b_gk_fwd, w_gk_bwd, b_gk_bwd,
              g_gla_out, g_q_lora, w_uq, g_kv_lora, w_ukv, g_qk_q, g_qk_k, w_out,
              w_router, b_router, w_exp_gate, w_exp_up, w_exp_down, w_sh_gate, w_sh_up, w_sh_down):
    xp, xs = x_prompt, x_sample
    new_f, new_b, new_ckv, new_kr = [], [], [], []
    for l in range(DEPTH):
        lp = {'g_norm1': g_norm1[l], 'g_norm2': g_norm2[l], 'w_in': w_in[l],
              'w_gk_fwd': w_gk_fwd[l], 'b_gk_fwd': b_gk_fwd[l], 'w_gk_bwd': w_gk_bwd[l], 'b_gk_bwd': b_gk_bwd[l],
              'g_gla_out': g_gla_out[l], 'g_q_lora': g_q_lora[l], 'w_uq': w_uq[l],
              'g_kv_lora': g_kv_lora[l], 'w_ukv': w_ukv[l], 'g_qk_q': g_qk_q[l], 'g_qk_k': g_qk_k[l],
              'w_out': w_out[l], 'w_router': w_router[l], 'b_router': b_router[l],
              'w_exp_gate': w_exp_gate[l], 'w_exp_up': w_exp_up[l], 'w_exp_down': w_exp_down[l],
              'w_sh_gate': w_sh_gate[l], 'w_sh_up': w_sh_up[l], 'w_sh_down': w_sh_down[l]}
        mod_ctx = (jax.nn.silu(c_ctx) @ w_ada[l] + b_ada[l])[None, None, :]
        mod_lat = (jax.nn.silu(c) @ w_ada[l] + b_ada[l])[:, None, :]
        zeros = jnp.zeros((xp.shape[0], GLA_HEADS, GLA_DK, GLA_DV), jnp.float32)
        xp, s_f, s_b, ckv_n, kr = adaln_layer(xp, mod_ctx, lp, zeros, zeros, None, None)
        new_f.append(s_f)
        new_b.append(s_b)
        new_ckv.append(ckv_n)
        new_kr.append(kr)
        xs, _, _, _, _ = adaln_layer(xs, mod_lat, lp, state_gla_fwd[:, l], state_gla_bwd[:, l],
                                     cache_mla_ckv[:, l], cache_mla_krope[:, l])
    return (xp, xs, jnp.stack(new_f, axis=1), jnp.stack(new_b, axis=1),
            jnp.stack(new_ckv, axis=1), jnp.stack(new_kr, axis=1))


_drawn_inputs = setup_inputs


def setup_inputs(seed=0):
    import zlib

    import numpy as np

    out = dict(_drawn_inputs(seed))
    spreads = {}
    factors = {'state_gla_fwd': 8.0,
     'state_gla_bwd': 6.768,
     'cache_mla_krope': 3.385,
     'g_gla_out': 12.898,
     'g_q_lora': 8.0,
     'g_kv_lora': 2.964,
     'g_qk_q': 8.0,
     'g_qk_k': 8.0,
     'g_norm2': 4.325}
    for name, (base, spread) in spreads.items():
        noise = np.random.default_rng([zlib.crc32(name.encode()), seed]).standard_normal(out[name].shape)
        drawn = base * np.exp(spread * noise) if base else spread * noise
        out[name] = __import__('jax').numpy.asarray(drawn.astype(out[name].dtype))
    for name, factor in factors.items():
        out[name] = (out[name] * factor).astype(out[name].dtype)
    return out
```

```python
from contextlib import ExitStack

import numpy as np
import concourse.bass as bass
from concourse import mybir

F32 = mybir.dt.float32
F32R = mybir.dt.float32r
BF16 = mybir.dt.bfloat16
I32 = mybir.dt.int32
ALU = mybir.AluOpType
ACT = mybir.ActivationFunctionType
AX = mybir.AxisListType

P = 128
D = 1024
NC = D // P
NT = 3
TOK = NT * P
EPS = 1e-6
GH, GDK, GDV = 4, 64, 128
MH, NOPE, ROPE, VD = 4, 64, 32, 128
QK = NOPE + ROPE
QL, KL = 256, 128
NE, NG, TOPG, TOPK, DE = 64, 8, 4, 8, 256
SCALE_OUT = 2.5
GATE_NORM = 16.0
GRID_W = 64
THETA = 10000.0
SLOT = 64
JG = 4
NOVER = 48
NJ = NE + NOVER


def shape_constants():
    i = np.arange(P)
    ident = np.eye(P, dtype=np.float32)
    before = (i[:, None] <= i[None, :]).astype(np.float32)
    after = (i[:, None] >= i[None, :]).astype(np.float32)
    strict = (i[:, None] < i[None, :]).astype(np.float32)
    half = ROPE // 4
    freq = THETA ** (-np.arange(half, dtype=np.float32) / half)
    pos = np.arange(2 * P)
    ang = np.stack([(pos // GRID_W)[:, None] * freq, (pos % GRID_W)[:, None] * freq], 1)
    ang = ang.astype(np.float32)
    cos, sin = np.cos(ang), np.sin(ang)
    c = np.stack([cos, cos], 2).reshape(2, P, ROPE).transpose(1, 0, 2).reshape(P, 2 * ROPE)
    s = np.stack([-sin, sin], 2).reshape(2, P, ROPE).transpose(1, 0, 2).reshape(P, 2 * ROPE)
    slot = np.broadcast_to((np.arange(JG * SLOT) % SLOT).astype(np.float32), (P, JG * SLOT))
    earlier = np.broadcast_to((np.arange(NG)[None, :] < np.arange(NG)[:, None]).reshape(1, NG * NG), (P, NG * NG))
    over = np.broadcast_to(np.arange(NOVER).astype(np.float32), (P, NOVER))
    sel = np.zeros((P, 2, P), np.float32)
    sel[0, 0] = sel[1, 1] = 1.0
    return np.ascontiguousarray(np.concatenate(
        [ident, before, after, strict, c, s, slot, earlier, over, i[:, None], sel.reshape(P, 2 * P),
         np.ones((P, P))], 1).astype(np.float32))


CW = {}
_o = 0
for _n, _w in (("ident", P), ("before", P), ("after", P), ("strict", P), ("cos", 2 * ROPE), ("sin", 2 * ROPE),
               ("slot", JG * SLOT), ("earlier", NG * NG), ("over", NOVER), ("index", 1), ("sel", 2 * P), ("ones", P)):
    CW[_n] = (_o, _w)
    _o += _w
CONST_W = _o

RW = {}
_o = 0
for _n, _w in (("g_gla_out", GDV), ("g_q_lora", QL), ("g_kv_lora", KL), ("g_qk_q", QK), ("g_qk_k", QK), ("b_router", NE)):
    RW[_n] = (_o, _w)
    _o += _w
ROW_W = _o

SPLITS = (("gu", 1), ("gu", 2), ("dn", 0), ("gu", 3), ("dn", 1), ("gu", 4), ("dn", 2), ("dn", 3))


KB = 1024


def rows_pc(w, n):
    return w.rearrange("(p c) n -> p c n", c=NC)


def build(nc, A, O, stop=None):
    ctx = ExitStack()
    with ctx:
        base = (nc.sbuf_base + 63) // 64 * 64

        def at(name, off, shape, dt=F32):
            return nc.alloc_sbuf_tensor_at(name, shape, dt, offset=base + int(off * KB))

        def sem(name):
            return ctx.enter_context(nc.semaphore(name))

        keep = at("keep", 0, [P, 3 * P + JG * SLOT])
        small = at("small", 2.5, [P, 600])
        x_sb = at("x_sb", 10, [P, NT, D])
        prob = at("prob", 10, [P, MH, TOK])
        cqT = at("cqT", 16, [P, 2, TOK])
        ckvnT = at("ckvnT", 19, [P, 4 * P])
        hT = at("hT", 22, [P, NC, TOK])
        probT = at("probT", 22, [P, MH, NT, P])
        prob0 = at("prob0", 28, [P, MH, P])
        prob0T = at("prob0T", 30, [P, MH, P])
        mixedT = at("mixedT", 22, [P, NC, TOK])
        mixed = at("mixed", 34, [P, NT, D])
        mla = at("mla", 46, [P, NT, QL + KL + ROPE])
        val = at("val", 50.875, [P, 4, MH, VD])
        key = at("key", 58.875, [P, 4, MH, QK])
        qry = at("qry", 64.875, [P, NT, MH, QK])
        keyT = at("keyT", 69.375, [QK, MH, 4 * P])
        qryT = at("qryT", 77.375, [QK, MH, TOK])
        tconst = at("tconst", 83.375, [P, CONST_W - 3 * P - JG * SLOT])
        rows = at("rows", 87.25, [P, ROW_W])
        krope = at("krope", 90.25, [P, 4, ROPE])
        ckvn = at("ckvn", 90.75, [P, 4, KL])
        cols = at("cols", 92.75, [P, 80])
        w_mla = at("w_mla", 94, [P, NC, 448])
        w_qk = at("w_qk", 108, [P, NC, 512])
        w_v = at("w_v", 124, [P, NC, 512])
        w_g = at("w_g", 140, [P, NC, 512])
        w_out = at("w_out", 124, [P, NC, D])
        decay_p = at("decay_p", 94, [P, 4, TOK])
        decay_m = at("decay_m", 100, [P, 4, TOK])
        kend = at("kend", 106, [P, 4, 2, P])
        kendT = at("kendT", 110, [P, 4, 2, P])
        attn = at("attn", 114, [P, 2, 2, 2, P])
        state0 = at("state0", 118, [P, 2, 2, GDV])
        state1 = at("state1", 120, [P, 4, 2, GDV])
        ada1 = at("ada1", 156, [P, 4, 2 * D])
        ada2 = at("ada2", 156, [P, NC, 256])
        w_uq = at("w_uq", 164, [P, 2, MH * QK])
        w_ukv = at("w_ukv", 167, [P, MH * (NOPE + VD)])
        modrow = at("modrow", 171, [2, 4 * D])
        v_sb = at("v_sb", 187, [P, NT, GH * GDV])
        g_sb = at("g_sb", 193, [P, NT, GH * GDV])
        qkT = at("qkT", 199, [P, 4, TOK])
        stateP = at("stateP", 199, [P, 2, 2, GH, GDV])
        mod1 = at("mod1", 34, [2, 2 * D])
        sq = at("sq", 42, [P, D])
        sq2 = at("sq2", 34, [P, 4 * MH * QK])
        osq = at("osq", 10, [P, GH * GDV])
        gexp = at("gexp", 16, [P, NT, GH * GDV])

        ident, strict, ones = (keep[:, k * P:(k + 1) * P] for k in range(3))
        slotrow = keep[:, 3 * P:3 * P + JG * SLOT]
        TCW, o = {}, 0
        for n, (_, w) in CW.items():
            if n not in ("ident", "strict", "ones", "slot"):
                TCW[n] = (o, w)
                o += w

        def tc(n):
            return tconst[:, TCW[n][0]:TCW[n][0] + TCW[n][1]]

        def row(n):
            return rows[:, RW[n][0]:RW[n][0] + RW[n][1]]

        small_used = [0]

        def sm(*shape):
            n = int(np.prod(shape))
            a = small[:, small_used[0]:small_used[0] + n]
            small_used[0] += n
            if len(shape) == 2:
                a = a.rearrange("p (a b) -> p a b", b=shape[1])
            if len(shape) == 3:
                a = a.rearrange("p (a b c) -> p a b c", b=shape[1], c=shape[2])
            return a

        ccol = cols[:, 0:16].rearrange("p (s c) -> p s c", s=2)
        g1col = cols[:, 16:24]
        bcol = cols[:, 24:40].rearrange("p (j c) -> p j c", j=2)
        gkcol = cols[:, 40:44]
        silu_c = sm(NC, 2)
        cexp = sm(2, NC)
        ss1 = sm(NT)
        v1 = sm(NT)
        r1 = sm(NT)
        t1 = sm(NT)
        modc = sm(2 * NC, 2)
        scale1 = sm(NC, 2)
        wgk = at("wgk", 5.5, [32, 2, 2, P])
        lrT = at("lrT", 7.5, [32, TOK])
        ss2, v2, r2, t2 = sm(2, NT), sm(2, NT), sm(2, NT), sm(2, NT)
        ssk, vk, rk, tk = sm(4, MH), sm(4, MH), sm(4, MH), sm(4, MH)
        ssq, vq, rq, tq = sm(NT, MH), sm(NT, MH), sm(NT, MH), sm(NT, MH)
        sso, vo, ro, to = sm(NT, MH), sm(NT, MH), sm(NT, MH), sm(NT, MH)
        nmax, psum_p, rden = sm(NT, MH), sm(NT, MH), sm(NT, MH)
        gsm = sm(3, 12)
        gex = sm(3, 12)
        gtot = sm(2, NT)
        gqs = at("gqs", 9.0, [P, QK])

        ps = ctx.enter_context(nc.psum_tensor("ps", [P, 8, 512], F32))

        names = ("consts_in x_in cols_in ada1_in w_mla_in w_qk_in w_v_in w_g_in w_u_in cache_in state_in brow_in ada2_in "
                 "w_out_in silu_ready mod1_done mod1_sb modT_done mod_sb xn_ready h_ready xT_done xT_sb proj_done proj_sb "
                 "ada1_used misc_done misc_sb rn_in rn_ln rn_out cqn_ready ckv_ready gate_e gate_l gate_d decay_ready sm_in sm_ready qe_ready kend_ready smp_ready "
                 "krope_ready kr_sb key_ready qry_ready sqk_in max_ready prob_ready rden_ready o_sq silu_g mix_ready "
                 "ada2_done ada2_sb dve_chain act_chain pool_chain out_done zero_ready gate_abs g1_ready mix_done").split()
        S = {n: sem(n) for n in names}
        ada1_in = [sem(f"ada1_in{k}") for k in range(4)]
        gt1 = at("gt1", 94, [P, 2, D])
        mul2 = at("mul2", 102, [P, 2, D])
        add2 = at("add2", 110, [P, 2, D])
        xtmp = at("xtmp", 118, [P, D])
        w_router = at("w_router", 122, [P, NC, NE])
        x1 = at("x1", 188, [P, NT, D])
        sq3 = at("sq3", 200, [P, D])
        g2row = at("g2row", 58, [P, D])
        h2 = at("h2", 34, [P, NT, D])
        h2T = at("h2T", 46, [P, NC, TOK])
        h2h = at("h2h", 10, [P, NT, NC, P], F32R)
        h2l = at("h2l", 22, [P, NT, NC, P], F32R)
        w_shgu = at("w_shgu", 156, [P, 2, NC, DE])
        w_shd = at("w_shd", 172, [P, 2, D])
        sh_sil = at("sh_sil", 180, [P, DE])
        sh_a = [at(f"sh_a{t}", 181 + t, [P, DE]) for t in range(NT)]
        sh_aT = at("sh_aT", 185.25, [P, 2, P])
        acc = at("acc", 34, [P, NT, D])
        rt = at("rt", 142, [P, 3500])
        rtb = at("rtb", 184, [P, 3 * NE + 3 * P], BF16)
        NJP = NJ + JG
        posj = at("posj", 5.5, [P, NT, NJP])
        gparts = at("gparts", 7, [P, NT, NJP, 3], BF16)
        jobs = at("jobs", 9.125, [1, NJP + 4], I32)
        identb = at("identb", 9.625, [P, P], BF16)
        raw_gu = [at(f"raw_gu{k}", 62 + 16 * k, [P, 2, NC, DE]) for k in range(2)]
        raw_dn = [at(f"raw_dn{k}", 46 + 8 * k, [P, 2, D]) for k in range(2)]
        wh = [at(f"wh{u}", 94 + 4 * u, [P, D], F32R) for u in range(6)]
        wl = [at(f"wl{u}", 118 + 4 * u, [P, D], F32R) for u in range(6)]
        xs = at("xs", 142, [P, JG, NC, 2, SLOT], F32R)
        yh = at("yh", 158, [P, JG, D], F32R)
        yl = at("yl", 174, [P, JG, D], F32R)
        pick = at("pick", 190, [P, NT, JG * SLOT], F32R)
        pickb = at("pickb", 193, [P, NT, JG, SLOT], BF16)
        place = at("place", 194.5, [P, JG, TOK], F32R)
        gu = at("gu", 200.5, [SLOT, 2, DE])
        act_a = [at("act_a0", 202.5, [SLOT, DE]), at("act_a1", 206.625, [SLOT, DE])]
        sil = at("sil", 203.5, [SLOT, DE])
        ast = [at(f"ast{k}", 204.5 + k, [P, 2, 2, SLOT], F32R) for k in range(2)]
        gslot = at("gslot", 206.5, [P, JG])
        x1b = at("x1b", 158, [P, NT, D])
        gt2 = at("gt2", 170, [P, 2, D])
        x1_dram = nc.dram_tensor("x1_spill", [P, NT, D], F32, kind="Internal").ap()
        gt2_dram = nc.dram_tensor("gt2_spill", [2, D], F32, kind="Internal").ap()

        rt_used = [0]

        def rtile(*shape):
            n = int(np.prod(shape))
            a = rt[:, rt_used[0]:rt_used[0] + n]
            rt_used[0] += n
            assert rt_used[0] <= 3500
            if len(shape) == 2:
                a = a.rearrange("p (a b) -> p a b", b=shape[1])
            if len(shape) == 3:
                a = a.rearrange("p (a b c) -> p a b c", b=shape[1], c=shape[2])
            return a

        score, select, weight, picked = (rtile(NT, NE) for _ in range(4))
        top2 = rtile(NT * NG, 8)
        gscore, grank, gmask = rtile(NT, NG), rtile(NT, NG), rtile(NT, NG)
        gcmp, gcmp2 = rtile(NT, NG, NG), rtile(NT, NG, NG)
        top8 = rtile(NT, 8)
        wsum = rtile(NT)
        posp, poscount = rtile(NT, NE), rtile(NT, NE)
        cnt, nov, start, end = rtile(1), rtile(1), rtile(1), rtile(1)
        thr, cmpc = rtile(5), rtile(5)
        owner, owner2, offs = rtile(NOVER), rtile(NOVER), rtile(NOVER)
        poT, gaT = rtile(NT, P), rtile(NT, P)
        offrow, erow = rtile(NOVER), rtile(NJP)
        gjob = rtile(NT, NJP)
        grow, gcount = rtile(12), rtile(1)
        maskb = rtb[:, 0:3 * NE].rearrange("p (t e) -> p t e", e=NE)
        strictb, onesb = rtb[:, 3 * NE:3 * NE + P], rtb[:, 3 * NE + P:3 * NE + 2 * P]
        ss3, v3, r3, t3 = sm(NT), sm(NT), sm(NT), sm(NT)

        names2 = ("x1_in w_router_in shgu_in shd_in g2_in mod_rows gt2_out x1_out bc_ready mixT_sb x1_ready sq_done "
                  "h2_ready h2s_ready score_ready mask_ready bfc_ready pos_sb cnt_sb start_sb owner_ready tab_sb jobs_ready "
                  "shgu_used sh_sil_ready sh_gu_ready sh_a_ready acc_ready h2T_free "
                  "hi_gu lo_gu_dve lo_gu_pool hi_d4 hi_d5 lo_d4 lo_d5 gu_used dn_used gate_up half_up gu_sum silu_done a_ready "
                  "aT_done ah_done al_done y_done yh_done yl_done pick_ready pickb_ready gather_done xs_done "
                  "gate_mm gate_sb place_mm place_sb scatter_done acc_done tail_in y_ready y_out tail_ready shared_done xs_act xs_dve b5_sb h2h_ready h2l_ready").split()
        S.update({n: sem(n) for n in names2})
        raw_gu_in = [sem(f"raw_gu_in{k}") for k in range(2)]
        raw_dn_in = [sem(f"raw_dn_in{k}") for k in range(2)]
        block = ctx.enter_context(nc.Block())

        lat = [(0, 0), (1, 1), (1, 2)]
        misc = (["ckvT"] + [f"z{k}" for k in range(4)] + ["cqT0", "cqT1"]
                + [f"kv{t}{n}" for t in range(4) for n in range(2)] + [f"qm{t}" for t in range(NT)]
                + [f"keyT{h}" for h in range(MH)] + [f"qryT{h}" for h in range(MH)]
                + ["A00", "A01", "kendT0", "kendT1", "U0", "U1", "p0T", "o0"] + [f"p1T{h}" for h in range(MH)]
                + ["A10", "A11", "pv0", "pv1", "o1"] + [f"p2T{h}" for h in range(MH)] + ["A20", "A21", "pv2", "o2"]
                + ["mT00", "mT01", "wo00", "wo01", "mT10", "mT11", "wo10", "wo11", "mT20", "mT21", "wo20", "wo21"]
                + ["sg0", "sg1", "pos", "cnt", "start", "sg2", "tabP", "tabG", "tabO", "tabJ"]
                + [f"{n}" for t in range(NT) for n in (f"sa{t}", f"sd{t}0", f"sd{t}1")])
        misc_no = {n: k for k, n in enumerate(misc)}
        proj = (["lr"] + [f"mla{t}" for t in range(NT)] + [f"qk{k}" for k in range(4)] + [f"v{t}" for t in range(NT)]
                + [f"g{t}" for t in range(NT)] + ["s0"] + [f"s{t}{h}" for t in (1, 2) for h in range(MH)]
                + [f"b{v}{s}{n}" for v in range(3) for s in range(2) for n in range(2)]
                + ["h00", "h01", "r0", "h10", "h11", "r1", "h20", "h21", "r2"])
        proj_no = {n: k for k, n in enumerate(proj)}
        NADA = 16

        def mbank(n, w=512):
            return ps[:, 5 + misc_no[n] % 3, 0:w]

        def pbank(n, w=512):
            return ps[:, proj_no[n] % 4, 0:w]

        combos = [(0, 0), (1, 0), (0, 1), (1, 2)]

        @block.sync
        def _(sp):
            def load(dst, src, s, n=16):
                sp.dma_start(dst, src).then_inc(S[s], n)

            load(keep[:], A["c_keep"], "consts_in")
            load(x_sb[:, 0, :], A["x_prompt"][0], "x_in")
            load(x_sb[:, 1:3, :], A["x_sample"][0].rearrange("(t p) d -> p t d", p=P), "x_in")
            load(cols[:, 0:44], A["c_cols"], "cols_in")
            w_ada = rows_pc(A["w_ada"][0], 6 * D)
            for c in range(4):
                sp.dma_start(ada1[:, c, :], w_ada[:, c, 0:2 * D]).then_inc(ada1_in[c], 16)
            load(tconst[:], A["c_trunk"], "consts_in")
            load(rows[:], A["c_rows"].partition_broadcast(P), "consts_in")
            load(wgk[:], A["c_wgk"], "consts_in")
            w_in = rows_pc(A["w_in"][0], 1984)
            for c in range(4, NC):
                sp.wait_ge(S["ada1_used"], c - 3)
                sp.dma_start(ada1[:, c - 4, :], w_ada[:, c, 0:2 * D]).then_inc(ada1_in[c - 4], 16)
            load(w_mla[:], w_in[:, :, 1536:1984], "w_mla_in")
            load(w_qk[:], w_in[:, :, 0:512], "w_qk_in")
            load(krope[:, 3, :], A["cache_mla_krope"][0, 0], "cache_in")
            load(ckvn[:, 3, :], A["cache_mla_ckv"][0, 0], "cache_in")
            load(w_v[:], w_in[:, :, 512:1024], "w_v_in")
            load(w_g[:], w_in[:, :, 1024:1536], "w_g_in")
            sp.wait_ge(S["ada1_used"], NC)
            load(w_uq[:], A["w_uq"][0].rearrange("(p c) n -> p c n", c=2), "w_u_in")
            load(w_ukv[:], A["w_ukv"][0], "w_u_in")
            load(modrow[:], A["b_ada"][0:1, 2 * D:].partition_broadcast(2), "brow_in")
            for k in range(NADA):
                if k:
                    sp.wait_ge(S["ada2_done"], k)
                load(ada2[:], w_ada[:, :, 2 * D + k * 256:2 * D + (k + 1) * 256], "ada2_in")
                if k == 1:
                    sp.wait_ge(S["misc_done"], misc_no["z0"])
                    load(state0[:, 0], A["state_gla_fwd"][0, 0].rearrange("(b h) k v -> (h k) b v", h=2), "state_in")
                    load(state0[:, 1], A["state_gla_bwd"][0, 0].rearrange("(b h) k v -> (h k) b v", h=2), "state_in")
                if k == 9:
                    sp.wait_ge(S["proj_done"], proj_no["g2"] + 1)
                    load(w_out[:], rows_pc(A["w_out"][0], D), "w_out_in")
            sp.wait_ge(S["ckv_ready"], 1)
            sp.dma_start(O["new_ckv"][0, 0], ckvn[:, 0, :]).then_inc(S["out_done"], 16)
            sp.dma_start(O["new_krope"][0, 0], mla[:, 0, QL + KL:]).then_inc(S["out_done"], 16)
            sp.wait_ge(S["misc_sb"], misc_no["U1"] + 1)
            for d, name in ((0, "new_fwd"), (1, "new_bwd")):
                sp.dma_start(O[name][0, 0].rearrange("(b h) k v -> (h k) b v", h=2), state1[:, d]).then_inc(S["out_done"], 16)
            sp.wait_ge(S["misc_done"], misc_no["o2"] + 1)
            sp.wait_ge(S["mix_done"], NT)
            sp.dma_start(g2row[:], A["g_norm2"][0:1].partition_broadcast(P)).then_inc(S["g2_in"], 16)
            sp.dma_start(x1[:, 0, :], A["x_prompt"][0]).then_inc(S["x1_in"], 16)
            sp.dma_start(x1[:, 1:3, :], A["x_sample"][0].rearrange("(t p) d -> p t d", p=P)).then_inc(S["x1_in"], 16)
            sp.dma_start(w_router[:], rows_pc(A["w_router"][0], NE)).then_inc(S["w_router_in"], 16)
            sp.wait_ge(S["ada2_sb"], NADA)
            sp.dma_start(gt2_dram, modrow[:, 3 * D:4 * D]).then_inc(S["gt2_out"], 16)

            def load_gu(slot, e):
                sp.dma_start(raw_gu[slot][:, 0], gate_of(e)).then_inc(raw_gu_in[slot], 16)
                sp.dma_start(raw_gu[slot][:, 1], up_of(e)).then_inc(raw_gu_in[slot], 16)

            def gate_of(e):
                return A["w_exp_gate"][0, e].rearrange("(p c) n -> p c n", c=NC)

            def up_of(e):
                return A["w_exp_up"][0, e].rearrange("(p c) n -> p c n", c=NC)

            def load_dn(slot, e):
                sp.dma_start(raw_dn[slot][:], A["w_exp_down"][0, e].rearrange("(p c) n -> p c n", c=2)).then_inc(raw_dn_in[slot], 16)

            load_gu(0, 0)
            sp.wait_ge(S["gt2_out"], 16)
            sp.wait_ge(S["proj_sb"], proj_no["b211"] + 1)
            sp.dma_start(w_shgu[:, 0], rows_pc(A["w_sh_gate"][0], DE)).then_inc(S["shgu_in"], 16)
            sp.dma_start(w_shgu[:, 1], rows_pc(A["w_sh_up"][0], DE)).then_inc(S["shgu_in"], 16)
            sp.dma_start(w_shd[:], A["w_sh_down"][0].rearrange("(p c) n -> p c n", c=2)).then_inc(S["shd_in"], 16)
            for t in range(NT):
                sp.wait_ge(S["x1_ready"], t + 1)
                sp.dma_start(x1_dram[:, t], x1[:, t]).then_inc(S["x1_out"], 16)
            sp.wait_ge(S["misc_done"], misc_no["sg2"] + 1)
            load_dn(0, 0)
            sp.wait_ge(S["jobs_ready"], 1)
            load_gu(1, 1)

            def group_loads(g, expert):
                for kind, j in SPLITS:
                    if kind == "gu":
                        sp.wait_ge(S["lo_gu_dve"], 2 * JG * g + 2 * j)
                        sp.wait_ge(S["lo_gu_pool"], 2 * JG * g + 2 * j)
                        load_gu(j % 2, expert(j))
                    else:
                        sp.wait_ge(S["lo_d4"], JG * g + j + 1)
                        sp.wait_ge(S["lo_d5"], JG * g + j + 1)
                        load_dn(j % 2, expert(j))

            for kind, j in SPLITS:
                if (kind, j) in (("gu", 1), ("dn", 0)):
                    continue
                if kind == "gu":
                    sp.wait_ge(S["lo_gu_dve"], 2 * j)
                    sp.wait_ge(S["lo_gu_pool"], 2 * j)
                    load_gu(j % 2, j)
                else:
                    if j >= 2:
                        sp.wait_ge(S["lo_d4"], j + 1)
                        sp.wait_ge(S["lo_d5"], j + 1)
                    load_dn(j % 2, j)
            n_groups = sp.value_load(jobs[0:1, NJP:NJP + 1], min_val=NE // JG, max_val=NJ // JG)
            with sp.Fori(1, n_groups) as g:
                experts = [sp.value_load(jobs[0:1, bass.ds(g * JG + j, 1)], min_val=0, max_val=NE - 1) for j in range(JG + 1)]
                group_loads(g, lambda j: experts[j])
            sp.wait_ge(S["tail_ready"], 1)
            sp.wait_ge(S["x1_out"], 16 * NT)
            sp.dma_start(x1b[:], x1_dram).then_inc(S["tail_in"], 16)
            for s in range(2):
                sp.dma_start(gt2[:, s], gt2_dram[s:s + 1].partition_broadcast(P)).then_inc(S["tail_in"], 16)
            for t in range(NT):
                sp.wait_ge(S["y_ready"], t + 1)
                dst = O["y_prompt"][0] if t == 0 else O["y_sample"][0, (t - 1) * P:t * P]
                sp.dma_start(dst, x1b[:, t]).then_inc(S["y_out"], 16)
            sp.wait_ge(S["y_out"], 16 * NT)
            sp.wait_ge(S["out_done"], 64)

        @block.tensor
        def _(pe):
            def mm(out, l, r, first, last):
                return nc.tensor.matmul(out, l, r, start=first, stop=last)

            def open_misc(n):
                k = misc_no[n]
                if k >= 3:
                    pe.wait_ge(S["misc_sb"], k - 2)
                return mbank(n)

            def open_proj(n):
                k = proj_no[n]
                if k >= 4:
                    pe.wait_ge(S["proj_sb"], k - 3)
                return pbank(n)

            ada_next = [0]

            def ada(n=1):
                for _ in range(n):
                    k = ada_next[0]
                    if k >= NADA:
                        return
                    pe.wait_ge(S["ada2_in"], 16 * (k + 1))
                    if k:
                        pe.wait_ge(S["ada2_sb"], k)
                    for c in range(NC):
                        last = mm(ps[0:2, 4, 0:256], silu_c[:, c, :], ada2[:, c, :], c == 0, c == NC - 1)
                    last.then_inc(S["ada2_done"], 1)
                    ada_next[0] += 1

            pe.wait_ge(S["silu_ready"], 1)
            for c in range(NC):
                if c == 4:
                    pe.wait_ge(S["consts_in"], 16)
                    pe.wait_ge(S["xn_ready"], 1)
                    for k in range(NC):
                        if k >= 4:
                            pe.wait_ge(S["xT_sb"], k - 3)
                        for t in range(NT):
                            last = nc.tensor.transpose(ps[:, 4 + k % 4, t * P:(t + 1) * P],
                                                       x_sb[:, t, k::NC], ident)
                        last.then_inc(S["xT_done"], 1)
                pe.wait_ge(ada1_in[c % 4], 16 * (c // 4 + 1))
                for n in range(4):
                    last = mm(ps[0:2, n, :], silu_c[:, c, :], ada1[:, c % 4, n * 512:(n + 1) * 512], c == 0, c == NC - 1)
                last.then_inc(S["ada1_used"], 1)
            pe.wait_ge(S["mod1_sb"], 1)
            pe.wait_ge(S["xT_sb"], NC)
            for j in range(2):
                for c in range(NC):
                    o = (j * NC + c) * 2
                    last = nc.tensor.transpose(ps[:, 4, o:o + 2], mod1[0:2, j * D + c:(j + 1) * D:NC], ident[0:2, 0:2])
            last.then_inc(S["modT_done"], 1)

            pe.wait_ge(S["h_ready"], 1)
            pe.wait_ge(S["w_mla_in"], 16)
            o = open_proj("lr")
            for c in range(NC):
                last = mm(o[0:32, 0:TOK], w_mla[:, c, 0:32], hT[:, c, :], c == 0, c == NC - 1)
            last.then_inc(S["proj_done"], 1)

            def token_rows(n, t, w):
                o = open_proj(n)[:, 0:w.shape[2]]
                for c in range(NC):
                    last = mm(o, hT[:, c, t * P:(t + 1) * P], w[:, c, :], c == 0, c == NC - 1)
                last.then_inc(S["proj_done"], 1)

            for t in range(NT):
                token_rows(f"mla{t}", t, w_mla[:, :, 32:448])
            pe.wait_ge(S["w_qk_in"], 16)
            for k in range(4):
                o = open_proj(f"qk{k}")[:, 0:TOK]
                for c in range(NC):
                    last = mm(o, w_qk[:, c, k * P:(k + 1) * P], hT[:, c, :], c == 0, c == NC - 1)
                last.then_inc(S["proj_done"], 1)
            pe.wait_ge(S["ckv_ready"], 1)
            pe.wait_ge(S["cache_in"], 32)
            o = open_misc("ckvT")
            for t in range(4):
                last = nc.tensor.transpose(o[:, t * P:(t + 1) * P], ckvn[:, t, :], ident)
            last.then_inc(S["misc_done"], 1)
            pe.wait_ge(S["proj_sb"], 1)
            pe.wait_ge(S["consts_in"], 64)
            for k in range(4):
                o = open_misc(f"z{k}")
                mm(o[:, 0:TOK], wgk[:, k // 2, k % 2, :], lrT[:], True, True).then_inc(S["misc_done"], 1)
            pe.wait_ge(S["cqn_ready"], 1)
            for c in range(2):
                o = open_misc(f"cqT{c}")
                for t in range(NT):
                    last = nc.tensor.transpose(o[:, t * P:(t + 1) * P], mla[:, t, c:QL:2], ident)
                last.then_inc(S["misc_done"], 1)
            pe.wait_ge(S["w_v_in"], 16)
            token_rows("v0", 0, w_v)
            pe.wait_ge(S["w_u_in"], 32)
            pe.wait_ge(S["misc_sb"], misc_no["ckvT"] + 1)
            for t in range(4):
                for n in range(2):
                    o = open_misc(f"kv{t}{n}")
                    mm(o[:, 0:384], ckvnT[:, t * P:(t + 1) * P], w_ukv[:, n * 384:(n + 1) * 384], True, True)\
                        .then_inc(S["misc_done"], 1)
            pe.wait_ge(S["misc_sb"], misc_no["cqT1"] + 1)
            for t in range(NT):
                o = open_misc(f"qm{t}")
                for c in range(2):
                    last = mm(o[:, 0:MH * QK], cqT[:, c, t * P:(t + 1) * P], w_uq[:, c, :], c == 0, c == 1)
                last.then_inc(S["misc_done"], 1)
            pe.wait_ge(S["brow_in"], 16)
            for t in (1, 2):
                token_rows(f"v{t}", t, w_v)
                ada()
            pe.wait_ge(S["w_g_in"], 16)
            for t in range(NT):
                token_rows(f"g{t}", t, w_g)
                ada()
            pe.wait_ge(S["key_ready"], 1)
            for h in range(MH):
                o = open_misc(f"keyT{h}")
                for t in range(4):
                    last = nc.tensor.transpose(o[0:QK, t * P:(t + 1) * P], key[:, t, h, :], ident)
                last.then_inc(S["misc_done"], 1)
            pe.wait_ge(S["qry_ready"], 1)
            for h in range(MH):
                o = open_misc(f"qryT{h}")
                for t in range(NT):
                    last = nc.tensor.transpose(o[0:QK, t * P:(t + 1) * P], qry[:, t, h, :], ident)
                last.then_inc(S["misc_done"], 1)

            pe.wait_ge(S["misc_sb"], misc_no["qryT3"] + 1)
            o = open_proj("s0")
            for h in range(MH):
                last = mm(o[:, h * P:(h + 1) * P], qryT[:, h, 0:P], keyT[:, h, 0:P], True, True)
            last.then_inc(S["proj_done"], 1)

            def scores(t):
                for h in range(MH):
                    o = open_proj(f"s{t}{h}")
                    mm(o[:, 0:TOK], qryT[:, h, t * P:(t + 1) * P], keyT[:, h, P:], True, True).then_inc(S["proj_done"], 1)

            def gla_scores(t):
                for par in range(2):
                    o = open_misc(f"A{t}{par}")
                    r = slice(par * GDK, (par + 1) * GDK)
                    for hh in range(2):
                        for d in range(2):
                            last = mm(o[:, (hh * 2 + d) * P:(hh * 2 + d + 1) * P],
                                      decay_m[r, d * 2 + hh, t * P:(t + 1) * P],
                                      decay_p[r, d * 2 + hh, t * P:(t + 1) * P], True, True)
                    last.then_inc(S["misc_done"], 1)

            def gla_out(t):
                pe.wait_ge(S["misc_sb"], misc_no[f"A{t}1"] + 1)
                if t:
                    pe.wait_ge(S["smp_ready"], t)
                o = open_misc(f"o{t}")
                for h in range(GH):
                    oh = o[:, h * GDV:(h + 1) * GDV]
                    for d in range(2):
                        last = mm(oh, attn[:, h % 2, h // 2, d, :], v_sb[:, t, h * GDV:(h + 1) * GDV], d == 0, not t and d == 1)
                    if t:
                        for d in range(2):
                            last = mm(oh, decay_p[:, d * 2 + h // 2, t * P:(t + 1) * P], stateP[:, t - 1, d, h, :], False, d == 1)
                last.then_inc(S["misc_done"], 1)

            def prob_t(t):
                for h in range(MH):
                    o = open_misc(f"p{t}T{h}")
                    pe.wait_ge(S["prob_ready"], 4 + (t - 1) * MH + h + 1)
                    for k in range(NT):
                        last = nc.tensor.transpose(o[:, k * P:(k + 1) * P], prob[:, h, k * P:(k + 1) * P], ident)
                    last.then_inc(S["misc_done"], 1)

            def prob_v(t):
                pe.wait_ge(S["misc_sb"], misc_no[f"p{t}T3"] + 1)
                o = open_misc(f"pv{t}")
                for h in range(MH):
                    for k in range(NT):
                        last = mm(o[:, h * VD:(h + 1) * VD], probT[:, h, k, :], val[:, 1 + k, h, :], k == 0, k == NT - 1)
                last.then_inc(S["misc_done"], 1)

            scores(1)
            pe.wait_ge(S["qe_ready"], 1)
            gla_scores(0)
            ada()
            pe.wait_ge(S["kend_ready"], 1)
            for n in range(2):
                o = open_misc(f"kendT{n}")
                for m in range(4):
                    last = nc.tensor.transpose(o[:, m * P:(m + 1) * P], kend[:, 2 * n + m // 2, m % 2, :], ident)
                last.then_inc(S["misc_done"], 1)
            ada()
            pe.wait_ge(S["misc_sb"], misc_no["kendT1"] + 1)
            pe.wait_ge(S["proj_sb"], proj_no["v2"] + 1)
            for n in range(2):
                o = open_misc(f"U{n}")
                for m in range(2):
                    k = 2 * n + m
                    for h in range(GH):
                        r = h % 2 * GDK
                        last = mm(o[r:r + GDK, (m * 2 + h // 2) * GDV:(m * 2 + h // 2 + 1) * GDV],
                                  kendT[:, k, h // 2, r:r + GDK], v_sb[:, combos[k][1], h * GDV:(h + 1) * GDV], True, True)
                last.then_inc(S["misc_done"], 1)
            pe.wait_ge(S["prob_ready"], 4)
            o = open_misc("p0T")
            for h in range(MH):
                last = nc.tensor.transpose(o[:, h * P:(h + 1) * P], prob0[:, h, :], ident)
            last.then_inc(S["misc_done"], 1)
            ada()
            gla_out(0)
            prob_t(1)
            ada()
            gla_scores(1)
            pe.wait_ge(S["misc_sb"], misc_no["p0T"] + 1)
            o = open_misc("pv0")
            for h in range(MH):
                last = mm(o[:, h * VD:(h + 1) * VD], prob0T[:, h, :], val[:, 0, h, :], True, True)
            last.then_inc(S["misc_done"], 1)
            prob_v(1)
            scores(2)
            gla_out(1)
            ada(2)
            prob_t(2)
            gla_scores(2)
            ada()
            prob_v(2)
            gla_out(2)
            ada(NADA)
            pe.wait_ge(S["ada2_sb"], NADA)
            for v in range(3):
                for s in range(2):
                    for n in range(2):
                        o = open_proj(f"b{v}{s}{n}")
                        mm(o, tc("sel")[0:2, s * P:(s + 1) * P], modrow[:, v * D + n * 512:v * D + (n + 1) * 512], True, True)\
                            .then_inc(S["proj_done"], 1)

            def mixed_t(t):
                pe.wait_ge(S["mix_done"], t + 1)
                for n in range(2):
                    o = open_misc(f"mT{t}{n}")
                    for c in range(4):
                        last = nc.tensor.transpose(o[:, c * P:(c + 1) * P], mixed[:, t, 4 * n + c::NC], ident)
                    last.then_inc(S["misc_done"], 1)

            def out_proj(t):
                pe.wait_ge(S["misc_sb"], misc_no[f"mT{t}1"] + 1)
                for n in range(2):
                    o = open_misc(f"wo{t}{n}")
                    for c in range(NC):
                        last = mm(o, mixedT[:, c, t * P:(t + 1) * P], w_out[:, c, n * 512:(n + 1) * 512], c == 0, c == NC - 1)
                    last.then_inc(S["misc_done"], 1)

            def h2_t(t):
                pe.wait_ge(S["h2_ready"], t + 1)
                for n in range(2):
                    o = open_proj(f"h{t}{n}")
                    for c in range(4):
                        last = nc.tensor.transpose(o[:, c * P:(c + 1) * P], h2[:, t, 4 * n + c::NC], ident)
                    last.then_inc(S["proj_done"], 1)

            def router(t):
                pe.wait_ge(S["w_router_in"], 16)
                pe.wait_ge(S["proj_sb"], proj_no[f"h{t}1"] + 1)
                o = open_proj(f"r{t}")[:, 0:NE]
                for c in range(NC):
                    last = mm(o, h2T[:, c, t * P:(t + 1) * P], w_router[:, c, :], c == 0, c == NC - 1)
                last.then_inc(S["proj_done"], 1)

            def shared_up(t):
                pe.wait_ge(S["shgu_in"], 32)
                o = open_misc(f"sg{t}")
                for c in range(NC):
                    last = mm(o, h2T[:, c, t * P:(t + 1) * P], w_shgu[:, :, c, :], c == 0, c == NC - 1)
                last.then_inc(S["misc_done"], 1)

            def shared_down(t):
                pe.wait_ge(S["shd_in"], 16)
                pe.wait_ge(S["sh_a_ready"], t + 1)
                o = open_misc(f"sa{t}")
                for f in range(2):
                    last = nc.tensor.transpose(o[:, f * P:(f + 1) * P], sh_a[t][:, f::2], ident)
                last.then_inc(S["misc_done"], 1)
                pe.wait_ge(S["misc_sb"], misc_no[f"sa{t}"] + 1)
                for n in range(2):
                    o = open_misc(f"sd{t}{n}")
                    for f in range(2):
                        last = mm(o, sh_aT[:, f, :], w_shd[:, f, n * 512:(n + 1) * 512], f == 0, f == 1)
                    last.then_inc(S["misc_done"], 1)

            pe.wait_ge(S["w_out_in"], 16)
            mixed_t(0)
            out_proj(0)
            mixed_t(1)
            out_proj(1)
            mixed_t(2)
            h2_t(0)
            router(0)
            out_proj(2)
            h2_t(1)
            router(1)
            shared_up(0)
            h2_t(2)
            router(2)
            shared_up(1)
            pe.wait_ge(S["mask_ready"], 1)
            o = open_misc("pos")
            for t in range(NT):
                for b in range(t + 1):
                    last = mm(o[:, t * NE:(t + 1) * NE], strictb if b == t else onesb, maskb[:, b, :], b == 0, b == t)
            last.then_inc(S["misc_done"], 1)
            o = open_misc("cnt")
            for t in range(NT):
                last = mm(o[0:NE, 0:1], maskb[:, t, :], onesb[:, 0:1], t == 0, t == NT - 1)
            last.then_inc(S["misc_done"], 1)
            pe.wait_ge(S["cnt_sb"], 1)
            o = open_misc("start")
            mm(o[0:NE, 0:1], strict[0:NE, 0:NE], nov[0:NE], True, True).then_inc(S["misc_done"], 1)
            shared_up(2)
            for n, z in (("tabP", posp), ("tabG", weight)):
                o = open_misc(n)
                for t in range(NT):
                    last = nc.tensor.transpose(o[0:NE, t * P:(t + 1) * P], z[:, t, :], ident)
                last.then_inc(S["misc_done"], 1)
            pe.wait_ge(S["owner_ready"], 1)
            o = open_misc("tabO")
            mm(o[:, 0:NOVER], ones[0:NE], offs[0:NE], True, True)
            mm(o[:, NOVER:2 * NOVER], tc("index")[0:NE].to_broadcast([NE, P]), owner[0:NE], True, True)
            mm(o[:, 2 * NOVER:2 * NOVER + 1], ones[0:NE], nov[0:NE], True, True).then_inc(S["misc_done"], 1)
            pe.wait_ge(S["misc_sb"], misc_no["tabG"] + 1)
            o = open_misc("tabJ")
            for k, z in enumerate((poT, gaT)):
                for t in range(NT):
                    last = mm(o[:, (k * NT + t) * NOVER:(k * NT + t + 1) * NOVER], z[0:NE, t, :], owner[0:NE], True, True)
            last.then_inc(S["misc_done"], 1)

            def gather(g):
                pe.wait_ge(S["pick_ready"], g + 2)
                for c in range(NC):
                    gather_chunk(g, c)

            def gather_chunk(g, c):
                if c < 2:
                    pe.wait_ge(S["acc_done"], 6 * g + 5 + c)
                else:
                    pe.wait_ge(S["xs_act" if c % 2 == 0 else "xs_dve"], 4 * g + 4 + c // 2)
                for z, h in enumerate((h2h, h2l)):
                    for t in range(NT):
                        last = mm(ps[:, 6 + c % 2, z * 256:(z + 1) * 256], h[:, t, c, :], pick[:, t, :], t == 0, t == NT - 1)
                last.then_inc(S["gather_done"], 1)

            def gate_slots(g, col):
                pe.wait_ge(S["pickb_ready"], g + 2)
                pe.wait_ge(S["b5_sb"], 5 * g + 5)
                for j in range(JG):
                    for t in range(NT):
                        last = mm(ps[0:SLOT, 5, j * 4:j * 4 + 3], pickb[:, t, j, :], gparts[:, t, col + j, :] if isinstance(col, int)
                                  else gparts[:, t, bass.ds(col + j, 1), :].rearrange("p a b -> p (a b)"), t == 0, t == NT - 1)
                last.then_inc(S["place_mm"], 1)

            def place_slots(g, j):
                pe.wait_ge(S["b5_sb"], 5 * g + 1 + j)
                for t in range(NT):
                    for half in range(2):
                        last = mm(ps[half * SLOT:(half + 1) * SLOT, 5, t * P:(t + 1) * P], pickb[:, t, j, :], identb[:], True, True)
                last.then_inc(S["place_mm"], 1)

            def up(g, j, units):
                for u in units:
                    if u == 0:
                        pe.wait_ge(S["gu_sum"], JG * g + j + 1)
                        if j == 0:
                            pe.wait_ge(S["xs_act"], 4 * g + 4)
                            pe.wait_ge(S["xs_dve"], 4 * g + 4)
                    pe.wait_ge(S["lo_gu_dve" if u % 2 == 0 else "lo_gu_pool"], 2 * JG * g + 2 * j + u // 2 + 3)
                    for cc in range(2):
                        c = 2 * u + cc
                        for w in (wh[u], wl[u]):
                            last = mm(ps[:, j % 2, :], xs[:, j, c].rearrange("p a b -> p (a b)"),
                                      w[:].rearrange("p (m c n) -> p m c n", m=2, c=2)[:, :, cc, :],
                                      c == 0 and w is wh[u], c == NC - 1 and w is wl[u])
                    last.then_inc(S["gu_used"], 1)

            def turn(g, j):
                pe.wait_ge(S["a_ready"], JG * g + j + 2)
                pe.wait_ge(S["al_done"], JG * g + j + 1)
                for f in range(2):
                    last = mm(ps[:, 4, f * SLOT:(f + 1) * SLOT], act_a[j % 2][:, f::2], ident[0:SLOT, 0:SLOT], True, True)
                last.then_inc(S["aT_done"], 1)

            def down(g, j):
                pe.wait_ge(S["al_done"], JG * g + j + 2)
                for f in range(2):
                    pe.wait_ge(S["lo_d4" if f == 0 else "lo_d5"], JG * g + j + 3)
                    for n in range(2):
                        if f == 0:
                            pe.wait_ge(S["yl_done"], 2 * JG * g + 2 * j + n + 1)
                        for w in (wh[4 + f], wl[4 + f]):
                            last = mm(ps[:, 2 + n, :], ast[j % 2][:, f].rearrange("p a b -> p (a b)"), w[:, n * 512:(n + 1) * 512],
                                      f == 0 and w is wh[4], f == 1 and w is wl[5])
                    last.then_inc(S["dn_used"], 1)

            def scatter(g):
                pe.wait_ge(S["yl_done"], 2 * JG * g + 2 * JG + 2)
                pe.wait_ge(S["b5_sb"], 5 * g + 5)
                for k in range(6):
                    if k < 2:
                        pe.wait_ge(S["xs_act" if k == 0 else "xs_dve"], 4 * g + 8)
                    else:
                        pe.wait_ge(S["acc_done"], 6 * g + k - 1 + 6)
                    t, n = k // 2, k % 2
                    for j in range(JG):
                        for y in (yh, yl):
                            last = mm(ps[:, 6 + k % 2, :], place[:, j, t * P:(t + 1) * P], y[:, j, n * 512:(n + 1) * 512],
                                      j == 0 and y is yh, j == JG - 1 and y is yl)
                    last.then_inc(S["scatter_done"], 1)

            pe.wait_ge(S["misc_sb"], misc_no["tabJ"] + 1)
            pe.wait_ge(S["proj_sb"], len(proj))
            for t in range(NT):
                shared_down(t)
            pe.wait_ge(S["h2s_ready"], 1)
            pe.wait_ge(S["misc_sb"], len(misc))
            pe.sem_inc(S["gu_used"], 4)
            pe.sem_inc(S["dn_used"], 4)
            pe.sem_inc(S["aT_done"], 2)
            pe.sem_inc(S["scatter_done"], 6)
            pe.wait_ge(S["pick_ready"], 1)
            pe.wait_ge(S["acc_done"], 6)
            for c in range(NC):
                if c >= 2:
                    pe.wait_ge(S["xs_act" if c % 2 == 0 else "xs_dve"], c // 2)
                for z, h in enumerate((h2h, h2l)):
                    for t in range(NT):
                        last = mm(ps[:, 6 + c % 2, z * 256:(z + 1) * 256], h[:, t, c, :], pick[:, t, :], t == 0, t == NT - 1)
                last.then_inc(S["gather_done"], 1)
            pe.wait_ge(S["pickb_ready"], 1)
            for j in range(JG):
                for t in range(NT):
                    last = mm(ps[0:SLOT, 5, j * 4:j * 4 + 3], pickb[:, t, j, :], gparts[:, t, j, :], t == 0, t == NT - 1)
            last.then_inc(S["place_mm"], 1)
            n_groups = pe.value_load(jobs[0:1, NJP:NJP + 1], min_val=NE // JG, max_val=NJ // JG)
            with pe.Fori(0, n_groups) as g:
                up(g, 0, range(4))
                place_slots(g, 0)
                up(g, 1, range(4))
                place_slots(g, 1)
                up(g, 2, range(3))
                turn(g, 0)
                up(g, 2, (3,))
                place_slots(g, 2)
                down(g, 0)
                up(g, 3, range(3))
                turn(g, 1)
                up(g, 3, (3,))
                place_slots(g, 3)
                down(g, 1)
                turn(g, 2)
                pe.wait_ge(S["pick_ready"], g + 2)
                for c in range(4):
                    gather_chunk(g, c)
                down(g, 2)
                turn(g, 3)
                for c in range(4, NC):
                    gather_chunk(g, c)
                gate_slots(g, g * JG + JG)
                down(g, 3)
                scatter(g)

        @block.scalar
        def _(act):
            chain = [0]

            def own(i):
                chain[0] += 1
                i.then_inc(S["act_chain"], 1)
                act.wait_ge(S["act_chain"], chain[0])

            roots = [0]

            def root(v, t, r):
                roots[0] += 1
                act.wait_ge(S["rn_in"], roots[0])
                own(nc.scalar.activation(t, v, ACT.Ln))
                nc.scalar.activation(r, t, ACT.Exp, scale=-0.5).then_inc(S["rn_out"], 1)

            def take(n, out, w=512, rowsn=P, scale=None):
                act.wait_ge(S["proj_done"], proj_no[n] + 1)
                i = pbank(n, w)[0:rowsn]
                if scale is None:
                    nc.scalar.copy(out, i).then_inc(S["proj_sb"], 1)
                else:
                    nc.scalar.mul(out, i, scale).then_inc(S["proj_sb"], 1)

            act.wait_ge(S["cols_in"], 16)
            nc.scalar.activation(cexp, ccol, ACT.Exp, scale=-1.0).then_inc(S["silu_g"], 1)
            act.wait_ge(S["x_in"], 32)
            for t in range(NT):
                i = nc.scalar.activation(sq[:, 0:D], x_sb[:, t, :], ACT.Square, accum_out=ss1[:, t:t + 1])
                own(i)
            act.sem_inc(S["rn_ln"], 1)
            root(v1, t1, r1)
            for c in range(NC):
                act.wait_ge(S["xT_done"], c + 1)
                nc.scalar.copy(hT[:, c, :], ps[:, 4 + c % 4, 0:TOK]).then_inc(S["xT_sb"], 1)
            take("lr", lrT[:], TOK, 32)
            for t in range(NT):
                take(f"mla{t}", mla[:, t, :], QL + KL + ROPE)
            act.wait_ge(S["proj_sb"], 4)
            for t in range(NT):
                own(nc.scalar.activation(sq[:, 0:QL], mla[:, t, 0:QL], ACT.Square, accum_out=ss2[:, 0, t:t + 1]))
                own(nc.scalar.activation(sq[:, 0:KL], mla[:, t, QL:QL + KL], ACT.Square, accum_out=ss2[:, 1, t:t + 1]))
            act.sem_inc(S["rn_ln"], 1)
            root(v2, t2, r2)
            for k in range(4):
                take(f"qk{k}", qkT[:, k, :], TOK, P, GDK ** -0.5 if k < 2 else None)
            act.wait_ge(S["misc_sb"], misc_no["z3"] + 1)
            own(nc.scalar.activation(decay_p[:], decay_m[:], ACT.Abs))
            own(nc.scalar.activation(decay_p[:], decay_p[:], ACT.Exp, scale=-1.0))
            nc.scalar.activation(decay_p[:], decay_p[:], ACT.Ln, bias=1.0).then_inc(S["gate_l"], 1)
            take("v0", v_sb[:, 0, :])
            act.wait_ge(S["gate_d"], 1)
            nc.scalar.activation(gex, gsm, ACT.Exp, scale=1.0 / GATE_NORM).then_inc(S["decay_ready"], 1)
            nc.scalar.activation(decay_p[:], decay_m[:], ACT.Exp, scale=1.0 / GATE_NORM).then_inc(S["decay_ready"], 1)
            act.wait_ge(S["decay_ready"], 2)
            nc.scalar.activation(decay_m[:], decay_m[:], ACT.Exp, scale=-1.0 / GATE_NORM).then_inc(S["decay_ready"], 1)
            take("v1", v_sb[:, 1, :])
            root(vk, tk, rk)
            take("v2", v_sb[:, 2, :])
            root(vq, tq, rq)
            for t in range(NT):
                take(f"g{t}", g_sb[:, t, :])
            act.wait_ge(S["max_ready"], 1)
            for h in range(MH):
                i = nc.scalar.activation(prob0[:, h, :], pbank("s0")[:, h * P:(h + 1) * P], ACT.Exp,
                                         bias=nmax[:, 0, h:h + 1], accum_out=psum_p[:, 0, h:h + 1])
                i.then_inc(S["prob_ready"], 1)
            act.wait_ge(S["prob_ready"], MH)
            act.sem_inc(S["proj_sb"], 1)
            for t in (1, 2):
                if t == 2:
                    act.wait_ge(S["misc_done"], misc_no["p1T3"] + 1)
                for h in range(MH):
                    act.wait_ge(S["max_ready"], 1 + (t - 1) * MH + h + 1)
                    nc.scalar.activation(prob[:, h, :], pbank(f"s{t}{h}", TOK), ACT.Exp,
                                         bias=nmax[:, t, h:h + 1], accum_out=psum_p[:, t, h:h + 1])\
                        .then_inc(S["prob_ready"], 1)
                    act.wait_ge(S["prob_ready"], MH + (t - 1) * MH + h + 1)
                    act.sem_inc(S["proj_sb"], 1)
                if t == 1:
                    act.wait_ge(S["misc_done"], misc_no["qm2"] + 1)
                    nc.scalar.activation(gexp[:], g_sb[:], ACT.Exp, scale=-1.0).then_inc(S["silu_g"], 1)
            root(vo, to, ro)
            for v in range(3):
                for s in range(2):
                    for n in range(2):
                        act.wait_ge(S["proj_done"], proj_no[f"b{v}{s}{n}"] + 1)
                        dst = (gt1, add2, mul2)[v][:, s, n * 512:(n + 1) * 512]
                        nc.scalar.activation(dst, pbank(f"b{v}{s}{n}"), ACT.Identity, bias=1.0 if v == 2 else 0.0)\
                            .then_inc(S["proj_sb"], 1)

            def norm2(t):
                act.wait_ge(S["x1_ready"], t + 1)
                nc.scalar.activation(sq3[:], x1[:, t], ACT.Square, accum_out=ss3[:, t:t + 1]).then_inc(S["sq_done"], 1)
                act.wait_ge(S["sq_done"], t + 1)
                root(v3[:, t:t + 1], t3[:, t:t + 1], r3[:, t:t + 1])

            def h2_take(t):
                for n in range(2):
                    act.wait_ge(S["proj_done"], proj_no[f"h{t}{n}"] + 1)
                    nc.scalar.copy(h2T[:, 4 * n:4 * n + 4, t * P:(t + 1) * P],
                                   pbank(f"h{t}{n}").rearrange("p (c j) -> p c j", c=4)).then_inc(S["proj_sb"], 1)

            def scores_take(t):
                act.wait_ge(S["proj_done"], proj_no[f"r{t}"] + 1)
                nc.scalar.activation(score[:, t, :], pbank(f"r{t}", NE), ACT.Sigmoid).then_inc(S["score_ready"], 1)
                act.wait_ge(S["score_ready"], t + 1)
                act.sem_inc(S["proj_sb"], 1)

            norm2(0)
            norm2(1)
            h2_take(0)
            act.wait_ge(S["misc_done"], misc_no["wo21"] + 1)
            norm2(2)
            scores_take(0)
            h2_take(1)
            scores_take(1)
            h2_take(2)
            scores_take(2)
            act.wait_ge(S["misc_done"], misc_no["wo21"] + 1)
            for t in range(NT):
                nc.scalar.copy(h2h[:, t], h2[:, t].rearrange("p (j c) -> p c j", c=NC)).then_inc(S["h2h_ready"], 1)
            for t in range(NT):
                if t:
                    act.wait_ge(S["sh_a_ready"], t)
                act.wait_ge(S["misc_done"], misc_no[f"sg{t}"] + 1)
                nc.scalar.activation(sh_sil[:], mbank(f"sg{t}")[:, 0:DE], ACT.Silu).then_inc(S["sh_sil_ready"], 1)

            def high_gu(g, j, u):
                if u == 0:
                    act.wait_ge(raw_gu_in[j % 2], 32 * (2 * g + j // 2 + 1))
                act.wait_ge(S["gu_used"], 4 * (JG * g + j) + u + 1)
                nc.scalar.copy(wh[u][:].rearrange("p (m c) -> p m c", m=2),
                               raw_gu[j % 2][:, :, 2 * u:2 * u + 2, :].rearrange("p m c n -> p m (c n)"))\
                    .then_inc(S["hi_gu"], 1)

            def high_dn(g, j):
                act.wait_ge(raw_dn_in[j % 2], 16 * (2 * g + j // 2 + 1))
                act.wait_ge(S["dn_used"], 2 * (JG * g + j) + 3)
                nc.scalar.copy(wh[4][:], raw_dn[j % 2][:, 0]).then_inc(S["hi_d4"], 1)

            def other_half(g, j):
                act.wait_ge(S["gu_used"], 4 * (JG * g + j) + 8)
                act.wait_ge(S["a_ready"], JG * g + j + 1)
                nc.scalar.copy(gu[:].rearrange("p m n -> p (m n)"), ps[SLOT:2 * SLOT, j % 2, :]).then_inc(S["half_up"], 1)

            def silu(g, j):
                act.wait_ge(S["gu_sum"], JG * g + j + 3)
                nc.scalar.activation(sil[:], gu[:, 0], ACT.Silu).then_inc(S["silu_done"], 1)

            def high_a(g, j):
                act.wait_ge(S["aT_done"], JG * g + j + 3)
                act.wait_ge(S["dn_used"], 2 * (JG * g + j) + 2)
                nc.scalar.copy(ast[j % 2][:, :, 0, :], ps[:, 4, 0:2 * SLOT].rearrange("p (f s) -> p f s", f=2))\
                    .then_inc(S["ah_done"], 1)

            def high_y(g, j):
                act.wait_ge(S["dn_used"], 2 * (JG * g + j) + 6)
                act.wait_ge(S["scatter_done"], 6 * g + 6)
                for n in range(2):
                    nc.scalar.copy(yh[:, j, n * 512:(n + 1) * 512], ps[:, 2 + n, :]).then_inc(S["yh_done"], 1)

            def tokens(g, c):
                act.wait_ge(S["gather_done"], NC * (g + 1) + c + 1)
                nc.scalar.copy(xs[:, :, c], ps[:, 6, :].rearrange("p (z j s) -> p j z s", z=2, j=JG)).then_inc(S["xs_act"], 1)

            act.wait_ge(S["shared_done"], 1)
            for u in range(4):
                high_gu(0, 0, u)
            for c in range(0, NC, 2):
                act.wait_ge(S["gather_done"], c + 1)
                nc.scalar.copy(xs[:, :, c], ps[:, 6, :].rearrange("p (z j s) -> p j z s", z=2, j=JG)).then_inc(S["xs_act"], 1)
            n_groups = act.value_load(jobs[0:1, NJP:NJP + 1], min_val=NE // JG, max_val=NJ // JG)
            with act.Fori(0, n_groups) as g:
                for u in range(3):
                    high_gu(g, 1, u)
                other_half(g, 0)
                high_gu(g, 1, 3)
                silu(g, 0)
                for u in range(3):
                    high_gu(g, 2, u)
                other_half(g, 1)
                high_gu(g, 2, 3)
                silu(g, 1)
                high_dn(g, 0)
                high_gu(g, 3, 0)
                high_gu(g, 3, 1)
                high_a(g, 0)
                high_gu(g, 3, 2)
                other_half(g, 2)
                high_gu(g, 3, 3)
                silu(g, 2)
                high_dn(g, 1)
                high_y(g, 0)
                high_gu(g, 4, 0)
                high_gu(g, 4, 1)
                high_a(g, 1)
                high_gu(g, 4, 2)
                other_half(g, 3)
                high_gu(g, 4, 3)
                silu(g, 3)
                high_y(g, 1)
                high_dn(g, 2)
                high_a(g, 2)
                tokens(g, 0)
                tokens(g, 2)
                high_y(g, 2)
                high_dn(g, 3)
                high_a(g, 3)
                tokens(g, 4)
                tokens(g, 6)
                high_y(g, 3)

        @block.vector
        def _(dve):
            V = nc.vector
            chain = [0]

            def own(i):
                chain[0] += 1
                i.then_inc(S["dve_chain"], 1)
                dve.wait_ge(S["dve_chain"], chain[0])

            roots = [0]

            def root(v, t, r, last=None):
                roots[0] += 1
                dve.wait_ge(S["rn_out"], roots[0])
                own(V.tensor_tensor(t, r, r, ALU.mult))
                own(V.tensor_tensor(t, t, v, ALU.mult))
                own(V.tensor_scalar(t, t, -0.5, 1.5, ALU.mult, ALU.add))
                own(V.tensor_tensor(r, r, t, ALU.mult))

            def take(n):
                dve.wait_ge(S["misc_done"], misc_no[n] + 1)
                return mbank(n)

            def freed(i):
                i.then_inc(S["misc_sb"], 1)

            ada_next = [0]

            def ada(n=1):
                for _ in range(n):
                    k = ada_next[0]
                    if k >= NADA:
                        return
                    dve.wait_ge(S["ada2_done"], k + 1)
                    m = modrow[:, k * 256:(k + 1) * 256]
                    V.tensor_tensor(m, m, ps[0:2, 4, 0:256], ALU.add).then_inc(S["ada2_sb"], 1)
                    ada_next[0] += 1

            dve.wait_ge(S["silu_g"], 1)
            own(V.tensor_scalar(cexp, cexp, 1.0, None, ALU.add))
            own(V.reciprocal(cexp, cexp))
            V.tensor_tensor(silu_c.rearrange("p c s -> p s c"), cexp, ccol, ALU.mult).then_inc(S["silu_ready"], 1)
            dve.wait_ge(S["rn_ln"], 1)
            V.tensor_scalar(v1, ss1, 1.0 / D, EPS, ALU.mult, ALU.add).then_inc(S["rn_in"], 1)
            root(v1, t1, r1)
            for t in range(NT):
                last = V.tensor_scalar(x_sb[:, t, :], x_sb[:, t, :], r1[:, t:t + 1], None, ALU.mult)
            last.then_inc(S["xn_ready"], 1)
            dve.wait_ge(S["ada1_used"], NC)
            V.tensor_copy(mod1[:].rearrange("p (n m) -> p n m", m=512), ps[0:2, 0:4, :]).then_inc(S["mod1_sb"], 1)
            dve.wait_ge(S["modT_done"], 1)
            own(V.tensor_tensor(modc, ps[:, 4, 0:4 * NC].rearrange("p (c s) -> p c s", s=2),
                                cols[:, 24:40].unsqueeze(2).to_broadcast([P, 2 * NC, 2]), ALU.add))
            own(V.scalar_tensor_tensor(scale1, modc[:, NC:, :], 1.0, g1col.unsqueeze(2).to_broadcast([P, NC, 2]),
                                       ALU.add, ALU.mult))
            dve.wait_ge(S["xT_sb"], NC)
            for c in range(NC):
                for s, a, b in ((0, 0, P), (1, P, TOK)):
                    last = V.tensor_scalar(hT[:, c, a:b], hT[:, c, a:b], scale1[:, c, s:s + 1], modc[:, c, s:s + 1],
                                           ALU.mult, ALU.add)
            last.then_inc(S["h_ready"], 1)

            dve.wait_ge(S["rn_ln"], 2)
            own(V.tensor_scalar(v2[:, 0, :], ss2[:, 0, :], 1.0 / QL, EPS, ALU.mult, ALU.add))
            V.tensor_scalar(v2[:, 1, :], ss2[:, 1, :], 1.0 / KL, EPS, ALU.mult, ALU.add).then_inc(S["rn_in"], 1)
            dve.wait_ge(S["rn_in"], 2)
            root(v2, t2, r2)
            dve.wait_ge(S["consts_in"], 64)
            for t in range(NT):
                last = V.scalar_tensor_tensor(ckvn[:, t, :], mla[:, t, QL:QL + KL], r2[:, 1, t:t + 1], row("g_kv_lora"),
                                              ALU.mult, ALU.mult)
            last.then_inc(S["ckv_ready"], 1)
            for t in range(NT):
                last = V.scalar_tensor_tensor(mla[:, t, 0:QL], mla[:, t, 0:QL], r2[:, 0, t:t + 1], row("g_q_lora"),
                                              ALU.mult, ALU.mult)
            last.then_inc(S["cqn_ready"], 1)
            i = take("ckvT")
            freed(V.tensor_copy(ckvnT[:], i))
            dve.wait_ge(S["proj_done"], proj_no["qk3"] + 1)
            for k in range(4):
                i = take(f"z{k}")
                freed(V.tensor_scalar(decay_m[:, k, :], i[:, 0:TOK], gkcol[:, k:k + 1], None, ALU.add))
            for c in range(2):
                i = take(f"cqT{c}")
                freed(V.tensor_copy(cqT[:, c, :], i[:, 0:TOK]))
            own(V.tensor_scalar(gqs[:], row("g_qk_q"), QK ** -0.5, None, ALU.mult))
            dve.wait_ge(S["gate_l"], 1)
            own(V.scalar_tensor_tensor(decay_m[:], decay_m[:], 0.0, decay_p[:], ALU.min, ALU.subtract))
            for k in range(4):
                for t in range(NT):
                    last = V.tensor_tensor_scan(decay_p[:, k, t * P:(t + 1) * P], ones, decay_m[:, k, t * P:(t + 1) * P],
                                                0.0, ALU.mult, ALU.add)
            own(last)
            seg_p = decay_p[:].rearrange("p k (t j) -> p (k t) j", j=P)
            seg_m = decay_m[:].rearrange("p k (t j) -> p (k t) j", j=P)
            tot = gtot.rearrange("p b t -> p (b t)")
            V.tensor_copy(gsm[:, 2, :].unsqueeze(2), seg_p[:, :, P - 1:P]).then_inc(S["gate_e"], 1)
            dve.wait_ge(S["gate_e"], 1)
            own(V.tensor_tensor(seg_p[:, 6:12, :], seg_m[:, 6:12, :], seg_p[:, 6:12, :], ALU.subtract))
            mid = P // 2 - 1
            V.tensor_copy(gsm[:, 0, 0:6].unsqueeze(2), seg_p[:, 0:6, mid:mid + 1])
            V.tensor_tensor(gsm[:, 0, 6:12].unsqueeze(2), seg_p[:, 6:12, mid:mid + 1], gsm[:, 2, 6:12].unsqueeze(2), ALU.add)
            V.tensor_tensor(gsm[:, 1, 0:6].unsqueeze(2), seg_p[:, 0:6, P - 1:P], seg_p[:, 0:6, mid:mid + 1], ALU.subtract)
            V.tensor_scalar(gsm[:, 1, 6:12].unsqueeze(2), seg_p[:, 6:12, mid:mid + 1], -1.0, None, ALU.mult)
            V.tensor_tensor(seg_m, seg_p, seg_p[:, :, mid:mid + 1].to_broadcast([P, 12, P]), ALU.subtract)\
                .then_inc(S["gate_d"], 1)
            for t in range(4):
                for n in range(2):
                    i = take(f"kv{t}{n}")[:, 0:384].rearrange("p (h w) -> p h w", w=NOPE + VD)
                    V.tensor_copy(key[:, t, 2 * n:2 * n + 2, 0:NOPE], i[:, :, 0:NOPE])
                    freed(V.tensor_copy(val[:, t, 2 * n:2 * n + 2, :], i[:, :, NOPE:]))
            for t in range(NT):
                i = take(f"qm{t}")
                freed(V.tensor_copy(qry[:, t].rearrange("p h w -> p (h w)"), i[:, 0:MH * QK]))
            dve.wait_ge(S["decay_ready"], 3)
            dve.wait_ge(S["proj_sb"], proj_no["qk3"] + 1)
            for d in range(2):
                V.tensor_tensor(decay_p[:, 2 * d:2 * d + 2, :], decay_p[:, 2 * d:2 * d + 2, :], qkT[:, 0:2, :], ALU.mult)
                last = V.tensor_tensor(decay_m[:, 2 * d:2 * d + 2, :], decay_m[:, 2 * d:2 * d + 2, :], qkT[:, 2:4, :], ALU.mult)
            last.then_inc(S["qe_ready"], 1)
            ada(1)

            def qk_norm(z, n, ss, v, t, r, gain, first):
                w = z[:].rearrange("p t h w -> p (t h) w")
                q = sq2[:, 0:n * MH * QK].rearrange("p (a w) -> p a w", w=QK)
                own(V.tensor_tensor(q, w, w, ALU.mult))
                own(V.tensor_reduce(ss.rearrange("p t h -> p (t h)"), q, AX.X, ALU.add))
                V.tensor_scalar(v, ss, 1.0 / QK, EPS, ALU.mult, ALU.add).then_inc(S["rn_in"], 1)
                root(v, t, r)
                own(V.tensor_tensor(w, w, r.rearrange("p t h -> p (t h)").unsqueeze(2).to_broadcast([P, n * MH, QK]), ALU.mult))
                own(V.tensor_tensor(w, w, gain.unsqueeze(1).to_broadcast([P, n * MH, QK]), ALU.mult))
                for k in range(2):
                    rot = z[:, 1 + k, :, NOPE:]
                    c = tc("cos")[:, k * ROPE:(k + 1) * ROPE].unsqueeze(1).to_broadcast([P, MH, ROPE])
                    s = tc("sin")[:, k * ROPE:(k + 1) * ROPE].rearrange("p (a b i) -> p a b i", a=2, b=2)
                    a = sq2[:, 0:MH * ROPE].rearrange("p (h w) -> p h w", h=MH)
                    b = sq2[:, MH * ROPE:2 * MH * ROPE].rearrange("p (h w) -> p h w", h=MH)
                    b4 = b.rearrange("p h (a b i) -> p h a b i", a=2, b=2)
                    r4 = rot.rearrange("p h (a b i) -> p h a b i", a=2, b=2)
                    V.tensor_tensor(a, rot, c, ALU.mult)
                    for half in range(2):
                        last = V.tensor_tensor(b4[:, :, :, half, :], r4[:, :, :, 1 - half, :],
                                               s[:, :, half, :].unsqueeze(1).to_broadcast([P, MH, 2, ROPE // 4]), ALU.mult)
                    own(last)
                    own(V.tensor_tensor(rot, a, b, ALU.add))

            dve.wait_ge(S["krope_ready"], 1)
            qk_norm(key, 4, ssk, vk, tk, rk, row("g_qk_k"), True)
            dve.sem_inc(S["key_ready"], 1)
            ada()
            qk_norm(qry, NT, ssq, vq, tq, rq, gqs[:], False)
            dve.sem_inc(S["qry_ready"], 1)
            ada()
            dve.wait_ge(S["qe_ready"], 1)
            for k, (d, t) in enumerate(combos):
                for b in range(2):
                    last = V.tensor_scalar(kend[:, k, b, :], decay_m[:, d * 2 + b, t * P:(t + 1) * P],
                                           gex[:, 1, d * 6 + b * 3 + t:d * 6 + b * 3 + t + 1], None, ALU.mult)
            last.then_inc(S["kend_ready"], 1)
            ada(2)
            for h in range(MH):
                i = take(f"keyT{h}")
                freed(V.tensor_copy(keyT[:, h, :], i[0:QK, :]))
            for h in range(MH):
                i = take(f"qryT{h}")
                freed(V.tensor_copy(qryT[:, h, :], i[0:QK, 0:TOK]))
            dve.wait_ge(S["proj_done"], proj_no["s0"] + 1)
            V.tensor_reduce(nmax[:, 0, :], pbank("s0").rearrange("p (h k) -> p h k", h=MH), AX.X, ALU.max, negate=True)\
                .then_inc(S["max_ready"], 1)

            def maxima(t):
                for h in range(MH):
                    dve.wait_ge(S["proj_done"], proj_no[f"s{t}{h}"] + 1)
                    V.tensor_reduce(nmax[:, t, h:h + 1], pbank(f"s{t}{h}", TOK), AX.X, ALU.max, negate=True)\
                        .then_inc(S["max_ready"], 1)

            def gla_masks(t):
                if t:
                    dve.wait_ge(S["misc_done"], misc_no[f"o{t - 1}"] + 1)
                m = tc("before")[:, 0:1]
                for par in range(2):
                    i = take(f"A{t}{par}").rearrange("p (a d j) -> p a d j", a=2, d=2)
                    masks = tconst[:, TCW["before"][0]:TCW["before"][0] + 2 * P].rearrange("p (d j) -> p d j", d=2)
                    freed(V.tensor_tensor(attn[:, par], i, masks.unsqueeze(1).to_broadcast([P, 2, 2, P]), ALU.mult))

            def gla_take(t):
                i = take(f"o{t}")
                freed(V.tensor_copy(mixed[:, t, 0:512], i))

            def prob_take(t):
                if t == 2:
                    dve.wait_ge(S["misc_done"], misc_no["pv1"] + 1)
                for h in range(MH):
                    i = take(f"p{t}T{h}")
                    freed(V.tensor_copy(probT[:, h].rearrange("p k q -> p (k q)"), i[:, 0:TOK]))

            def pv_take(t):
                dve.wait_ge(S["prob_ready"], MH + t * MH)
                own(V.reciprocal(rden[:, t, :], psum_p[:, t, :]))
                i = take(f"pv{t}").rearrange("p (h w) -> p h w", h=MH)
                freed(V.tensor_tensor(mixed[:, t, 512:].rearrange("p (h w) -> p h w", h=MH), i,
                                      rden[:, t, :].unsqueeze(2).to_broadcast([P, MH, VD]), ALU.mult))

            maxima(1)
            gla_masks(0)
            ada()
            for n in range(2):
                i = take(f"kendT{n}")
                freed(V.tensor_copy(kendT[:, 2 * n:2 * n + 2].rearrange("p k b j -> p (k b j)"), i))
            ada()
            for n in range(2):
                i = take(f"U{n}")
                freed(V.tensor_copy(state1[:, 2 * n:2 * n + 2].rearrange("p k b j -> p (k b j)"), i))
            dve.wait_ge(S["state_in"], 32)
            dve.wait_ge(S["misc_sb"], misc_no["U1"] + 1)
            dve.wait_ge(S["zero_ready"], 1)

            def g(kind, d, b, t):
                k = d * 6 + b * 3 + t
                return gex[:, kind, k:k + 1]

            for d in range(2):
                near, far = (1, 2) if d == 0 else (2, 1)
                for b in range(2):
                    own(V.scalar_tensor_tensor(state1[:, 2 + d, b, :], state0[:, d, b, :], g(2, d, b, near), state1[:, 2 + d, b, :],
                                               ALU.mult, ALU.add))
                    for hh in range(2):
                        r = slice(hh * GDK, (hh + 1) * GDK)
                        V.tensor_scalar(stateP[r, near - 1, d, 2 * b + hh, :], state0[r, d, b, :], g(0, d, b, near)[r], None, ALU.mult)
                        last = V.tensor_scalar(stateP[r, far - 1, d, 2 * b + hh, :], state1[r, 2 + d, b, :], g(0, d, b, far)[r], None, ALU.mult)
            last.then_inc(S["smp_ready"], 2)
            i = take("p0T")
            freed(V.tensor_copy(prob0T[:].rearrange("p h q -> p (h q)"), i))
            ada()
            gla_take(0)
            prob_take(1)
            ada()
            gla_masks(1)
            pv_take(0)
            pv_take(1)
            maxima(2)
            gla_take(1)
            ada(2)
            dve.wait_ge(S["silu_g"], 2)
            own(V.tensor_scalar(gexp[:], gexp[:], 1.0, None, ALU.add))
            V.reciprocal(gexp[:], gexp[:]).then_inc(S["g1_ready"], 1)
            prob_take(2)
            gla_masks(2)
            ada()
            pv_take(2)
            gla_take(2)
            dve.wait_ge(S["misc_sb"], misc_no["o2"] + 1)
            og = mixed[:, :, 0:512].rearrange("p t (h w) -> p t h w", h=GH)
            for t in range(NT):
                own(V.tensor_tensor(osq[:, 0:512], mixed[:, t, 0:512], mixed[:, t, 0:512], ALU.mult))
                own(V.tensor_reduce(sso[:, t, :], osq[:, 0:512].rearrange("p (h w) -> p h w", h=GH), AX.X, ALU.add))
            V.tensor_scalar(vo, sso, 1.0 / GDV, EPS, ALU.mult, ALU.add).then_inc(S["rn_in"], 1)
            root(vo, to, ro)
            dve.wait_ge(S["mix_ready"], 1)
            for t in range(NT):
                own(V.tensor_tensor(og[:, t], og[:, t], ro[:, t, :].unsqueeze(2).to_broadcast([P, GH, GDV]), ALU.mult))
                V.tensor_tensor(mixed[:, t, 0:512], mixed[:, t, 0:512], g_sb[:, t, :], ALU.mult).then_inc(S["mix_done"], 1)
            ada(NADA)
            def mixed_take(t):
                for n in range(2):
                    i = take(f"mT{t}{n}").rearrange("p (c j) -> p c j", c=4)
                    freed(V.tensor_copy(mixedT[:, 4 * n:4 * n + 4, t * P:(t + 1) * P], i))

            def residual(t):
                s = min(t, 1)
                for n in range(2):
                    h = slice(n * 512, (n + 1) * 512)
                    i = take(f"wo{t}{n}")
                    freed(V.tensor_tensor(xtmp[:, h], i, gt1[:, s, h], ALU.mult))
                    dve.wait_ge(S["misc_sb"], misc_no[f"wo{t}{n}"] + 1)
                    last = V.tensor_tensor(x1[:, t, h], x1[:, t, h], xtmp[:, h], ALU.add)
                last.then_inc(S["x1_ready"], 1)

            def norm2(t):
                s = min(t, 1)
                r = r3[:, t:t + 1]
                dve.wait_ge(S["sq_done"], t + 1)
                V.tensor_scalar(v3[:, t:t + 1], ss3[:, t:t + 1], 1.0 / D, EPS, ALU.mult, ALU.add).then_inc(S["rn_in"], 1)
                root(v3[:, t:t + 1], t3[:, t:t + 1], r)
                own(V.scalar_tensor_tensor(h2[:, t], x1[:, t], r, mul2[:, s], ALU.mult, ALU.mult))
                V.tensor_tensor(h2[:, t], h2[:, t], add2[:, s], ALU.add).then_inc(S["h2_ready"], 1)

            dve.wait_ge(S["x1_in"], 32)
            dve.wait_ge(S["proj_sb"], proj_no["b011"] + 1)
            mixed_take(0)
            residual(0)
            mixed_take(1)
            dve.wait_ge(S["mod_rows"], 1)
            norm2(0)
            residual(1)
            mixed_take(2)
            norm2(1)
            residual(2)
            norm2(2)

            dve.wait_ge(S["gt2_out"], 16)
            V.tensor_copy(strictb, strict)
            V.tensor_copy(onesb, ones)
            V.tensor_copy(identb[:], ident)
            dve.wait_ge(S["score_ready"], NT)
            own(V.tensor_tensor(select, score, row("b_router").unsqueeze(1).to_broadcast([P, NT, NE]), ALU.add))
            for k in range(NT * NG):
                last = V.max(top2[:, k, :], select[:, k // NG, k % NG * 8:k % NG * 8 + 8])
            own(last)
            gs = gscore.rearrange("p t g -> p (t g)")
            own(V.tensor_tensor(gs.unsqueeze(2), top2[:, :, 0:1], top2[:, :, 1:2], ALU.add))
            other = gscore.unsqueeze(2).to_broadcast([P, NT, NG, NG])
            self_ = gscore.unsqueeze(3).to_broadcast([P, NT, NG, NG])
            V.tensor_tensor(gcmp, other, self_, ALU.is_gt)
            own(V.tensor_tensor(gcmp2, other, self_, ALU.is_equal))
            own(V.tensor_tensor(gcmp2.rearrange("p t g h -> p t (g h)"), gcmp2.rearrange("p t g h -> p t (g h)"),
                                tc("earlier").unsqueeze(1).to_broadcast([P, NT, NG * NG]), ALU.mult))
            own(V.tensor_tensor(gcmp, gcmp, gcmp2, ALU.add))
            gr = grank.rearrange("p t g -> p (t g)")
            own(V.tensor_reduce(gr, gcmp.rearrange("p t g h -> p (t g) h"), AX.X, ALU.add))
            gm = gmask.rearrange("p t g -> p (t g)")
            own(V.tensor_scalar(gm, gr, float(TOPG), 1.0, ALU.is_lt, ALU.subtract))
            s3 = select.rearrange("p t (g e) -> p (t g) e", e=8)
            own(V.scalar_tensor_tensor(s3, gm.unsqueeze(2).to_broadcast([P, NT * NG, 8]), 1e30, s3, ALU.mult, ALU.add))
            for t in range(NT):
                last = V.max(top8[:, t, :], select[:, t, :])
            own(last)
            for t in range(NT):
                last = V.match_replace(picked[:, t, :], top8[:, t, :], select[:, t, :], 2e30)
            own(last)
            own(V.tensor_scalar(picked, picked, 1e30, None, ALU.is_ge))
            V.tensor_copy(maskb, picked).then_inc(S["mask_ready"], 1)
            own(V.tensor_tensor(weight, score, picked, ALU.mult))
            own(V.tensor_reduce(wsum, weight, AX.X, ALU.add))
            own(V.reciprocal(wsum, wsum))
            own(V.scalar_tensor_tensor(weight, weight, SCALE_OUT, wsum.unsqueeze(2).to_broadcast([P, NT, NE]), ALU.mult, ALU.mult))

            def shared_act(t):
                dve.wait_ge(S["sh_sil_ready"], t + 1)
                i = take(f"sg{t}")
                freed(V.tensor_tensor(sh_a[t][:], i[:, DE:], sh_sil[:], ALU.mult))
                dve.wait_ge(S["misc_sb"], misc_no[f"sg{t}"] + 1)
                dve.sem_inc(S["sh_a_ready"], 1)

            shared_act(0)
            shared_act(1)
            i = take("pos")
            freed(V.scalar_tensor_tensor(posp, i[:, 0:NT * NE].rearrange("p (t e) -> p t e", t=NT), 1.0, picked, ALU.add, ALU.mult))
            i = take("cnt")
            freed(V.tensor_copy(cnt[0:NE], i[0:NE, 0:1]))
            own(V.tensor_scalar(thr[0:NE], tc("over")[0:NE, 1:6], float(SLOT), None, ALU.mult))
            dve.wait_ge(S["misc_sb"], misc_no["cnt"] + 1)
            own(V.tensor_scalar(cmpc[0:NE], thr[0:NE], cnt[0:NE], None, ALU.is_lt))
            V.tensor_reduce(nov[0:NE], cmpc[0:NE], AX.X, ALU.add).then_inc(S["cnt_sb"], 1)
            dve.wait_ge(S["cnt_sb"], 1)
            i = take("start")
            freed(V.tensor_copy(start[0:NE], i[0:NE, 0:1]))
            dve.wait_ge(S["misc_sb"], misc_no["start"] + 1)
            own(V.tensor_tensor(end[0:NE], start[0:NE], nov[0:NE], ALU.add))
            ov = tc("over")[0:NE]
            own(V.tensor_scalar(owner[0:NE], ov, start[0:NE], None, ALU.is_ge))
            own(V.tensor_scalar(owner2[0:NE], ov, end[0:NE], None, ALU.is_lt))
            own(V.tensor_tensor(owner[0:NE], owner[0:NE], owner2[0:NE], ALU.mult))
            own(V.tensor_scalar(offs[0:NE], ov, start[0:NE], 1.0, ALU.subtract, ALU.add))
            V.scalar_tensor_tensor(offs[0:NE], offs[0:NE], float(SLOT), owner[0:NE], ALU.mult, ALU.mult).then_inc(S["owner_ready"], 1)
            shared_act(2)
            i = take("tabP")
            freed(V.tensor_copy(poT[0:NE].rearrange("p t j -> p (t j)"), i[0:NE, 0:TOK]))
            i = take("tabG")
            freed(V.tensor_copy(gaT[0:NE].rearrange("p t j -> p (t j)"), i[0:NE, 0:TOK]))
            i = take("tabO")
            own(V.tensor_copy(offrow, i[:, 0:NOVER]))
            own(V.tensor_scalar(grow, tc("over")[:, 0:NOVER // JG], float(JG), i[:, 2 * NOVER:2 * NOVER + 1], ALU.mult, ALU.is_lt))
            own(V.tensor_copy(erow[:, NE:NJ], i[:, NOVER:2 * NOVER]))
            freed(V.memset(erow[:, NJ:], 0.0))
            own(V.tensor_copy(erow[:, 0:NE], slotrow[:, 0:NE]))
            own(V.tensor_reduce(gcount, grow, AX.X, ALU.add))
            own(V.tensor_scalar(gcount, gcount, float(NE // JG), None, ALU.add))
            V.tensor_copy(jobs[0:1, NJP:NJP + 1], gcount[0:1])
            V.tensor_copy(jobs[0:1, 0:NJP], erow[0:1])
            i = take("tabJ")
            own(V.tensor_scalar(posj[:, :, 0:NE], posp, -1.0, None, ALU.add))
            own(V.scalar_tensor_tensor(posj[:, :, NE:NJ], i[:, 0:NT * NOVER].rearrange("p (t j) -> p t j", t=NT), -1.0,
                                       offrow.unsqueeze(1).to_broadcast([P, NT, NOVER]), ALU.add, ALU.subtract))
            V.memset(posj[:, :, NJ:], -1.0)
            V.tensor_copy(gjob[:, :, 0:NE], weight)
            V.memset(gjob[:, :, NJ:], 0.0)
            freed(V.tensor_copy(gjob[:, :, NE:NJ], i[:, NT * NOVER:2 * NT * NOVER].rearrange("p (t j) -> p t j", t=NT)))
            dve.wait_ge(S["misc_sb"], misc_no["tabJ"] + 1)
            own(V.tensor_copy(gparts[:, :, :, 0], gjob))
            own(V.tensor_tensor(gjob, gjob, gparts[:, :, :, 0], ALU.subtract))
            own(V.tensor_copy(gparts[:, :, :, 1], gjob))
            own(V.tensor_tensor(gjob, gjob, gparts[:, :, :, 1], ALU.subtract))
            own(V.tensor_copy(gparts[:, :, :, 2], gjob))
            dve.sem_inc(S["jobs_ready"], 1)
            dve.wait_ge(S["h2s_ready"], 1)
            for t in range(NT):
                i = take(f"sa{t}")
                if t:
                    dve.wait_ge(S["misc_done"], misc_no[f"sd{t - 1}1"] + 1)
                freed(V.tensor_copy(sh_aT[:].rearrange("p f j -> p (f j)"), i[:, 0:2 * P]))
                for n in range(2):
                    i = take(f"sd{t}{n}")
                    freed(V.tensor_copy(acc[:, t, n * 512:(n + 1) * 512], i))
            dve.wait_ge(S["misc_sb"], len(misc))
            dve.sem_inc(S["shared_done"], 1)

            dve.wait_ge(S["x1_out"], 16 * NT)
            for s, n in (("lo_gu_dve", 2), ("lo_d4", 2), ("gu_sum", 2), ("a_ready", 1), ("al_done", 1), ("yl_done", 2), ("acc_done", 6)):
                dve.sem_inc(S[s], n)

            def low_gu(g, j, u):
                dve.wait_ge(S["hi_gu"], 4 * (JG * g + j) + u + 1)
                three = lambda w: w.rearrange("p (m c) -> p m c", m=2)
                V.tensor_tensor(three(wl[u][:]), raw_gu[j % 2][:, :, 2 * u:2 * u + 2, :].rearrange("p m c n -> p m (c n)"),
                                three(wh[u][:].bitcast(F32)), ALU.subtract).then_inc(S["lo_gu_dve"], 1)

            def split_dn(g, j):
                dve.wait_ge(raw_dn_in[j % 2], 16 * (2 * g + j // 2 + 1))
                dve.wait_ge(S["dn_used"], 2 * (JG * g + j) + 4)
                V.tensor_copy(wh[5][:], raw_dn[j % 2][:, 1]).then_inc(S["hi_d5"], 1)
                dve.wait_ge(S["hi_d4"], JG * g + j + 1)
                V.tensor_tensor(wl[4][:], raw_dn[j % 2][:, 0], wh[4][:].bitcast(F32), ALU.subtract).then_inc(S["lo_d4"], 1)

            def sum_up(g, j):
                dve.wait_ge(S["half_up"], JG * g + j + 1)
                u = gu[:].rearrange("p m n -> p (m n)")
                V.tensor_tensor(u, ps[0:SLOT, j % 2, :], u, ALU.add).then_inc(S["gu_sum"], 1)

            def gated(g, j):
                dve.wait_ge(S["silu_done"], JG * g + j + 1)
                dve.wait_ge(S["aT_done"], JG * g + j + 1)
                V.scalar_tensor_tensor(act_a[j % 2][:], gu[:, 1], gslot[0:SLOT, j:j + 1], sil[:], ALU.mult, ALU.mult)\
                    .then_inc(S["a_ready"], 1)

            def place_take(g, j):
                dve.wait_ge(S["place_mm"], 5 * g + 2 + j)
                dve.wait_ge(S["scatter_done"], 6 * g + 6)
                V.tensor_copy(place[:, j, :], ps[:, 5, 0:TOK]).then_inc(S["b5_sb"], 1)

            def low_a(g, j):
                dve.wait_ge(S["ah_done"], JG * g + j + 1)
                a = ast[j % 2]
                V.tensor_tensor(a[:, :, 1, :], ps[:, 4, 0:2 * SLOT].rearrange("p (f s) -> p f s", f=2),
                                a[:].bitcast(F32)[:, :, 0, :], ALU.subtract).then_inc(S["al_done"], 1)

            def low_y(g, j):
                for n in range(2):
                    dve.wait_ge(S["yh_done"], 2 * (JG * g + j) + n + 1)
                    h = slice(n * 512, (n + 1) * 512)
                    V.tensor_tensor(yl[:, j, h], ps[:, 2 + n, :], yh[:].bitcast(F32)[:, j, h], ALU.subtract).then_inc(S["yl_done"], 1)

            def pick_slots(cols_):
                i = slotrow.rearrange("p (j s) -> p j s", j=JG).unsqueeze(1).to_broadcast([P, NT, JG, SLOT])
                k = cols_.unsqueeze(3).to_broadcast([P, NT, JG, SLOT])
                return i, k

            def tokens(g, c):
                dve.wait_ge(S["gather_done"], NC * (g + 1) + c + 1)
                V.tensor_copy(xs[:, :, c], ps[:, 7, :].rearrange("p (z j s) -> p j z s", z=2, j=JG)).then_inc(S["xs_dve"], 1)

            def gates(n):
                dve.wait_ge(S["place_mm"], n)
                V.tensor_reduce(gslot[0:SLOT, :], ps[0:SLOT, 5, 0:4 * JG].rearrange("p (j k) -> p j k", k=4)[:, :, 0:3],
                                AX.X, ALU.add).then_inc(S["b5_sb"], 1)

            pick4 = pick[:].rearrange("p t (j s) -> p t j s", j=JG)
            i, k = pick_slots(posj[:, :, 0:JG])
            V.tensor_tensor(pick4, i, k, ALU.is_equal).then_inc(S["pick_ready"], 1)
            V.tensor_tensor(pickb[:], i, k, ALU.is_equal).then_inc(S["pickb_ready"], 1)
            low_gu(0, 0, 0)
            low_gu(0, 0, 2)
            for c in range(1, NC, 2):
                dve.wait_ge(S["gather_done"], c + 1)
                V.tensor_copy(xs[:, :, c], ps[:, 7, :].rearrange("p (z j s) -> p j z s", z=2, j=JG)).then_inc(S["xs_dve"], 1)
            gates(1)
            n_groups = dve.value_load(jobs[0:1, NJP:NJP + 1], min_val=NE // JG, max_val=NJ // JG)
            with dve.Fori(0, n_groups) as g:
                low_gu(g, 1, 0)
                low_gu(g, 1, 2)
                sum_up(g, 0)
                dve.wait_ge(S["b5_sb"], 5 * g + 1)
                gated(g, 0)
                place_take(g, 0)
                low_gu(g, 2, 0)
                low_gu(g, 2, 2)
                sum_up(g, 1)
                gated(g, 1)
                place_take(g, 1)
                split_dn(g, 0)
                low_gu(g, 3, 0)
                low_a(g, 0)
                low_gu(g, 3, 2)
                sum_up(g, 2)
                gated(g, 2)
                place_take(g, 2)
                split_dn(g, 1)
                low_y(g, 0)
                low_gu(g, 4, 0)
                low_a(g, 1)
                low_gu(g, 4, 2)
                sum_up(g, 3)
                gated(g, 3)
                place_take(g, 3)
                i, k = pick_slots(posj[:, :, bass.ds(g * JG + JG, JG)])
                dve.wait_ge(S["gather_done"], NC * g + NC)
                V.tensor_tensor(pick4, i, k, ALU.is_equal).then_inc(S["pick_ready"], 1)
                low_y(g, 1)
                dve.wait_ge(S["place_mm"], 5 * g + 5)
                V.tensor_tensor(pickb[:], i, k, ALU.is_equal).then_inc(S["pickb_ready"], 1)
                split_dn(g, 2)
                low_a(g, 2)
                tokens(g, 1)
                tokens(g, 3)
                low_y(g, 2)
                split_dn(g, 3)
                low_a(g, 3)
                tokens(g, 5)
                tokens(g, 7)
                dve.wait_ge(S["a_ready"], JG * g + JG + 1)
                gates(5 * g + 6)
                low_y(g, 3)
                for m in range(6):
                    dve.wait_ge(S["scatter_done"], 6 * g + m + 7)
                    dve.wait_ge(S["acc_done"], 6 * g + m + 1)
                    a = acc[:, m // 2, m % 2 * 512:(m % 2 + 1) * 512]
                    V.tensor_tensor(a, a, ps[:, 6 + m % 2, :], ALU.add).then_inc(S["acc_done"], 1)
            dve.wait_ge(S["acc_done"], 6 * n_groups + 6)
            dve.sem_inc(S["tail_ready"], 1)
            dve.wait_ge(S["tail_in"], 48)
            for t in range(NT):
                own(V.tensor_tensor(acc[:, t], acc[:, t], gt2[:, min(t, 1)], ALU.mult))
                V.tensor_tensor(x1b[:, t], x1b[:, t], acc[:, t], ALU.add).then_inc(S["y_ready"], 1)

        @block.gpsimd
        def _(pool):
            G = nc.gpsimd
            pool.wait_ge(S["cache_in"], 32)
            pool.wait_ge(S["proj_sb"], proj_no["mla2"] + 1)
            for t in range(NT):
                i = G.tensor_copy(krope[:, t, :], mla[:, t, QL + KL:])
                i.then_inc(S["pool_chain"], 1)
            pool.wait_ge(S["pool_chain"], NT)
            for t in range(4):
                i = G.tensor_copy(key[:, t, :, NOPE:], krope[:, t, :].unsqueeze(1).to_broadcast([P, MH, ROPE]))
                i.then_inc(S["pool_chain"], 1)
            pool.wait_ge(S["pool_chain"], NT + 4)
            pool.sem_inc(S["krope_ready"], 1)
            pool.wait_ge(S["qe_ready"], 1)
            G.memset(stateP[:], 0.0).then_inc(S["zero_ready"], 1)
            pool.wait_ge(S["g1_ready"], 1)
            pool.wait_ge(S["proj_sb"], proj_no["g2"] + 1)
            G.tensor_tensor(g_sb[:], g_sb[:], gexp[:], ALU.mult).then_inc(S["pool_chain"], 1)
            pool.wait_ge(S["pool_chain"], NT + 5)
            gw = g_sb[:].rearrange("p t (h w) -> p (t h) w", h=GH)
            G.tensor_tensor(gw, gw, row("g_gla_out").unsqueeze(1).to_broadcast([P, NT * GH, GDV]), ALU.mult)\
                .then_inc(S["mix_ready"], 1)
            pool.wait_ge(S["proj_sb"], proj_no["b211"] + 1)
            pool.wait_ge(S["g2_in"], 16)
            G.tensor_tensor(mul2[:], mul2[:], g2row[:].unsqueeze(1).to_broadcast([P, 2, D]), ALU.mult).then_inc(S["mod_rows"], 1)
            for t in range(NT):
                pool.wait_ge(S["h2h_ready"], t + 1)
                G.tensor_tensor(h2l[:, t], h2[:, t].rearrange("p (j c) -> p c j", c=NC), h2h[:].bitcast(F32)[:, t], ALU.subtract)\
                    .then_inc(S["h2l_ready"], 1)
            pool.wait_ge(S["h2l_ready"], NT)
            pool.sem_inc(S["h2s_ready"], 1)

            pool.wait_ge(S["shared_done"], 1)
            pool.sem_inc(S["lo_gu_pool"], 2)
            pool.sem_inc(S["lo_d5"], 2)

            def low_gu(g, j):
                for u in (1, 3):
                    pool.wait_ge(S["hi_gu"], 4 * (JG * g + j) + u + 1)
                    three = lambda w: w.rearrange("p (m c) -> p m c", m=2)
                    G.tensor_tensor(three(wl[u][:]), raw_gu[j % 2][:, :, 2 * u:2 * u + 2, :].rearrange("p m c n -> p m (c n)"),
                                    three(wh[u][:].bitcast(F32)), ALU.subtract).then_inc(S["lo_gu_pool"], 1)

            def low_dn(g, j):
                pool.wait_ge(S["hi_d5"], JG * g + j + 1)
                G.tensor_tensor(wl[5][:], raw_dn[j % 2][:, 1], wh[5][:].bitcast(F32), ALU.subtract).then_inc(S["lo_d5"], 1)

            low_gu(0, 0)
            n_groups = pool.value_load(jobs[0:1, NJP:NJP + 1], min_val=NE // JG, max_val=NJ // JG)
            with pool.Fori(0, n_groups) as g:
                for kind, j in SPLITS:
                    (low_gu if kind == "gu" else low_dn)(g, j)


_OUTS = [("y_prompt", (1, P, D)), ("y_sample", (1, 2 * P, D)), ("new_fwd", (1, 1, GH, GDK, GDV)),
         ("new_bwd", (1, 1, GH, GDK, GDV)), ("new_ckv", (1, 1, P, KL)), ("new_krope", (1, 1, P, ROPE))]
_WHOLE = ("x_prompt", "x_sample", "state_gla_fwd", "state_gla_bwd", "cache_mla_ckv", "cache_mla_krope", "w_ada", "b_ada",
          "g_norm2", "w_in", "w_uq", "w_ukv", "w_out", "w_router", "w_exp_gate", "w_exp_up", "w_exp_down", "w_sh_gate",
          "w_sh_up", "w_sh_down")


def kernel(**inputs):
    import numpy as _np
    import concourse.bacc as _bacc
    from concourse import mybir as _mybir
    from concourse.bass_utils import run_bass_kernel_spmd as _run

    a = {n: _np.ascontiguousarray(v) for n, v in inputs.items()}
    arrays = {n: a[n] for n in _WHOLE}
    pc = lambda v: v.reshape(P, NC)
    arrays["c_cols"] = _np.ascontiguousarray(_np.concatenate(
        [pc(a["c_ctx"]), pc(a["c"][0]), pc(a["g_norm1"][0]), pc(a["b_ada"][0, 0:D]), pc(a["b_ada"][0, D:2 * D]),
         a["b_gk_fwd"][0].reshape(2, P).T, a["b_gk_bwd"][0].reshape(2, P).T], 1))
    arrays["c_rows"] = _np.concatenate([a[n][0] for n in ("g_gla_out", "g_q_lora", "g_kv_lora", "g_qk_q", "g_qk_k",
                                                          "b_router")])[None]
    gates = _np.zeros((32, 2, 2, P), _np.float32)
    gates[0:16, 0] = a["w_gk_fwd"][0].reshape(16, 2, P)
    gates[16:32, 1] = a["w_gk_bwd"][0].reshape(16, 2, P)
    arrays["c_wgk"] = gates
    const = shape_constants()
    part = lambda n: const[:, CW[n][0]:CW[n][0] + CW[n][1]]
    kept = ("ident", "strict", "ones", "slot")
    arrays["c_keep"] = _np.ascontiguousarray(_np.concatenate([part(n) for n in kept], 1))
    arrays["c_trunk"] = _np.ascontiguousarray(_np.concatenate([part(n) for n in CW if n not in kept], 1))

    nc = _bacc.Bacc("TRN2", target_bir_lowering=False, num_devices=1)
    A = {n: nc.dram_tensor(f"in_{n}", v.shape, _mybir.dt.from_np(v.dtype), kind="ExternalInput").ap()
         for n, v in arrays.items()}
    O = {n: nc.dram_tensor(f"out_{n}", s, _mybir.dt.float32, kind="ExternalOutput").ap() for n, s in _OUTS}
    build(nc, A, O)
    r = _run(nc, [{f"in_{n}": v for n, v in arrays.items()}], core_ids=[0])
    return tuple(r.results[0][f"out_{n}"] for n, _ in _OUTS)
```

```python
from contextlib import ExitStack

import numpy as np
import concourse.bass as bass
from concourse import mybir

F32 = mybir.dt.float32
F32R = mybir.dt.float32r
BF16 = mybir.dt.bfloat16
I32 = mybir.dt.int32
ALU = mybir.AluOpType
ACT = mybir.ActivationFunctionType
AX = mybir.AxisListType

P = 128
D = 1024
NC = D // P
NT = 3
TOK = NT * P
EPS = 1e-6
GH, GDK, GDV = 4, 64, 128
MH, NOPE, ROPE, VD = 4, 64, 32, 128
QK = NOPE + ROPE
QL, KL = 256, 128
NE, NG, TOPG, TOPK, DE = 64, 8, 4, 8, 256
SCALE_OUT = 2.5
GATE_NORM = 16.0
GRID_W = 64
THETA = 10000.0
SLOT = 64
JG = 4
NOVER = 48
NJ = NE + NOVER


def shape_constants():
    i = np.arange(P)
    ident = np.eye(P, dtype=np.float32)
    before = (i[:, None] <= i[None, :]).astype(np.float32)
    after = (i[:, None] >= i[None, :]).astype(np.float32)
    strict = (i[:, None] < i[None, :]).astype(np.float32)
    half = ROPE // 4
    freq = THETA ** (-np.arange(half, dtype=np.float32) / half)
    pos = np.arange(2 * P)
    ang = np.stack([(pos // GRID_W)[:, None] * freq, (pos % GRID_W)[:, None] * freq], 1)
    ang = ang.astype(np.float32)
    cos, sin = np.cos(ang), np.sin(ang)
    c = np.stack([cos, cos], 2).reshape(2, P, ROPE).transpose(1, 0, 2).reshape(P, 2 * ROPE)
    s = np.stack([-sin, sin], 2).reshape(2, P, ROPE).transpose(1, 0, 2).reshape(P, 2 * ROPE)
    slot = np.broadcast_to((np.arange(JG * SLOT) % SLOT).astype(np.float32), (P, JG * SLOT))
    earlier = np.broadcast_to((np.arange(NG)[None, :] < np.arange(NG)[:, None]).reshape(1, NG * NG), (P, NG * NG))
    over = np.broadcast_to(np.arange(NOVER).astype(np.float32), (P, NOVER))
    sel = np.zeros((P, 2, P), np.float32)
    sel[0, 0] = sel[1, 1] = 1.0
    return np.ascontiguousarray(np.concatenate(
        [ident, before, after, strict, c, s, slot, earlier, over, i[:, None], sel.reshape(P, 2 * P),
         np.ones((P, P))], 1).astype(np.float32))


CW = {}
_o = 0
for _n, _w in (("ident", P), ("before", P), ("after", P), ("strict", P), ("cos", 2 * ROPE), ("sin", 2 * ROPE),
               ("slot", JG * SLOT), ("earlier", NG * NG), ("over", NOVER), ("index", 1), ("sel", 2 * P), ("ones", P)):
    CW[_n] = (_o, _w)
    _o += _w
CONST_W = _o

RW = {}
_o = 0
for _n, _w in (("g_gla_out", GDV), ("g_q_lora", QL), ("g_kv_lora", KL), ("g_qk_q", QK), ("g_qk_k", QK), ("b_router", NE)):
    RW[_n] = (_o, _w)
    _o += _w
ROW_W = _o

SPLITS = (("gu", 2), ("dn", 1), ("gu", 3), ("dn", 2), ("gu", 4), ("dn", 3), ("gu", 5), ("dn", 4))


KB = 1024


def rows_pc(w, n):
    return w.rearrange("(p c) n -> p c n", c=NC)


def build(nc, A, O):
    ctx = ExitStack()
    with ctx:
        base = (nc.sbuf_base + 63) // 64 * 64

        def at(name, off, shape, dt=F32):
            return nc.alloc_sbuf_tensor_at(name, shape, dt, offset=base + int(off * KB))

        def sem(name):
            return ctx.enter_context(nc.semaphore(name))

        keep = at("keep", 0, [P, 3 * P + JG * SLOT])
        small = at("small", 2.5, [P, 600])
        x_sb = at("x_sb", 10, [P, NT, D])
        prob = at("prob", 10, [P, MH, TOK])
        cqT = at("cqT", 16, [P, 2, TOK])
        ckvnT = at("ckvnT", 19, [P, 4 * P])
        hT = at("hT", 22, [P, NC, TOK])
        probT = at("probT", 22, [P, MH, NT, P])
        prob0 = at("prob0", 28, [P, MH, P])
        prob0T = at("prob0T", 30, [P, MH, P])
        mixedT = at("mixedT", 22, [P, NC, TOK])
        mixed = at("mixed", 34, [P, NT, D])
        mla = at("mla", 46, [P, NT, QL + KL + ROPE])
        val = at("val", 50.875, [P, 4, MH, VD])
        key = at("key", 58.875, [P, 4, MH, QK])
        qry = at("qry", 64.875, [P, NT, MH, QK])
        keyT = at("keyT", 69.375, [QK, MH, 4 * P])
        qryT = at("qryT", 77.375, [QK, MH, TOK])
        tconst = at("tconst", 83.375, [P, CONST_W - 3 * P - JG * SLOT])
        rows = at("rows", 87.25, [P, ROW_W])
        krope = at("krope", 90.25, [P, 4, ROPE])
        ckvn = at("ckvn", 90.75, [P, 4, KL])
        cols = at("cols", 92.75, [P, 80])
        w_mla = at("w_mla", 94, [P, NC, 448])
        w_qk = at("w_qk", 108, [P, NC, 512])
        w_v = at("w_v", 124, [P, NC, 512])
        w_g = at("w_g", 140, [P, NC, 512])
        w_out = at("w_out", 124, [P, NC, D])
        decay_p = at("decay_p", 94, [P, 4, TOK])
        decay_m = at("decay_m", 100, [P, 4, TOK])
        kend = at("kend", 106, [P, 4, 2, P])
        kendT = at("kendT", 110, [P, 4, 2, P])
        attn = at("attn", 114, [P, 2, 2, 2, P])
        state0 = at("state0", 118, [P, 2, 2, GDV])
        state1 = at("state1", 120, [P, 4, 2, GDV])
        ada1 = at("ada1", 156, [P, 4, 2 * D])
        ada2 = at("ada2", 156, [P, NC, 256])
        w_uq = at("w_uq", 164, [P, 2, MH * QK])
        w_ukv = at("w_ukv", 167, [P, MH * (NOPE + VD)])
        modrow = at("modrow", 171, [2, 4 * D])
        v_sb = at("v_sb", 187, [P, NT, GH * GDV])
        g_sb = at("g_sb", 193, [P, NT, GH * GDV])
        qkT = at("qkT", 199, [P, 4, TOK])
        stateP = at("stateP", 199, [P, 2, 2, GH, GDV])
        mod1 = at("mod1", 34, [2, 2 * D])
        sq = at("sq", 42, [P, D])
        sq2 = at("sq2", 34, [P, 4 * MH * QK])
        osq = at("osq", 10, [P, GH * GDV])
        gexp = at("gexp", 16, [P, NT, GH * GDV])

        ident, strict, ones = (keep[:, k * P:(k + 1) * P] for k in range(3))
        slotrow = keep[:, 3 * P:3 * P + JG * SLOT]
        TCW, o = {}, 0
        for n, (_, w) in CW.items():
            if n not in ("ident", "strict", "ones", "slot"):
                TCW[n] = (o, w)
                o += w

        def tc(n):
            return tconst[:, TCW[n][0]:TCW[n][0] + TCW[n][1]]

        def row(n):
            return rows[:, RW[n][0]:RW[n][0] + RW[n][1]]

        small_used = [0]

        def sm(*shape):
            n = int(np.prod(shape))
            a = small[:, small_used[0]:small_used[0] + n]
            small_used[0] += n
            if len(shape) == 2:
                a = a.rearrange("p (a b) -> p a b", b=shape[1])
            if len(shape) == 3:
                a = a.rearrange("p (a b c) -> p a b c", b=shape[1], c=shape[2])
            return a

        ccol = cols[:, 0:16].rearrange("p (s c) -> p s c", s=2)
        g1col = cols[:, 16:24]
        bcol = cols[:, 24:40].rearrange("p (j c) -> p j c", j=2)
        gkcol = cols[:, 40:44]
        silu_c = sm(NC, 2)
        cexp = sm(2, NC)
        ss1 = sm(NT)
        v1 = sm(NT)
        r1 = sm(NT)
        t1 = sm(NT)
        modc = sm(2 * NC, 2)
        scale1 = sm(NC, 2)
        wgk = at("wgk", 5.5, [32, 2, 2, P])
        lrT = at("lrT", 7.5, [32, TOK])
        ss2, v2, r2, t2 = sm(2, NT), sm(2, NT), sm(2, NT), sm(2, NT)
        ssk, vk, rk, tk = sm(4, MH), sm(4, MH), sm(4, MH), sm(4, MH)
        ssq, vq, rq, tq = sm(NT, MH), sm(NT, MH), sm(NT, MH), sm(NT, MH)
        sso, vo, ro, to = sm(NT, MH), sm(NT, MH), sm(NT, MH), sm(NT, MH)
        nmax, psum_p, rden = sm(NT, MH), sm(NT, MH), sm(NT, MH)
        gsm = sm(3, 12)
        gex = sm(3, 12)
        gtot = sm(2, NT)
        gqs = at("gqs", 9.0, [P, QK])

        ps = ctx.enter_context(nc.psum_tensor("ps", [P, 8, 512], F32))

        names = ("consts_in x_in cols_in w_mla_in w_qk_in w_v_in w_g_in w_u_in cache_in state_in brow_in ada2_in "
                 "w_out_in silu_ready mod1_sb modT_done xn_ready h_ready xT_done xT_sb proj_done proj_sb "
                 "ada1_used misc_done misc_sb rn_in rn_ln rn_out cqn_ready ckv_ready gate_e gate_l gate_d "
                 "decay_ready qe_ready kend_ready smp_ready krope_ready key_ready qry_ready max_ready prob_ready "
                 "silu_g mix_ready ada2_done ada2_sb dve_chain act_chain pool_chain out_done zero_ready g1_ready "
                 "mix_done").split()
        S = {n: sem(n) for n in names}
        ada1_in = [sem(f"ada1_in{k}") for k in range(4)]
        gt1 = at("gt1", 94, [P, 2, D])
        mul2 = at("mul2", 102, [P, 2, D])
        add2 = at("add2", 110, [P, 2, D])
        xtmp = at("xtmp", 118, [P, D])
        w_router = at("w_router", 122, [P, NC, NE])
        x1 = at("x1", 188, [P, NT, D])
        sq3 = at("sq3", 200, [P, D])
        g2row = at("g2row", 58, [P, D])
        h2 = at("h2", 34, [P, NT, D])
        h2T = at("h2T", 46, [P, NC, TOK])
        h2h = at("h2h", 10, [P, NT, NC, P], F32R)
        h2l = at("h2l", 22, [P, NT, NC, P], F32R)
        w_shgu = at("w_shgu", 156, [P, 2, NC, DE])
        w_shd = at("w_shd", 172, [P, 2, D])
        sh_sil = at("sh_sil", 180, [P, DE])
        sh_a = [at(f"sh_a{t}", 181 + t, [P, DE]) for t in range(NT)]
        sh_aT = at("sh_aT", 185.25, [P, 2, P])
        acc = at("acc", 34, [P, NT, D])
        rt = at("rt", 142, [P, 3500])
        rtb = at("rtb", 184, [P, 3 * NE + 3 * P], BF16)
        NJP = NJ + 2 * JG
        posj = at("posj", 5.5, [P, NT, NJP])
        gparts = at("gparts", 7, [P, NT, NJP, 3], BF16)
        jobs = at("jobs", 9.125, [1, NJP + 4], I32)
        identb = at("identb", 9.625, [P, P], BF16)
        raw_gu = [at(f"raw_gu{k}", 62 + 16 * k, [P, 2, NC, DE]) for k in range(2)]
        raw_dn = [at(f"raw_dn{k}", 46 + 8 * k, [P, 2, D]) for k in range(2)]
        wh = [at(f"wh{u}", 94 + 4 * u, [P, D], F32R) for u in range(6)]
        wl = [at(f"wl{u}", 118 + 4 * u, [P, D], F32R) for u in range(6)]
        xs = [at(f"xs{k}", 142 + 16 * k, [P, JG, NC, 2, SLOT], F32R) for k in range(2)]
        ys = at("ys", 174, [P, JG, D], F32R)
        pick = at("pick", 190, [P, NT, JG * SLOT], F32R)
        pickb = at("pickb", 193, [P, NT, JG, SLOT], BF16)
        place = at("place", 194.5, [P, JG, TOK], F32R)
        shared = at("shared", 200.5, [P, D])
        HI = slice(SLOT, 2 * SLOT)
        yt, gu, sil = shared[0:SLOT, :], shared[HI, 0:2 * DE], shared[HI, 2 * DE:3 * DE]
        act_a = [shared[:, 3 * DE:], at("act_a1", 206.625, [P, DE])]
        ast = [at(f"ast{k}", 204.5 + k, [P, 2, 2, SLOT], F32R) for k in range(2)]
        gslot = at("gslot", 206.5, [P, JG])
        x1b = at("x1b", 10, [P, NT, D])
        gt2 = at("gt2", 22, [P, 2, D])
        x1_dram = nc.dram_tensor("x1_spill", [P, NT, D], F32, kind="Internal").ap()
        gt2_dram = nc.dram_tensor("gt2_spill", [2, D], F32, kind="Internal").ap()

        rt_used = [0]

        def rtile(*shape):
            n = int(np.prod(shape))
            a = rt[:, rt_used[0]:rt_used[0] + n]
            rt_used[0] += n
            assert rt_used[0] <= 3500
            if len(shape) == 2:
                a = a.rearrange("p (a b) -> p a b", b=shape[1])
            if len(shape) == 3:
                a = a.rearrange("p (a b c) -> p a b c", b=shape[1], c=shape[2])
            return a

        score, select, weight, picked = (rtile(NT, NE) for _ in range(4))
        top2 = rtile(NT * NG, 8)
        gscore, grank, gmask = rtile(NT, NG), rtile(NT, NG), rtile(NT, NG)
        gcmp, gcmp2 = rtile(NT, NG, NG), rtile(NT, NG, NG)
        top8 = rtile(NT, 8)
        wsum = rtile(NT)
        posp = rtile(NT, NE)
        cnt, nov, start, end = rtile(1), rtile(1), rtile(1), rtile(1)
        thr, cmpc = rtile(5), rtile(5)
        owner, owner2, offs = rtile(NOVER), rtile(NOVER), rtile(NOVER)
        poT, gaT = rtile(NT, P), rtile(NT, P)
        offrow, erow = rtile(NOVER), rtile(NJP)
        gjob = rtile(NT, NJP)
        grow, gcount = rtile(NOVER // (2 * JG)), rtile(1)
        maskb = rtb[:, 0:3 * NE].rearrange("p (t e) -> p t e", e=NE)
        strictb, onesb = rtb[:, 3 * NE:3 * NE + P], rtb[:, 3 * NE + P:3 * NE + 2 * P]
        ss3, v3, r3, t3 = sm(NT), sm(NT), sm(NT), sm(NT)

        names2 = ("x1_in w_router_in shgu_in shd_in g2_in mod_rows gt2_out x1_out x1_ready sq_done h2_ready "
                 "h2s_ready score_ready mask_ready cnt_sb owner_ready jobs_ready sh_sil_ready sh_a_ready hi_gu "
                 "lo_gu_dve lo_gu_pool hi_d4 hi_d5 lo_d4 lo_d5 gu_used dn_used half_up gu_sum silu_done a_ready "
                 "aT_done ah_done al_done y_half y_sum yh_done yl_dve yl_pool zeroed pick_ready pickb_ready "
                 "gather_done place_mm scatter_done acc_done tail_in y_ready y_out shared_done xs_act xs_dve "
                 "b5_sb h2h_ready h2l_ready").split()
        S.update({n: sem(n) for n in names2})
        raw_gu_in = [sem(f"raw_gu_in{k}") for k in range(2)]
        raw_dn_in = [sem(f"raw_dn_in{k}") for k in range(2)]
        block = ctx.enter_context(nc.Block())

        lat = [(0, 0), (1, 1), (1, 2)]
        misc = (["ckvT"] + [f"z{k}" for k in range(4)] + ["cqT0", "cqT1"]
                + [f"kv{t}{n}" for t in range(4) for n in range(2)] + [f"qm{t}" for t in range(NT)]
                + [f"keyT{h}" for h in range(MH)] + [f"qryT{h}" for h in range(MH)]
                + ["A00", "A01", "kendT0", "kendT1", "U0", "U1", "p0T", "o0"] + [f"p1T{h}" for h in range(MH)]
                + ["A10", "A11", "pv0", "pv1", "o1"] + [f"p2T{h}" for h in range(MH)] + ["A20", "A21", "pv2", "o2"]
                + ["mT00", "mT01", "wo00", "wo01", "mT10", "mT11", "wo10", "wo11", "mT20", "mT21", "wo20", "wo21"]
                + ["sg0", "sg1", "pos", "cnt", "start", "sg2", "tabP", "tabG", "tabO", "tabJ"]
                + [f"{n}" for t in range(NT) for n in (f"sa{t}", f"sd{t}0", f"sd{t}1")])
        misc_no = {n: k for k, n in enumerate(misc)}
        proj = (["lr"] + [f"mla{t}" for t in range(NT)] + [f"qk{k}" for k in range(4)] + [f"v{t}" for t in range(NT)]
                + [f"g{t}" for t in range(NT)] + ["s0"] + [f"s{t}{h}" for t in (1, 2) for h in range(MH)]
                + [f"b{v}{s}{n}" for v in range(3) for s in range(2) for n in range(2)]
                + ["h00", "h01", "r0", "h10", "h11", "r1", "h20", "h21", "r2"])
        proj_no = {n: k for k, n in enumerate(proj)}
        NADA = 16

        def mbank(n, w=512):
            return ps[:, 5 + misc_no[n] % 3, 0:w]

        def pbank(n, w=512):
            return ps[:, proj_no[n] % 4, 0:w]

        combos = [(0, 0), (1, 0), (0, 1), (1, 2)]

        @block.sync
        def _(sp):
            def load(dst, src, s, n=16):
                sp.dma_start(dst, src).then_inc(S[s], n)

            load(keep[:], A["c_keep"], "consts_in")
            load(x_sb[:, 0, :], A["x_prompt"][0], "x_in")
            load(x_sb[:, 1:3, :], A["x_sample"][0].rearrange("(t p) d -> p t d", p=P), "x_in")
            load(cols[:, 0:44], A["c_cols"], "cols_in")
            w_ada = rows_pc(A["w_ada"][0], 6 * D)
            for c in range(4):
                sp.dma_start(ada1[:, c, :], w_ada[:, c, 0:2 * D]).then_inc(ada1_in[c], 16)
            load(tconst[:], A["c_trunk"], "consts_in")
            load(rows[:], A["c_rows"].partition_broadcast(P), "consts_in")
            load(wgk[:], A["c_wgk"], "consts_in")
            w_in = rows_pc(A["w_in"][0], 1984)
            for c in range(4, NC):
                sp.wait_ge(S["ada1_used"], c - 3)
                sp.dma_start(ada1[:, c - 4, :], w_ada[:, c, 0:2 * D]).then_inc(ada1_in[c - 4], 16)
            load(w_mla[:], w_in[:, :, 1536:1984], "w_mla_in")
            load(w_qk[:], w_in[:, :, 0:512], "w_qk_in")
            load(krope[:, 3, :], A["cache_mla_krope"][0, 0], "cache_in")
            load(ckvn[:, 3, :], A["cache_mla_ckv"][0, 0], "cache_in")
            load(w_v[:], w_in[:, :, 512:1024], "w_v_in")
            load(w_g[:], w_in[:, :, 1024:1536], "w_g_in")
            sp.wait_ge(S["ada1_used"], NC)
            load(w_uq[:], A["w_uq"][0].rearrange("(p c) n -> p c n", c=2), "w_u_in")
            load(w_ukv[:], A["w_ukv"][0], "w_u_in")
            load(modrow[:], A["b_ada"][0:1, 2 * D:].partition_broadcast(2), "brow_in")
            for k in range(NADA):
                if k:
                    sp.wait_ge(S["ada2_done"], k)
                load(ada2[:], w_ada[:, :, 2 * D + k * 256:2 * D + (k + 1) * 256], "ada2_in")
                if k == 1:
                    sp.wait_ge(S["misc_done"], misc_no["z0"])
                    load(state0[:, 0], A["state_gla_fwd"][0, 0].rearrange("(b h) k v -> (h k) b v", h=2), "state_in")
                    load(state0[:, 1], A["state_gla_bwd"][0, 0].rearrange("(b h) k v -> (h k) b v", h=2), "state_in")
                if k == 9:
                    sp.wait_ge(S["proj_done"], proj_no["g2"] + 1)
                    load(w_out[:], rows_pc(A["w_out"][0], D), "w_out_in")
            sp.wait_ge(S["ckv_ready"], 1)
            sp.dma_start(O["new_ckv"][0, 0], ckvn[:, 0, :]).then_inc(S["out_done"], 16)
            sp.dma_start(O["new_krope"][0, 0], mla[:, 0, QL + KL:]).then_inc(S["out_done"], 16)
            sp.wait_ge(S["misc_sb"], misc_no["U1"] + 1)
            for d, name in ((0, "new_fwd"), (1, "new_bwd")):
                sp.dma_start(O[name][0, 0].rearrange("(b h) k v -> (h k) b v", h=2), state1[:, d]).then_inc(S["out_done"], 16)
            sp.wait_ge(S["misc_done"], misc_no["o2"] + 1)
            sp.wait_ge(S["mix_done"], NT)
            sp.dma_start(g2row[:], A["g_norm2"][0:1].partition_broadcast(P)).then_inc(S["g2_in"], 16)
            sp.dma_start(x1[:, 0, :], A["x_prompt"][0]).then_inc(S["x1_in"], 16)
            sp.dma_start(x1[:, 1:3, :], A["x_sample"][0].rearrange("(t p) d -> p t d", p=P)).then_inc(S["x1_in"], 16)
            sp.dma_start(w_router[:], rows_pc(A["w_router"][0], NE)).then_inc(S["w_router_in"], 16)
            sp.wait_ge(S["ada2_sb"], NADA)
            sp.dma_start(gt2_dram, modrow[:, 3 * D:4 * D]).then_inc(S["gt2_out"], 16)

            def load_gu(slot, e):
                sp.dma_start(raw_gu[slot][:, 0], gate_of(e)).then_inc(raw_gu_in[slot], 16)
                sp.dma_start(raw_gu[slot][:, 1], up_of(e)).then_inc(raw_gu_in[slot], 16)

            def gate_of(e):
                return A["w_exp_gate"][0, e].rearrange("(p c) n -> p c n", c=NC)

            def up_of(e):
                return A["w_exp_up"][0, e].rearrange("(p c) n -> p c n", c=NC)

            def load_dn(slot, e):
                sp.dma_start(raw_dn[slot][:], A["w_exp_down"][0, e].rearrange("(p c) n -> p c n", c=2)).then_inc(raw_dn_in[slot], 16)

            load_gu(0, 0)
            sp.wait_ge(S["gt2_out"], 16)
            sp.wait_ge(S["proj_sb"], proj_no["b211"] + 1)
            sp.dma_start(w_shgu[:, 0], rows_pc(A["w_sh_gate"][0], DE)).then_inc(S["shgu_in"], 16)
            sp.dma_start(w_shgu[:, 1], rows_pc(A["w_sh_up"][0], DE)).then_inc(S["shgu_in"], 16)
            sp.dma_start(w_shd[:], A["w_sh_down"][0].rearrange("(p c) n -> p c n", c=2)).then_inc(S["shd_in"], 16)
            for t in range(NT):
                sp.wait_ge(S["x1_ready"], t + 1)
                sp.dma_start(x1_dram[:, t], x1[:, t]).then_inc(S["x1_out"], 16)
            sp.wait_ge(S["misc_done"], misc_no["sg2"] + 1)
            load_dn(0, 0)
            sp.wait_ge(S["jobs_ready"], 1)
            load_gu(1, 1)

            def group_loads(g, expert):
                for kind, j in SPLITS:
                    if kind == "gu":
                        sp.wait_ge(S["lo_gu_dve"], 2 * JG * g + 2 * j)
                        sp.wait_ge(S["lo_gu_pool"], 2 * JG * g + 2 * j)
                        load_gu(j % 2, expert(j))
                    else:
                        sp.wait_ge(S["lo_d4"], JG * g + j + 1)
                        sp.wait_ge(S["lo_d5"], JG * g + j + 1)
                        load_dn(j % 2, expert(j))

            n_rounds = sp.value_load(jobs[0:1, NJP:NJP + 1], min_val=NE // (2 * JG), max_val=NJ // (2 * JG))
            with sp.Fori(0, n_rounds) as r:
                for half in range(2):
                    g = 2 * r + half
                    experts = [sp.value_load(jobs[0:1, bass.ds(g * JG + j, 1)], min_val=0, max_val=NE - 1) for j in range(1, JG + 2)]
                    group_loads(g, lambda j: experts[j - 1])
            sp.wait_ge(S["gather_done"], NC * (2 * n_rounds + 1))
            sp.wait_ge(S["x1_out"], 16 * NT)
            sp.dma_start(x1b[:], x1_dram).then_inc(S["tail_in"], 16)
            for s in range(2):
                sp.dma_start(gt2[:, s], gt2_dram[s:s + 1].partition_broadcast(P)).then_inc(S["tail_in"], 16)
            for t in range(NT):
                sp.wait_ge(S["y_ready"], t + 1)
                dst = O["y_prompt"][0] if t == 0 else O["y_sample"][0, (t - 1) * P:t * P]
                sp.dma_start(dst, x1b[:, t]).then_inc(S["y_out"], 16)
            sp.wait_ge(S["y_out"], 16 * NT)
            sp.wait_ge(S["out_done"], 64)

        @block.tensor
        def _(pe):
            def mm(out, l, r, first, last):
                return nc.tensor.matmul(out, l, r, start=first, stop=last)

            def open_misc(n):
                k = misc_no[n]
                if k >= 3:
                    pe.wait_ge(S["misc_sb"], k - 2)
                return mbank(n)

            def open_proj(n):
                k = proj_no[n]
                if k >= 4:
                    pe.wait_ge(S["proj_sb"], k - 3)
                return pbank(n)

            ada_next = [0]

            def ada(n=1):
                for _ in range(n):
                    k = ada_next[0]
                    if k >= NADA:
                        return
                    pe.wait_ge(S["ada2_in"], 16 * (k + 1))
                    if k:
                        pe.wait_ge(S["ada2_sb"], k)
                    for c in range(NC):
                        last = mm(ps[0:2, 4, 0:256], silu_c[:, c, :], ada2[:, c, :], c == 0, c == NC - 1)
                    last.then_inc(S["ada2_done"], 1)
                    ada_next[0] += 1

            pe.wait_ge(S["silu_ready"], 1)
            for c in range(NC):
                if c == 4:
                    pe.wait_ge(S["consts_in"], 16)
                    pe.wait_ge(S["xn_ready"], 1)
                    for k in range(NC):
                        if k >= 4:
                            pe.wait_ge(S["xT_sb"], k - 3)
                        for t in range(NT):
                            last = nc.tensor.transpose(ps[:, 4 + k % 4, t * P:(t + 1) * P],
                                                       x_sb[:, t, k::NC], ident)
                        last.then_inc(S["xT_done"], 1)
                pe.wait_ge(ada1_in[c % 4], 16 * (c // 4 + 1))
                for n in range(4):
                    last = mm(ps[0:2, n, :], silu_c[:, c, :], ada1[:, c % 4, n * 512:(n + 1) * 512], c == 0, c == NC - 1)
                last.then_inc(S["ada1_used"], 1)
            pe.wait_ge(S["mod1_sb"], 1)
            pe.wait_ge(S["xT_sb"], NC)
            for j in range(2):
                for c in range(NC):
                    o = (j * NC + c) * 2
                    last = nc.tensor.transpose(ps[:, 4, o:o + 2], mod1[0:2, j * D + c:(j + 1) * D:NC], ident[0:2, 0:2])
            last.then_inc(S["modT_done"], 1)

            pe.wait_ge(S["h_ready"], 1)
            pe.wait_ge(S["w_mla_in"], 16)
            o = open_proj("lr")
            for c in range(NC):
                last = mm(o[0:32, 0:TOK], w_mla[:, c, 0:32], hT[:, c, :], c == 0, c == NC - 1)
            last.then_inc(S["proj_done"], 1)

            def token_rows(n, t, w):
                o = open_proj(n)[:, 0:w.shape[2]]
                for c in range(NC):
                    last = mm(o, hT[:, c, t * P:(t + 1) * P], w[:, c, :], c == 0, c == NC - 1)
                last.then_inc(S["proj_done"], 1)

            for t in range(NT):
                token_rows(f"mla{t}", t, w_mla[:, :, 32:448])
            pe.wait_ge(S["w_qk_in"], 16)
            for k in range(4):
                o = open_proj(f"qk{k}")[:, 0:TOK]
                for c in range(NC):
                    last = mm(o, w_qk[:, c, k * P:(k + 1) * P], hT[:, c, :], c == 0, c == NC - 1)
                last.then_inc(S["proj_done"], 1)
            pe.wait_ge(S["ckv_ready"], 1)
            pe.wait_ge(S["cache_in"], 32)
            o = open_misc("ckvT")
            for t in range(4):
                last = nc.tensor.transpose(o[:, t * P:(t + 1) * P], ckvn[:, t, :], ident)
            last.then_inc(S["misc_done"], 1)
            pe.wait_ge(S["proj_sb"], 1)
            pe.wait_ge(S["consts_in"], 64)
            for k in range(4):
                o = open_misc(f"z{k}")
                mm(o[:, 0:TOK], wgk[:, k // 2, k % 2, :], lrT[:], True, True).then_inc(S["misc_done"], 1)
            pe.wait_ge(S["cqn_ready"], 1)
            for c in range(2):
                o = open_misc(f"cqT{c}")
                for t in range(NT):
                    last = nc.tensor.transpose(o[:, t * P:(t + 1) * P], mla[:, t, c:QL:2], ident)
                last.then_inc(S["misc_done"], 1)
            pe.wait_ge(S["w_v_in"], 16)
            token_rows("v0", 0, w_v)
            pe.wait_ge(S["w_u_in"], 32)
            pe.wait_ge(S["misc_sb"], misc_no["ckvT"] + 1)
            for t in range(4):
                for n in range(2):
                    o = open_misc(f"kv{t}{n}")
                    mm(o[:, 0:384], ckvnT[:, t * P:(t + 1) * P], w_ukv[:, n * 384:(n + 1) * 384], True, True)\
                        .then_inc(S["misc_done"], 1)
            pe.wait_ge(S["misc_sb"], misc_no["cqT1"] + 1)
            for t in range(NT):
                o = open_misc(f"qm{t}")
                for c in range(2):
                    last = mm(o[:, 0:MH * QK], cqT[:, c, t * P:(t + 1) * P], w_uq[:, c, :], c == 0, c == 1)
                last.then_inc(S["misc_done"], 1)
            pe.wait_ge(S["brow_in"], 16)
            for t in (1, 2):
                token_rows(f"v{t}", t, w_v)
                ada()
            pe.wait_ge(S["w_g_in"], 16)
            for t in range(NT):
                token_rows(f"g{t}", t, w_g)
                ada()
            pe.wait_ge(S["key_ready"], 1)
            for h in range(MH):
                o = open_misc(f"keyT{h}")
                for t in range(4):
                    last = nc.tensor.transpose(o[0:QK, t * P:(t + 1) * P], key[:, t, h, :], ident)
                last.then_inc(S["misc_done"], 1)
            pe.wait_ge(S["qry_ready"], 1)
            for h in range(MH):
                o = open_misc(f"qryT{h}")
                for t in range(NT):
                    last = nc.tensor.transpose(o[0:QK, t * P:(t + 1) * P], qry[:, t, h, :], ident)
                last.then_inc(S["misc_done"], 1)

            pe.wait_ge(S["misc_sb"], misc_no["qryT3"] + 1)
            o = open_proj("s0")
            for h in range(MH):
                last = mm(o[:, h * P:(h + 1) * P], qryT[:, h, 0:P], keyT[:, h, 0:P], True, True)
            last.then_inc(S["proj_done"], 1)

            def scores(t):
                for h in range(MH):
                    o = open_proj(f"s{t}{h}")
                    mm(o[:, 0:TOK], qryT[:, h, t * P:(t + 1) * P], keyT[:, h, P:], True, True).then_inc(S["proj_done"], 1)

            def gla_scores(t):
                for par in range(2):
                    o = open_misc(f"A{t}{par}")
                    r = slice(par * GDK, (par + 1) * GDK)
                    for hh in range(2):
                        for d in range(2):
                            last = mm(o[:, (hh * 2 + d) * P:(hh * 2 + d + 1) * P],
                                      decay_m[r, d * 2 + hh, t * P:(t + 1) * P],
                                      decay_p[r, d * 2 + hh, t * P:(t + 1) * P], True, True)
                    last.then_inc(S["misc_done"], 1)

            def gla_out(t):
                pe.wait_ge(S["misc_sb"], misc_no[f"A{t}1"] + 1)
                if t:
                    pe.wait_ge(S["smp_ready"], t)
                o = open_misc(f"o{t}")
                for h in range(GH):
                    oh = o[:, h * GDV:(h + 1) * GDV]
                    for d in range(2):
                        last = mm(oh, attn[:, h % 2, h // 2, d, :], v_sb[:, t, h * GDV:(h + 1) * GDV], d == 0, not t and d == 1)
                    if t:
                        for d in range(2):
                            last = mm(oh, decay_p[:, d * 2 + h // 2, t * P:(t + 1) * P], stateP[:, t - 1, d, h, :], False, d == 1)
                last.then_inc(S["misc_done"], 1)

            def prob_t(t):
                for h in range(MH):
                    o = open_misc(f"p{t}T{h}")
                    pe.wait_ge(S["prob_ready"], 4 + (t - 1) * MH + h + 1)
                    for k in range(NT):
                        last = nc.tensor.transpose(o[:, k * P:(k + 1) * P], prob[:, h, k * P:(k + 1) * P], ident)
                    last.then_inc(S["misc_done"], 1)

            def prob_v(t):
                pe.wait_ge(S["misc_sb"], misc_no[f"p{t}T3"] + 1)
                o = open_misc(f"pv{t}")
                for h in range(MH):
                    for k in range(NT):
                        last = mm(o[:, h * VD:(h + 1) * VD], probT[:, h, k, :], val[:, 1 + k, h, :], k == 0, k == NT - 1)
                last.then_inc(S["misc_done"], 1)

            scores(1)
            pe.wait_ge(S["qe_ready"], 1)
            gla_scores(0)
            ada()
            pe.wait_ge(S["kend_ready"], 1)
            for n in range(2):
                o = open_misc(f"kendT{n}")
                for m in range(4):
                    last = nc.tensor.transpose(o[:, m * P:(m + 1) * P], kend[:, 2 * n + m // 2, m % 2, :], ident)
                last.then_inc(S["misc_done"], 1)
            ada()
            pe.wait_ge(S["misc_sb"], misc_no["kendT1"] + 1)
            pe.wait_ge(S["proj_sb"], proj_no["v2"] + 1)
            for n in range(2):
                o = open_misc(f"U{n}")
                for m in range(2):
                    k = 2 * n + m
                    for h in range(GH):
                        r = h % 2 * GDK
                        last = mm(o[r:r + GDK, (m * 2 + h // 2) * GDV:(m * 2 + h // 2 + 1) * GDV],
                                  kendT[:, k, h // 2, r:r + GDK], v_sb[:, combos[k][1], h * GDV:(h + 1) * GDV], True, True)
                last.then_inc(S["misc_done"], 1)
            pe.wait_ge(S["prob_ready"], 4)
            o = open_misc("p0T")
            for h in range(MH):
                last = nc.tensor.transpose(o[:, h * P:(h + 1) * P], prob0[:, h, :], ident)
            last.then_inc(S["misc_done"], 1)
            ada()
            gla_out(0)
            prob_t(1)
            ada()
            gla_scores(1)
            pe.wait_ge(S["misc_sb"], misc_no["p0T"] + 1)
            o = open_misc("pv0")
            for h in range(MH):
                last = mm(o[:, h * VD:(h + 1) * VD], prob0T[:, h, :], val[:, 0, h, :], True, True)
            last.then_inc(S["misc_done"], 1)
            prob_v(1)
            scores(2)
            gla_out(1)
            ada(2)
            prob_t(2)
            gla_scores(2)
            ada()
            prob_v(2)
            gla_out(2)
            ada(NADA)
            pe.wait_ge(S["ada2_sb"], NADA)
            for v in range(3):
                for s in range(2):
                    for n in range(2):
                        o = open_proj(f"b{v}{s}{n}")
                        mm(o, tc("sel")[0:2, s * P:(s + 1) * P], modrow[:, v * D + n * 512:v * D + (n + 1) * 512], True, True)\
                            .then_inc(S["proj_done"], 1)

            def mixed_t(t):
                pe.wait_ge(S["mix_done"], t + 1)
                for n in range(2):
                    o = open_misc(f"mT{t}{n}")
                    for c in range(4):
                        last = nc.tensor.transpose(o[:, c * P:(c + 1) * P], mixed[:, t, 4 * n + c::NC], ident)
                    last.then_inc(S["misc_done"], 1)

            def out_proj(t):
                pe.wait_ge(S["misc_sb"], misc_no[f"mT{t}1"] + 1)
                for n in range(2):
                    o = open_misc(f"wo{t}{n}")
                    for c in range(NC):
                        last = mm(o, mixedT[:, c, t * P:(t + 1) * P], w_out[:, c, n * 512:(n + 1) * 512], c == 0, c == NC - 1)
                    last.then_inc(S["misc_done"], 1)

            def h2_t(t):
                pe.wait_ge(S["h2_ready"], t + 1)
                for n in range(2):
                    o = open_proj(f"h{t}{n}")
                    for c in range(4):
                        last = nc.tensor.transpose(o[:, c * P:(c + 1) * P], h2[:, t, 4 * n + c::NC], ident)
                    last.then_inc(S["proj_done"], 1)

            def router(t):
                pe.wait_ge(S["w_router_in"], 16)
                pe.wait_ge(S["proj_sb"], proj_no[f"h{t}1"] + 1)
                o = open_proj(f"r{t}")[:, 0:NE]
                for c in range(NC):
                    last = mm(o, h2T[:, c, t * P:(t + 1) * P], w_router[:, c, :], c == 0, c == NC - 1)
                last.then_inc(S["proj_done"], 1)

            def shared_up(t):
                pe.wait_ge(S["shgu_in"], 32)
                o = open_misc(f"sg{t}")
                for c in range(NC):
                    last = mm(o, h2T[:, c, t * P:(t + 1) * P], w_shgu[:, :, c, :], c == 0, c == NC - 1)
                last.then_inc(S["misc_done"], 1)

            def shared_down(t):
                pe.wait_ge(S["shd_in"], 16)
                pe.wait_ge(S["sh_a_ready"], t + 1)
                o = open_misc(f"sa{t}")
                for f in range(2):
                    last = nc.tensor.transpose(o[:, f * P:(f + 1) * P], sh_a[t][:, f::2], ident)
                last.then_inc(S["misc_done"], 1)
                pe.wait_ge(S["misc_sb"], misc_no[f"sa{t}"] + 1)
                for n in range(2):
                    o = open_misc(f"sd{t}{n}")
                    for f in range(2):
                        last = mm(o, sh_aT[:, f, :], w_shd[:, f, n * 512:(n + 1) * 512], f == 0, f == 1)
                    last.then_inc(S["misc_done"], 1)

            pe.wait_ge(S["w_out_in"], 16)
            mixed_t(0)
            out_proj(0)
            mixed_t(1)
            out_proj(1)
            mixed_t(2)
            h2_t(0)
            router(0)
            out_proj(2)
            h2_t(1)
            router(1)
            shared_up(0)
            h2_t(2)
            router(2)
            shared_up(1)
            pe.wait_ge(S["mask_ready"], 1)
            o = open_misc("pos")
            for t in range(NT):
                for b in range(t + 1):
                    last = mm(o[:, t * NE:(t + 1) * NE], strictb if b == t else onesb, maskb[:, b, :], b == 0, b == t)
            last.then_inc(S["misc_done"], 1)
            o = open_misc("cnt")
            for t in range(NT):
                last = mm(o[0:NE, 0:1], maskb[:, t, :], onesb[:, 0:1], t == 0, t == NT - 1)
            last.then_inc(S["misc_done"], 1)
            pe.wait_ge(S["cnt_sb"], 1)
            o = open_misc("start")
            mm(o[0:NE, 0:1], strict[0:NE, 0:NE], nov[0:NE], True, True).then_inc(S["misc_done"], 1)
            shared_up(2)
            for n, z in (("tabP", posp), ("tabG", weight)):
                o = open_misc(n)
                for t in range(NT):
                    last = nc.tensor.transpose(o[0:NE, t * P:(t + 1) * P], z[:, t, :], ident)
                last.then_inc(S["misc_done"], 1)
            pe.wait_ge(S["owner_ready"], 1)
            o = open_misc("tabO")
            mm(o[:, 0:NOVER], ones[0:NE], offs[0:NE], True, True)
            mm(o[:, NOVER:2 * NOVER], tc("index")[0:NE].to_broadcast([NE, P]), owner[0:NE], True, True)
            mm(o[:, 2 * NOVER:2 * NOVER + 1], ones[0:NE], nov[0:NE], True, True).then_inc(S["misc_done"], 1)
            pe.wait_ge(S["misc_sb"], misc_no["tabG"] + 1)
            o = open_misc("tabJ")
            for k, z in enumerate((poT, gaT)):
                for t in range(NT):
                    last = mm(o[:, (k * NT + t) * NOVER:(k * NT + t + 1) * NOVER], z[0:NE, t, :], owner[0:NE], True, True)
            last.then_inc(S["misc_done"], 1)

            def gather_chunk(g, c):
                pe.wait_ge(S["pick_ready"], g + 2)
                if c < 2:
                    pe.wait_ge(S["acc_done"], 6 * g + 11 + c)
                else:
                    pe.wait_ge(S["xs_act" if c % 2 == 0 else "xs_dve"], 4 * g + 4 + c // 2)
                for z, h in enumerate((h2h, h2l)):
                    for t in range(NT):
                        last = mm(ps[:, 6 + c % 2, z * 256:(z + 1) * 256], h[:, t, c, :], pick[:, t, :], t == 0, t == NT - 1)
                last.then_inc(S["gather_done"], 1)

            def gate_slots(g, col):
                pe.wait_ge(S["pickb_ready"], g + 2)
                pe.wait_ge(S["b5_sb"], 5 * g + 5)
                for j in range(JG):
                    for t in range(NT):
                        last = mm(ps[0:SLOT, 5, j * 4:j * 4 + 3], pickb[:, t, j, :], gparts[:, t, col + j, :] if isinstance(col, int)
                                  else gparts[:, t, bass.ds(col + j, 1), :].rearrange("p a b -> p (a b)"), t == 0, t == NT - 1)
                last.then_inc(S["place_mm"], 1)

            def place_slots(g, j):
                pe.wait_ge(S["b5_sb"], 5 * g + 1 + j)
                for t in range(NT):
                    for half in range(2):
                        last = mm(ps[half * SLOT:(half + 1) * SLOT, 5, t * P:(t + 1) * P], pickb[:, t, j, :], identb[:], True, True)
                last.then_inc(S["place_mm"], 1)

            def up(g, j, units):
                for u in units:
                    if u == 0:
                        pe.wait_ge(S["gu_sum"], JG * g + j + 1)
                    if j % JG == 0:
                        pe.wait_ge(S["xs_act"], JG * g + j + u + 1)
                        pe.wait_ge(S["xs_dve"], JG * g + j + u + 1)
                    pe.wait_ge(S["lo_gu_dve" if u % 2 == 0 else "lo_gu_pool"], 2 * JG * g + 2 * j + u // 2 + 3)
                    for cc in range(2):
                        c = 2 * u + cc
                        for w in (wh[u], wl[u]):
                            last = mm(ps[:, j % 2, :], xs[(half + j // JG) % 2][:, j % JG, c].rearrange("p a b -> p (a b)"),
                                      w[:].rearrange("p (m c n) -> p m c n", m=2, c=2)[:, :, cc, :],
                                      c == 0 and w is wh[u], c == NC - 1 and w is wl[u])
                    last.then_inc(S["gu_used"], 1)

            def turn(g, j):
                pe.wait_ge(S["a_ready"], JG * g + j + 2)
                pe.wait_ge(S["al_done"], JG * g + j + 1)
                for f in range(2):
                    last = mm(ps[:, 4, f * SLOT:(f + 1) * SLOT], act_a[j % 2][HI, f::2], ident[HI, SLOT:2 * SLOT], True, True)
                last.then_inc(S["aT_done"], 1)

            def down(g, j):
                pe.wait_ge(S["al_done"], JG * g + j + 2)
                for f in range(2):
                    pe.wait_ge(S["lo_d4" if f == 0 else "lo_d5"], JG * g + j + 3)
                    for n in range(2):
                        if f == 0:
                            pe.wait_ge(S["y_sum"], 2 * JG * g + 2 * j + n + 1)
                        for w in (wh[4 + f], wl[4 + f]):
                            last = mm(ps[:, 2 + n, :], ast[j % 2][:, f].rearrange("p a b -> p (a b)"), w[:, n * 512:(n + 1) * 512],
                                      f == 0 and w is wh[4], f == 1 and w is wl[5])
                    last.then_inc(S["dn_used"], 1)

            def scatter(g, ranges=range(6)):
                pe.wait_ge(S["yl_dve"], JG * g + 1)
                pe.wait_ge(S["yl_pool"], JG * g + 1)
                pe.wait_ge(S["b5_sb"], 5 * g + 1)
                for k in ranges:
                    if k < 2:
                        pe.wait_ge(S["xs_act" if k == 0 else "xs_dve"], 4 * g + 4)
                    else:
                        pe.wait_ge(S["acc_done"], 6 * g + 5 + k)
                    t, n = k // 2, k % 2
                    for j in range(JG):
                        last = mm(ps[:, 6 + k % 2, :], place[:, j, t * P:(t + 1) * P], ys[:, j, n * 512:(n + 1) * 512],
                                  j == 0, j == JG - 1)
                    last.then_inc(S["scatter_done"], 1)

            pe.wait_ge(S["misc_sb"], misc_no["tabJ"] + 1)
            pe.wait_ge(S["proj_sb"], len(proj))
            for t in range(NT):
                shared_down(t)
            pe.wait_ge(S["h2s_ready"], 1)
            pe.wait_ge(S["misc_sb"], len(misc))
            pe.sem_inc(S["gu_used"], 4)
            pe.sem_inc(S["dn_used"], 4)
            pe.sem_inc(S["aT_done"], 2)
            pe.wait_ge(S["pick_ready"], 1)
            pe.wait_ge(S["acc_done"], 6)
            for c in range(NC):
                if c >= 2:
                    pe.wait_ge(S["xs_act" if c % 2 == 0 else "xs_dve"], c // 2)
                for z, h in enumerate((h2h, h2l)):
                    for t in range(NT):
                        last = mm(ps[:, 6 + c % 2, z * 256:(z + 1) * 256], h[:, t, c, :], pick[:, t, :], t == 0, t == NT - 1)
                last.then_inc(S["gather_done"], 1)
            pe.wait_ge(S["pickb_ready"], 1)
            for j in range(JG):
                for t in range(NT):
                    last = mm(ps[0:SLOT, 5, j * 4:j * 4 + 3], pickb[:, t, j, :], gparts[:, t, j, :], t == 0, t == NT - 1)
            last.then_inc(S["place_mm"], 1)
            half = 0
            up(0, 0, range(4))
            turn(0, 0)
            pe.wait_ge(S["zeroed"], 3)
            n_rounds = pe.value_load(jobs[0:1, NJP:NJP + 1], min_val=NE // (2 * JG), max_val=NJ // (2 * JG))
            with pe.Fori(0, n_rounds) as r:
                for half in range(2):
                    g = 2 * r + half
                    up(g, 1, range(4))
                    scatter(g, range(2))
                    down(g, 0)
                    scatter(g, range(2, 6))
                    place_slots(g, 0)
                    turn(g, 1)
                    up(g, 2, range(4))
                    place_slots(g, 1)
                    gather_chunk(g, 0)
                    gather_chunk(g, 1)
                    down(g, 1)
                    gather_chunk(g, 2)
                    gather_chunk(g, 3)
                    place_slots(g, 2)
                    turn(g, 2)
                    up(g, 3, range(4))
                    place_slots(g, 3)
                    gather_chunk(g, 4)
                    gather_chunk(g, 5)
                    down(g, 2)
                    gather_chunk(g, 6)
                    gather_chunk(g, 7)
                    gate_slots(g, g * JG + JG)
                    turn(g, 3)
                    up(g, 4, range(4))
                    down(g, 3)
                    turn(g, 4)
            scatter(2 * n_rounds)

        @block.scalar
        def _(act):
            chain = [0]

            def own(i):
                chain[0] += 1
                i.then_inc(S["act_chain"], 1)
                act.wait_ge(S["act_chain"], chain[0])

            roots = [0]

            def root(v, t, r):
                roots[0] += 1
                act.wait_ge(S["rn_in"], roots[0])
                own(nc.scalar.activation(t, v, ACT.Ln))
                nc.scalar.activation(r, t, ACT.Exp, scale=-0.5).then_inc(S["rn_out"], 1)

            def take(n, out, w=512, rowsn=P, scale=None):
                act.wait_ge(S["proj_done"], proj_no[n] + 1)
                i = pbank(n, w)[0:rowsn]
                if scale is None:
                    nc.scalar.copy(out, i).then_inc(S["proj_sb"], 1)
                else:
                    nc.scalar.mul(out, i, scale).then_inc(S["proj_sb"], 1)

            act.wait_ge(S["cols_in"], 16)
            nc.scalar.activation(cexp, ccol, ACT.Exp, scale=-1.0).then_inc(S["silu_g"], 1)
            act.wait_ge(S["x_in"], 32)
            for t in range(NT):
                i = nc.scalar.activation(sq[:, 0:D], x_sb[:, t, :], ACT.Square, accum_out=ss1[:, t:t + 1])
                own(i)
            act.sem_inc(S["rn_ln"], 1)
            root(v1, t1, r1)
            for c in range(NC):
                act.wait_ge(S["xT_done"], c + 1)
                nc.scalar.copy(hT[:, c, :], ps[:, 4 + c % 4, 0:TOK]).then_inc(S["xT_sb"], 1)
            take("lr", lrT[:], TOK, 32)
            for t in range(NT):
                take(f"mla{t}", mla[:, t, :], QL + KL + ROPE)
            act.wait_ge(S["proj_sb"], 4)
            for t in range(NT):
                own(nc.scalar.activation(sq[:, 0:QL], mla[:, t, 0:QL], ACT.Square, accum_out=ss2[:, 0, t:t + 1]))
                own(nc.scalar.activation(sq[:, 0:KL], mla[:, t, QL:QL + KL], ACT.Square, accum_out=ss2[:, 1, t:t + 1]))
            act.sem_inc(S["rn_ln"], 1)
            root(v2, t2, r2)
            for k in range(4):
                take(f"qk{k}", qkT[:, k, :], TOK, P, GDK ** -0.5 if k < 2 else None)
            act.wait_ge(S["misc_sb"], misc_no["z3"] + 1)
            own(nc.scalar.activation(decay_p[:], decay_m[:], ACT.Abs))
            own(nc.scalar.activation(decay_p[:], decay_p[:], ACT.Exp, scale=-1.0))
            nc.scalar.activation(decay_p[:], decay_p[:], ACT.Ln, bias=1.0).then_inc(S["gate_l"], 1)
            take("v0", v_sb[:, 0, :])
            act.wait_ge(S["gate_d"], 1)
            nc.scalar.activation(gex, gsm, ACT.Exp, scale=1.0 / GATE_NORM).then_inc(S["decay_ready"], 1)
            nc.scalar.activation(decay_p[:], decay_m[:], ACT.Exp, scale=1.0 / GATE_NORM).then_inc(S["decay_ready"], 1)
            act.wait_ge(S["decay_ready"], 2)
            nc.scalar.activation(decay_m[:], decay_m[:], ACT.Exp, scale=-1.0 / GATE_NORM).then_inc(S["decay_ready"], 1)
            take("v1", v_sb[:, 1, :])
            root(vk, tk, rk)
            take("v2", v_sb[:, 2, :])
            root(vq, tq, rq)
            for t in range(NT):
                take(f"g{t}", g_sb[:, t, :])
            act.wait_ge(S["max_ready"], 1)
            for h in range(MH):
                i = nc.scalar.activation(prob0[:, h, :], pbank("s0")[:, h * P:(h + 1) * P], ACT.Exp,
                                         bias=nmax[:, 0, h:h + 1], accum_out=psum_p[:, 0, h:h + 1])
                i.then_inc(S["prob_ready"], 1)
            act.wait_ge(S["prob_ready"], MH)
            act.sem_inc(S["proj_sb"], 1)
            for t in (1, 2):
                if t == 2:
                    act.wait_ge(S["misc_done"], misc_no["p1T3"] + 1)
                for h in range(MH):
                    act.wait_ge(S["max_ready"], 1 + (t - 1) * MH + h + 1)
                    nc.scalar.activation(prob[:, h, :], pbank(f"s{t}{h}", TOK), ACT.Exp,
                                         bias=nmax[:, t, h:h + 1], accum_out=psum_p[:, t, h:h + 1])\
                        .then_inc(S["prob_ready"], 1)
                    act.wait_ge(S["prob_ready"], MH + (t - 1) * MH + h + 1)
                    act.sem_inc(S["proj_sb"], 1)
                if t == 1:
                    act.wait_ge(S["misc_done"], misc_no["qm2"] + 1)
                    nc.scalar.activation(gexp[:], g_sb[:], ACT.Exp, scale=-1.0).then_inc(S["silu_g"], 1)
            root(vo, to, ro)
            for v in range(3):
                for s in range(2):
                    for n in range(2):
                        act.wait_ge(S["proj_done"], proj_no[f"b{v}{s}{n}"] + 1)
                        dst = (gt1, add2, mul2)[v][:, s, n * 512:(n + 1) * 512]
                        nc.scalar.activation(dst, pbank(f"b{v}{s}{n}"), ACT.Identity, bias=1.0 if v == 2 else 0.0)\
                            .then_inc(S["proj_sb"], 1)

            def norm2(t):
                act.wait_ge(S["x1_ready"], t + 1)
                nc.scalar.activation(sq3[:], x1[:, t], ACT.Square, accum_out=ss3[:, t:t + 1]).then_inc(S["sq_done"], 1)
                act.wait_ge(S["sq_done"], t + 1)
                root(v3[:, t:t + 1], t3[:, t:t + 1], r3[:, t:t + 1])

            def h2_take(t):
                for n in range(2):
                    act.wait_ge(S["proj_done"], proj_no[f"h{t}{n}"] + 1)
                    nc.scalar.copy(h2T[:, 4 * n:4 * n + 4, t * P:(t + 1) * P],
                                   pbank(f"h{t}{n}").rearrange("p (c j) -> p c j", c=4)).then_inc(S["proj_sb"], 1)

            def scores_take(t):
                act.wait_ge(S["proj_done"], proj_no[f"r{t}"] + 1)
                nc.scalar.activation(score[:, t, :], pbank(f"r{t}", NE), ACT.Sigmoid).then_inc(S["score_ready"], 1)
                act.wait_ge(S["score_ready"], t + 1)
                act.sem_inc(S["proj_sb"], 1)

            norm2(0)
            norm2(1)
            h2_take(0)
            act.wait_ge(S["misc_done"], misc_no["wo21"] + 1)
            norm2(2)
            scores_take(0)
            h2_take(1)
            scores_take(1)
            h2_take(2)
            scores_take(2)
            act.wait_ge(S["misc_done"], misc_no["wo21"] + 1)
            for t in range(NT):
                nc.scalar.copy(h2h[:, t], h2[:, t].rearrange("p (j c) -> p c j", c=NC)).then_inc(S["h2h_ready"], 1)
            for t in range(NT):
                if t:
                    act.wait_ge(S["sh_a_ready"], t)
                act.wait_ge(S["misc_done"], misc_no[f"sg{t}"] + 1)
                nc.scalar.activation(sh_sil[:], mbank(f"sg{t}")[:, 0:DE], ACT.Silu).then_inc(S["sh_sil_ready"], 1)

            def high_gu(g, j, u):
                if u == 0:
                    act.wait_ge(raw_gu_in[j % 2], 32 * (2 * g + j // 2 + 1))
                act.wait_ge(S["gu_used"], 4 * (JG * g + j) + u + 1)
                nc.scalar.copy(wh[u][:].rearrange("p (m c) -> p m c", m=2),
                               raw_gu[j % 2][:, :, 2 * u:2 * u + 2, :].rearrange("p m c n -> p m (c n)"))\
                    .then_inc(S["hi_gu"], 1)

            def high_dn(g, j):
                act.wait_ge(raw_dn_in[j % 2], 16 * (2 * g + j // 2 + 1))
                act.wait_ge(S["dn_used"], 2 * (JG * g + j) + 3)
                nc.scalar.copy(wh[4][:], raw_dn[j % 2][:, 0]).then_inc(S["hi_d4"], 1)

            def other_half(g, j):
                act.wait_ge(S["gu_used"], 4 * (JG * g + j) + 8)
                act.wait_ge(S["a_ready"], JG * g + j + 1)
                nc.scalar.copy(gu, ps[0:SLOT, j % 2, :]).then_inc(S["half_up"], 1)

            def silu(g, j):
                act.wait_ge(S["gu_sum"], JG * g + j + 3)
                nc.scalar.activation(sil, gu[:, 0:DE], ACT.Silu).then_inc(S["silu_done"], 1)

            def high_a(g, j):
                act.wait_ge(S["aT_done"], JG * g + j + 3)
                act.wait_ge(S["dn_used"], 2 * (JG * g + j) + 2)
                nc.scalar.copy(ast[j % 2][:, :, 0, :], ps[:, 4, 0:2 * SLOT].rearrange("p (f s) -> p f s", f=2))\
                    .then_inc(S["ah_done"], 1)

            def other_y(g, j):
                act.wait_ge(S["dn_used"], 2 * (JG * g + j) + 6)
                act.wait_ge(S["yl_dve"], JG * g + j + 1)
                act.wait_ge(S["yl_pool"], JG * g + j + 1)
                for n in range(2):
                    nc.scalar.copy(yt[:, n * 512:(n + 1) * 512], ps[HI, 2 + n, :]).then_inc(S["y_half"], 1)

            def high_y(g, j):
                act.wait_ge(S["y_sum"], 2 * (JG * g + j) + 4)
                if j == 0:
                    act.wait_ge(S["scatter_done"], 6 * g + 6)
                nc.scalar.copy(ys[0:SLOT, j % JG, :], yt).then_inc(S["yh_done"], 1)

            def place_take(g, j):
                act.wait_ge(S["place_mm"], 5 * g + 2 + j)
                act.wait_ge(S["scatter_done"], 6 * g + 6)
                nc.scalar.copy(place[:, j, :], ps[:, 5, 0:TOK]).then_inc(S["b5_sb"], 1)

            def tokens(g, c):
                act.wait_ge(S["gather_done"], NC * (g + 1) + c + 1)
                nc.scalar.copy(xs[(half + 1) % 2][:, :, c], ps[:, 6, :].rearrange("p (z j s) -> p j z s", z=2, j=JG)).then_inc(S["xs_act"], 1)

            act.wait_ge(S["shared_done"], 1)
            for u in range(4):
                high_gu(0, 0, u)
            for c in range(0, NC, 2):
                act.wait_ge(S["gather_done"], c + 1)
                nc.scalar.copy(xs[0][:, :, c], ps[:, 6, :].rearrange("p (z j s) -> p j z s", z=2, j=JG)).then_inc(S["xs_act"], 1)
            for u in range(3):
                high_gu(0, 1, u)
            other_half(0, 0)
            high_gu(0, 1, 3)
            silu(0, 0)
            high_dn(0, 0)
            act.wait_ge(S["zeroed"], 3)
            n_rounds = act.value_load(jobs[0:1, NJP:NJP + 1], min_val=NE // (2 * JG), max_val=NJ // (2 * JG))
            with act.Fori(0, n_rounds) as r:
                for half in range(2):
                    g = 2 * r + half
                    for j in range(1, JG + 1):
                        high_a(g, j - 1)
                        high_gu(g, j + 1, 0)
                        high_y(g, j - 2)
                        high_gu(g, j + 1, 1)
                        high_gu(g, j + 1, 2)
                        other_half(g, j)
                        high_gu(g, j + 1, 3)
                        silu(g, j)
                        if j in (2, 3):
                            place_take(g, 2 * j - 3)
                        if j in (2, 3):
                            tokens(g, 4 * j - 8)
                        high_dn(g, j)
                        if j in (2, 3):
                            tokens(g, 4 * j - 6)
                        other_y(g, j - 1)
                        if j in (1, 2):
                            place_take(g, 2 * j - 2)
            high_y(2 * n_rounds, -1)

        @block.vector
        def _(dve):
            V = nc.vector
            chain = [0]

            def own(i):
                chain[0] += 1
                i.then_inc(S["dve_chain"], 1)
                dve.wait_ge(S["dve_chain"], chain[0])

            roots = [0]

            def root(v, t, r, last=None):
                roots[0] += 1
                dve.wait_ge(S["rn_out"], roots[0])
                own(V.tensor_tensor(t, r, r, ALU.mult))
                own(V.tensor_tensor(t, t, v, ALU.mult))
                own(V.tensor_scalar(t, t, -0.5, 1.5, ALU.mult, ALU.add))
                own(V.tensor_tensor(r, r, t, ALU.mult))

            def take(n):
                dve.wait_ge(S["misc_done"], misc_no[n] + 1)
                return mbank(n)

            def freed(i):
                i.then_inc(S["misc_sb"], 1)

            ada_next = [0]

            def ada(n=1):
                for _ in range(n):
                    k = ada_next[0]
                    if k >= NADA:
                        return
                    dve.wait_ge(S["ada2_done"], k + 1)
                    m = modrow[:, k * 256:(k + 1) * 256]
                    V.tensor_tensor(m, m, ps[0:2, 4, 0:256], ALU.add).then_inc(S["ada2_sb"], 1)
                    ada_next[0] += 1

            dve.wait_ge(S["silu_g"], 1)
            own(V.tensor_scalar(cexp, cexp, 1.0, None, ALU.add))
            own(V.reciprocal(cexp, cexp))
            V.tensor_tensor(silu_c.rearrange("p c s -> p s c"), cexp, ccol, ALU.mult).then_inc(S["silu_ready"], 1)
            dve.wait_ge(S["rn_ln"], 1)
            V.tensor_scalar(v1, ss1, 1.0 / D, EPS, ALU.mult, ALU.add).then_inc(S["rn_in"], 1)
            root(v1, t1, r1)
            for t in range(NT):
                last = V.tensor_scalar(x_sb[:, t, :], x_sb[:, t, :], r1[:, t:t + 1], None, ALU.mult)
            last.then_inc(S["xn_ready"], 1)
            dve.wait_ge(S["ada1_used"], NC)
            V.tensor_copy(mod1[:].rearrange("p (n m) -> p n m", m=512), ps[0:2, 0:4, :]).then_inc(S["mod1_sb"], 1)
            dve.wait_ge(S["modT_done"], 1)
            own(V.tensor_tensor(modc, ps[:, 4, 0:4 * NC].rearrange("p (c s) -> p c s", s=2),
                                cols[:, 24:40].unsqueeze(2).to_broadcast([P, 2 * NC, 2]), ALU.add))
            own(V.scalar_tensor_tensor(scale1, modc[:, NC:, :], 1.0, g1col.unsqueeze(2).to_broadcast([P, NC, 2]),
                                       ALU.add, ALU.mult))
            dve.wait_ge(S["xT_sb"], NC)
            for c in range(NC):
                for s, a, b in ((0, 0, P), (1, P, TOK)):
                    last = V.tensor_scalar(hT[:, c, a:b], hT[:, c, a:b], scale1[:, c, s:s + 1], modc[:, c, s:s + 1],
                                           ALU.mult, ALU.add)
            last.then_inc(S["h_ready"], 1)

            dve.wait_ge(S["rn_ln"], 2)
            own(V.tensor_scalar(v2[:, 0, :], ss2[:, 0, :], 1.0 / QL, EPS, ALU.mult, ALU.add))
            V.tensor_scalar(v2[:, 1, :], ss2[:, 1, :], 1.0 / KL, EPS, ALU.mult, ALU.add).then_inc(S["rn_in"], 1)
            dve.wait_ge(S["rn_in"], 2)
            root(v2, t2, r2)
            dve.wait_ge(S["consts_in"], 64)
            for t in range(NT):
                last = V.scalar_tensor_tensor(ckvn[:, t, :], mla[:, t, QL:QL + KL], r2[:, 1, t:t + 1], row("g_kv_lora"),
                                              ALU.mult, ALU.mult)
            last.then_inc(S["ckv_ready"], 1)
            for t in range(NT):
                last = V.scalar_tensor_tensor(mla[:, t, 0:QL], mla[:, t, 0:QL], r2[:, 0, t:t + 1], row("g_q_lora"),
                                              ALU.mult, ALU.mult)
            last.then_inc(S["cqn_ready"], 1)
            i = take("ckvT")
            freed(V.tensor_copy(ckvnT[:], i))
            dve.wait_ge(S["proj_done"], proj_no["qk3"] + 1)
            for k in range(4):
                i = take(f"z{k}")
                freed(V.tensor_scalar(decay_m[:, k, :], i[:, 0:TOK], gkcol[:, k:k + 1], None, ALU.add))
            for c in range(2):
                i = take(f"cqT{c}")
                freed(V.tensor_copy(cqT[:, c, :], i[:, 0:TOK]))
            own(V.tensor_scalar(gqs[:], row("g_qk_q"), QK ** -0.5, None, ALU.mult))
            dve.wait_ge(S["gate_l"], 1)
            own(V.scalar_tensor_tensor(decay_m[:], decay_m[:], 0.0, decay_p[:], ALU.min, ALU.subtract))
            for k in range(4):
                for t in range(NT):
                    last = V.tensor_tensor_scan(decay_p[:, k, t * P:(t + 1) * P], ones, decay_m[:, k, t * P:(t + 1) * P],
                                                0.0, ALU.mult, ALU.add)
            own(last)
            seg_p = decay_p[:].rearrange("p k (t j) -> p (k t) j", j=P)
            seg_m = decay_m[:].rearrange("p k (t j) -> p (k t) j", j=P)
            tot = gtot.rearrange("p b t -> p (b t)")
            V.tensor_copy(gsm[:, 2, :].unsqueeze(2), seg_p[:, :, P - 1:P]).then_inc(S["gate_e"], 1)
            dve.wait_ge(S["gate_e"], 1)
            own(V.tensor_tensor(seg_p[:, 6:12, :], seg_m[:, 6:12, :], seg_p[:, 6:12, :], ALU.subtract))
            mid = P // 2 - 1
            V.tensor_copy(gsm[:, 0, 0:6].unsqueeze(2), seg_p[:, 0:6, mid:mid + 1])
            V.tensor_tensor(gsm[:, 0, 6:12].unsqueeze(2), seg_p[:, 6:12, mid:mid + 1], gsm[:, 2, 6:12].unsqueeze(2), ALU.add)
            V.tensor_tensor(gsm[:, 1, 0:6].unsqueeze(2), seg_p[:, 0:6, P - 1:P], seg_p[:, 0:6, mid:mid + 1], ALU.subtract)
            V.tensor_scalar(gsm[:, 1, 6:12].unsqueeze(2), seg_p[:, 6:12, mid:mid + 1], -1.0, None, ALU.mult)
            V.tensor_tensor(seg_m, seg_p, seg_p[:, :, mid:mid + 1].to_broadcast([P, 12, P]), ALU.subtract)\
                .then_inc(S["gate_d"], 1)
            for t in range(4):
                for n in range(2):
                    i = take(f"kv{t}{n}")[:, 0:384].rearrange("p (h w) -> p h w", w=NOPE + VD)
                    V.tensor_copy(key[:, t, 2 * n:2 * n + 2, 0:NOPE], i[:, :, 0:NOPE])
                    freed(V.tensor_copy(val[:, t, 2 * n:2 * n + 2, :], i[:, :, NOPE:]))
            for t in range(NT):
                i = take(f"qm{t}")
                freed(V.tensor_copy(qry[:, t].rearrange("p h w -> p (h w)"), i[:, 0:MH * QK]))
            dve.wait_ge(S["decay_ready"], 3)
            dve.wait_ge(S["proj_sb"], proj_no["qk3"] + 1)
            for d in range(2):
                V.tensor_tensor(decay_p[:, 2 * d:2 * d + 2, :], decay_p[:, 2 * d:2 * d + 2, :], qkT[:, 0:2, :], ALU.mult)
                last = V.tensor_tensor(decay_m[:, 2 * d:2 * d + 2, :], decay_m[:, 2 * d:2 * d + 2, :], qkT[:, 2:4, :], ALU.mult)
            last.then_inc(S["qe_ready"], 1)
            ada(1)

            def qk_norm(z, n, ss, v, t, r, gain, first):
                w = z[:].rearrange("p t h w -> p (t h) w")
                q = sq2[:, 0:n * MH * QK].rearrange("p (a w) -> p a w", w=QK)
                own(V.tensor_tensor(q, w, w, ALU.mult))
                own(V.tensor_reduce(ss.rearrange("p t h -> p (t h)"), q, AX.X, ALU.add))
                V.tensor_scalar(v, ss, 1.0 / QK, EPS, ALU.mult, ALU.add).then_inc(S["rn_in"], 1)
                root(v, t, r)
                own(V.tensor_tensor(w, w, r.rearrange("p t h -> p (t h)").unsqueeze(2).to_broadcast([P, n * MH, QK]), ALU.mult))
                own(V.tensor_tensor(w, w, gain.unsqueeze(1).to_broadcast([P, n * MH, QK]), ALU.mult))
                for k in range(2):
                    rot = z[:, 1 + k, :, NOPE:]
                    c = tc("cos")[:, k * ROPE:(k + 1) * ROPE].unsqueeze(1).to_broadcast([P, MH, ROPE])
                    s = tc("sin")[:, k * ROPE:(k + 1) * ROPE].rearrange("p (a b i) -> p a b i", a=2, b=2)
                    a = sq2[:, 0:MH * ROPE].rearrange("p (h w) -> p h w", h=MH)
                    b = sq2[:, MH * ROPE:2 * MH * ROPE].rearrange("p (h w) -> p h w", h=MH)
                    b4 = b.rearrange("p h (a b i) -> p h a b i", a=2, b=2)
                    r4 = rot.rearrange("p h (a b i) -> p h a b i", a=2, b=2)
                    V.tensor_tensor(a, rot, c, ALU.mult)
                    for half in range(2):
                        last = V.tensor_tensor(b4[:, :, :, half, :], r4[:, :, :, 1 - half, :],
                                               s[:, :, half, :].unsqueeze(1).to_broadcast([P, MH, 2, ROPE // 4]), ALU.mult)
                    own(last)
                    own(V.tensor_tensor(rot, a, b, ALU.add))

            dve.wait_ge(S["krope_ready"], 1)
            qk_norm(key, 4, ssk, vk, tk, rk, row("g_qk_k"), True)
            dve.sem_inc(S["key_ready"], 1)
            ada()
            qk_norm(qry, NT, ssq, vq, tq, rq, gqs[:], False)
            dve.sem_inc(S["qry_ready"], 1)
            ada()
            dve.wait_ge(S["qe_ready"], 1)
            for k, (d, t) in enumerate(combos):
                for b in range(2):
                    last = V.tensor_scalar(kend[:, k, b, :], decay_m[:, d * 2 + b, t * P:(t + 1) * P],
                                           gex[:, 1, d * 6 + b * 3 + t:d * 6 + b * 3 + t + 1], None, ALU.mult)
            last.then_inc(S["kend_ready"], 1)
            ada(2)
            for h in range(MH):
                i = take(f"keyT{h}")
                freed(V.tensor_copy(keyT[:, h, :], i[0:QK, :]))
            for h in range(MH):
                i = take(f"qryT{h}")
                freed(V.tensor_copy(qryT[:, h, :], i[0:QK, 0:TOK]))
            dve.wait_ge(S["proj_done"], proj_no["s0"] + 1)
            V.tensor_reduce(nmax[:, 0, :], pbank("s0").rearrange("p (h k) -> p h k", h=MH), AX.X, ALU.max, negate=True)\
                .then_inc(S["max_ready"], 1)

            def maxima(t):
                for h in range(MH):
                    dve.wait_ge(S["proj_done"], proj_no[f"s{t}{h}"] + 1)
                    V.tensor_reduce(nmax[:, t, h:h + 1], pbank(f"s{t}{h}", TOK), AX.X, ALU.max, negate=True)\
                        .then_inc(S["max_ready"], 1)

            def gla_masks(t):
                if t:
                    dve.wait_ge(S["misc_done"], misc_no[f"o{t - 1}"] + 1)
                m = tc("before")[:, 0:1]
                for par in range(2):
                    i = take(f"A{t}{par}").rearrange("p (a d j) -> p a d j", a=2, d=2)
                    masks = tconst[:, TCW["before"][0]:TCW["before"][0] + 2 * P].rearrange("p (d j) -> p d j", d=2)
                    freed(V.tensor_tensor(attn[:, par], i, masks.unsqueeze(1).to_broadcast([P, 2, 2, P]), ALU.mult))

            def gla_take(t):
                i = take(f"o{t}")
                freed(V.tensor_copy(mixed[:, t, 0:512], i))

            def prob_take(t):
                if t == 2:
                    dve.wait_ge(S["misc_done"], misc_no["pv1"] + 1)
                for h in range(MH):
                    i = take(f"p{t}T{h}")
                    freed(V.tensor_copy(probT[:, h].rearrange("p k q -> p (k q)"), i[:, 0:TOK]))

            def pv_take(t):
                dve.wait_ge(S["prob_ready"], MH + t * MH)
                own(V.reciprocal(rden[:, t, :], psum_p[:, t, :]))
                i = take(f"pv{t}").rearrange("p (h w) -> p h w", h=MH)
                freed(V.tensor_tensor(mixed[:, t, 512:].rearrange("p (h w) -> p h w", h=MH), i,
                                      rden[:, t, :].unsqueeze(2).to_broadcast([P, MH, VD]), ALU.mult))

            maxima(1)
            gla_masks(0)
            ada()
            for n in range(2):
                i = take(f"kendT{n}")
                freed(V.tensor_copy(kendT[:, 2 * n:2 * n + 2].rearrange("p k b j -> p (k b j)"), i))
            ada()
            for n in range(2):
                i = take(f"U{n}")
                freed(V.tensor_copy(state1[:, 2 * n:2 * n + 2].rearrange("p k b j -> p (k b j)"), i))
            dve.wait_ge(S["state_in"], 32)
            dve.wait_ge(S["misc_sb"], misc_no["U1"] + 1)
            dve.wait_ge(S["zero_ready"], 1)

            def g(kind, d, b, t):
                k = d * 6 + b * 3 + t
                return gex[:, kind, k:k + 1]

            for d in range(2):
                near, far = (1, 2) if d == 0 else (2, 1)
                for b in range(2):
                    own(V.scalar_tensor_tensor(state1[:, 2 + d, b, :], state0[:, d, b, :], g(2, d, b, near), state1[:, 2 + d, b, :],
                                               ALU.mult, ALU.add))
                    for hh in range(2):
                        r = slice(hh * GDK, (hh + 1) * GDK)
                        V.tensor_scalar(stateP[r, near - 1, d, 2 * b + hh, :], state0[r, d, b, :], g(0, d, b, near)[r], None, ALU.mult)
                        last = V.tensor_scalar(stateP[r, far - 1, d, 2 * b + hh, :], state1[r, 2 + d, b, :], g(0, d, b, far)[r], None, ALU.mult)
            last.then_inc(S["smp_ready"], 2)
            i = take("p0T")
            freed(V.tensor_copy(prob0T[:].rearrange("p h q -> p (h q)"), i))
            ada()
            gla_take(0)
            prob_take(1)
            ada()
            gla_masks(1)
            pv_take(0)
            pv_take(1)
            maxima(2)
            gla_take(1)
            ada(2)
            dve.wait_ge(S["silu_g"], 2)
            own(V.tensor_scalar(gexp[:], gexp[:], 1.0, None, ALU.add))
            V.reciprocal(gexp[:], gexp[:]).then_inc(S["g1_ready"], 1)
            prob_take(2)
            gla_masks(2)
            ada()
            pv_take(2)
            gla_take(2)
            dve.wait_ge(S["misc_sb"], misc_no["o2"] + 1)
            og = mixed[:, :, 0:512].rearrange("p t (h w) -> p t h w", h=GH)
            for t in range(NT):
                own(V.tensor_tensor(osq[:, 0:512], mixed[:, t, 0:512], mixed[:, t, 0:512], ALU.mult))
                own(V.tensor_reduce(sso[:, t, :], osq[:, 0:512].rearrange("p (h w) -> p h w", h=GH), AX.X, ALU.add))
            V.tensor_scalar(vo, sso, 1.0 / GDV, EPS, ALU.mult, ALU.add).then_inc(S["rn_in"], 1)
            root(vo, to, ro)
            dve.wait_ge(S["mix_ready"], 1)
            for t in range(NT):
                own(V.tensor_tensor(og[:, t], og[:, t], ro[:, t, :].unsqueeze(2).to_broadcast([P, GH, GDV]), ALU.mult))
                V.tensor_tensor(mixed[:, t, 0:512], mixed[:, t, 0:512], g_sb[:, t, :], ALU.mult).then_inc(S["mix_done"], 1)
            ada(NADA)
            def mixed_take(t):
                for n in range(2):
                    i = take(f"mT{t}{n}").rearrange("p (c j) -> p c j", c=4)
                    freed(V.tensor_copy(mixedT[:, 4 * n:4 * n + 4, t * P:(t + 1) * P], i))

            def residual(t):
                s = min(t, 1)
                for n in range(2):
                    h = slice(n * 512, (n + 1) * 512)
                    i = take(f"wo{t}{n}")
                    freed(V.tensor_tensor(xtmp[:, h], i, gt1[:, s, h], ALU.mult))
                    dve.wait_ge(S["misc_sb"], misc_no[f"wo{t}{n}"] + 1)
                    last = V.tensor_tensor(x1[:, t, h], x1[:, t, h], xtmp[:, h], ALU.add)
                last.then_inc(S["x1_ready"], 1)

            def norm2(t):
                s = min(t, 1)
                r = r3[:, t:t + 1]
                dve.wait_ge(S["sq_done"], t + 1)
                V.tensor_scalar(v3[:, t:t + 1], ss3[:, t:t + 1], 1.0 / D, EPS, ALU.mult, ALU.add).then_inc(S["rn_in"], 1)
                root(v3[:, t:t + 1], t3[:, t:t + 1], r)
                own(V.scalar_tensor_tensor(h2[:, t], x1[:, t], r, mul2[:, s], ALU.mult, ALU.mult))
                V.tensor_tensor(h2[:, t], h2[:, t], add2[:, s], ALU.add).then_inc(S["h2_ready"], 1)

            dve.wait_ge(S["x1_in"], 32)
            dve.wait_ge(S["proj_sb"], proj_no["b011"] + 1)
            mixed_take(0)
            residual(0)
            mixed_take(1)
            dve.wait_ge(S["mod_rows"], 1)
            norm2(0)
            residual(1)
            mixed_take(2)
            norm2(1)
            residual(2)
            norm2(2)

            dve.wait_ge(S["gt2_out"], 16)
            V.tensor_copy(strictb, strict)
            V.tensor_copy(onesb, ones)
            V.tensor_copy(identb[:], ident)
            dve.wait_ge(S["score_ready"], NT)
            own(V.tensor_tensor(select, score, row("b_router").unsqueeze(1).to_broadcast([P, NT, NE]), ALU.add))
            for k in range(NT * NG):
                last = V.max(top2[:, k, :], select[:, k // NG, k % NG * 8:k % NG * 8 + 8])
            own(last)
            gs = gscore.rearrange("p t g -> p (t g)")
            own(V.tensor_tensor(gs.unsqueeze(2), top2[:, :, 0:1], top2[:, :, 1:2], ALU.add))
            other = gscore.unsqueeze(2).to_broadcast([P, NT, NG, NG])
            self_ = gscore.unsqueeze(3).to_broadcast([P, NT, NG, NG])
            V.tensor_tensor(gcmp, other, self_, ALU.is_gt)
            own(V.tensor_tensor(gcmp2, other, self_, ALU.is_equal))
            own(V.tensor_tensor(gcmp2.rearrange("p t g h -> p t (g h)"), gcmp2.rearrange("p t g h -> p t (g h)"),
                                tc("earlier").unsqueeze(1).to_broadcast([P, NT, NG * NG]), ALU.mult))
            own(V.tensor_tensor(gcmp, gcmp, gcmp2, ALU.add))
            gr = grank.rearrange("p t g -> p (t g)")
            own(V.tensor_reduce(gr, gcmp.rearrange("p t g h -> p (t g) h"), AX.X, ALU.add))
            gm = gmask.rearrange("p t g -> p (t g)")
            own(V.tensor_scalar(gm, gr, float(TOPG), 1.0, ALU.is_lt, ALU.subtract))
            s3 = select.rearrange("p t (g e) -> p (t g) e", e=8)
            own(V.scalar_tensor_tensor(s3, gm.unsqueeze(2).to_broadcast([P, NT * NG, 8]), 1e30, s3, ALU.mult, ALU.add))
            for t in range(NT):
                last = V.max(top8[:, t, :], select[:, t, :])
            own(last)
            for t in range(NT):
                last = V.match_replace(picked[:, t, :], top8[:, t, :], select[:, t, :], 2e30)
            own(last)
            own(V.tensor_scalar(picked, picked, 1e30, None, ALU.is_ge))
            V.tensor_copy(maskb, picked).then_inc(S["mask_ready"], 1)
            own(V.tensor_tensor(weight, score, picked, ALU.mult))
            own(V.tensor_reduce(wsum, weight, AX.X, ALU.add))
            own(V.reciprocal(wsum, wsum))
            own(V.scalar_tensor_tensor(weight, weight, SCALE_OUT, wsum.unsqueeze(2).to_broadcast([P, NT, NE]), ALU.mult, ALU.mult))

            def shared_act(t):
                dve.wait_ge(S["sh_sil_ready"], t + 1)
                i = take(f"sg{t}")
                freed(V.tensor_tensor(sh_a[t][:], i[:, DE:], sh_sil[:], ALU.mult))
                dve.wait_ge(S["misc_sb"], misc_no[f"sg{t}"] + 1)
                dve.sem_inc(S["sh_a_ready"], 1)

            shared_act(0)
            shared_act(1)
            i = take("pos")
            freed(V.scalar_tensor_tensor(posp, i[:, 0:NT * NE].rearrange("p (t e) -> p t e", t=NT), 1.0, picked, ALU.add, ALU.mult))
            i = take("cnt")
            freed(V.tensor_copy(cnt[0:NE], i[0:NE, 0:1]))
            own(V.tensor_scalar(thr[0:NE], tc("over")[0:NE, 1:6], float(SLOT), None, ALU.mult))
            dve.wait_ge(S["misc_sb"], misc_no["cnt"] + 1)
            own(V.tensor_scalar(cmpc[0:NE], thr[0:NE], cnt[0:NE], None, ALU.is_lt))
            V.tensor_reduce(nov[0:NE], cmpc[0:NE], AX.X, ALU.add).then_inc(S["cnt_sb"], 1)
            dve.wait_ge(S["cnt_sb"], 1)
            i = take("start")
            freed(V.tensor_copy(start[0:NE], i[0:NE, 0:1]))
            dve.wait_ge(S["misc_sb"], misc_no["start"] + 1)
            own(V.tensor_tensor(end[0:NE], start[0:NE], nov[0:NE], ALU.add))
            ov = tc("over")[0:NE]
            own(V.tensor_scalar(owner[0:NE], ov, start[0:NE], None, ALU.is_ge))
            own(V.tensor_scalar(owner2[0:NE], ov, end[0:NE], None, ALU.is_lt))
            own(V.tensor_tensor(owner[0:NE], owner[0:NE], owner2[0:NE], ALU.mult))
            own(V.tensor_scalar(offs[0:NE], ov, start[0:NE], 1.0, ALU.subtract, ALU.add))
            V.scalar_tensor_tensor(offs[0:NE], offs[0:NE], float(SLOT), owner[0:NE], ALU.mult, ALU.mult).then_inc(S["owner_ready"], 1)
            shared_act(2)
            i = take("tabP")
            freed(V.tensor_copy(poT[0:NE].rearrange("p t j -> p (t j)"), i[0:NE, 0:TOK]))
            i = take("tabG")
            freed(V.tensor_copy(gaT[0:NE].rearrange("p t j -> p (t j)"), i[0:NE, 0:TOK]))
            i = take("tabO")
            own(V.tensor_copy(offrow, i[:, 0:NOVER]))
            own(V.tensor_scalar(grow, tc("over")[:, 0:NOVER // (2 * JG)], float(2 * JG), i[:, 2 * NOVER:2 * NOVER + 1], ALU.mult, ALU.is_lt))
            own(V.tensor_copy(erow[:, NE:NJ], i[:, NOVER:2 * NOVER]))
            freed(V.memset(erow[:, NJ:], 0.0))
            own(V.tensor_copy(erow[:, 0:NE], slotrow[:, 0:NE]))
            own(V.tensor_reduce(gcount, grow, AX.X, ALU.add))
            own(V.tensor_scalar(gcount, gcount, float(NE // (2 * JG)), None, ALU.add))
            V.tensor_copy(jobs[0:1, NJP:NJP + 1], gcount[0:1])
            V.tensor_copy(jobs[0:1, 0:NJP], erow[0:1])
            i = take("tabJ")
            own(V.tensor_scalar(posj[:, :, 0:NE], posp, -1.0, None, ALU.add))
            own(V.scalar_tensor_tensor(posj[:, :, NE:NJ], i[:, 0:NT * NOVER].rearrange("p (t j) -> p t j", t=NT), -1.0,
                                       offrow.unsqueeze(1).to_broadcast([P, NT, NOVER]), ALU.add, ALU.subtract))
            V.memset(posj[:, :, NJ:], -1.0)
            V.tensor_copy(gjob[:, :, 0:NE], weight)
            V.memset(gjob[:, :, NJ:], 0.0)
            freed(V.tensor_copy(gjob[:, :, NE:NJ], i[:, NT * NOVER:2 * NT * NOVER].rearrange("p (t j) -> p t j", t=NT)))
            dve.wait_ge(S["misc_sb"], misc_no["tabJ"] + 1)
            own(V.tensor_copy(gparts[:, :, :, 0], gjob))
            own(V.tensor_tensor(gjob, gjob, gparts[:, :, :, 0], ALU.subtract))
            own(V.tensor_copy(gparts[:, :, :, 1], gjob))
            own(V.tensor_tensor(gjob, gjob, gparts[:, :, :, 1], ALU.subtract))
            own(V.tensor_copy(gparts[:, :, :, 2], gjob))
            dve.sem_inc(S["jobs_ready"], 1)
            dve.wait_ge(S["h2s_ready"], 1)
            for t in range(NT):
                i = take(f"sa{t}")
                if t:
                    dve.wait_ge(S["misc_done"], misc_no[f"sd{t - 1}1"] + 1)
                freed(V.tensor_copy(sh_aT[:].rearrange("p f j -> p (f j)"), i[:, 0:2 * P]))
                for n in range(2):
                    i = take(f"sd{t}{n}")
                    freed(V.tensor_copy(acc[:, t, n * 512:(n + 1) * 512], i))
            dve.wait_ge(S["misc_sb"], len(misc))
            dve.sem_inc(S["shared_done"], 1)

            dve.wait_ge(S["x1_out"], 16 * NT)
            for s, n in (("lo_gu_dve", 2), ("lo_d4", 2), ("gu_sum", 2), ("a_ready", 1), ("al_done", 1), ("y_sum", 2),
                         ("acc_done", 6)):
                dve.sem_inc(S[s], n)
            V.memset(place[:].bitcast(F32), 0.0).then_inc(S["zeroed"], 1)
            V.memset(yt, 0.0).then_inc(S["zeroed"], 1)

            def low_gu(g, j, u):
                dve.wait_ge(S["hi_gu"], 4 * (JG * g + j) + u + 1)
                three = lambda w: w.rearrange("p (m c) -> p m c", m=2)
                V.tensor_tensor(three(wl[u][:]), raw_gu[j % 2][:, :, 2 * u:2 * u + 2, :].rearrange("p m c n -> p m (c n)"),
                                three(wh[u][:].bitcast(F32)), ALU.subtract).then_inc(S["lo_gu_dve"], 1)

            def split_dn(g, j):
                dve.wait_ge(raw_dn_in[j % 2], 16 * (2 * g + j // 2 + 1))
                dve.wait_ge(S["dn_used"], 2 * (JG * g + j) + 4)
                V.tensor_copy(wh[5][:], raw_dn[j % 2][:, 1]).then_inc(S["hi_d5"], 1)
                dve.wait_ge(S["hi_d4"], JG * g + j + 1)
                V.tensor_tensor(wl[4][:], raw_dn[j % 2][:, 0], wh[4][:].bitcast(F32), ALU.subtract).then_inc(S["lo_d4"], 1)

            def sum_up(g, j):
                dve.wait_ge(S["half_up"], JG * g + j + 1)
                V.tensor_tensor(gu, ps[HI, j % 2, :], gu, ALU.add).then_inc(S["gu_sum"], 1)

            def gated(g, j):
                dve.wait_ge(S["silu_done"], JG * g + j + 1)
                dve.wait_ge(S["aT_done"], JG * g + j + 1)
                V.scalar_tensor_tensor(act_a[j % 2][HI], gu[:, DE:], gslot[HI, j % JG:j % JG + 1], sil, ALU.mult, ALU.mult)\
                    .then_inc(S["a_ready"], 1)

            def low_a(g, j):
                dve.wait_ge(S["ah_done"], JG * g + j + 1)
                a = ast[j % 2]
                V.tensor_tensor(a[:, :, 1, :], ps[:, 4, 0:2 * SLOT].rearrange("p (f s) -> p f s", f=2),
                                a[:].bitcast(F32)[:, :, 0, :], ALU.subtract).then_inc(S["al_done"], 1)

            def sum_y(g, j):
                for n in range(2):
                    dve.wait_ge(S["y_half"], 2 * (JG * g + j) + n + 1)
                    h = slice(n * 512, (n + 1) * 512)
                    V.tensor_tensor(yt[:, h], ps[0:SLOT, 2 + n, :], yt[:, h], ALU.add).then_inc(S["y_sum"], 1)

            def low_y(g, j):
                dve.wait_ge(S["yh_done"], JG * g + j + 2)
                V.tensor_tensor(ys[HI, j % JG, 0:512], yt[:, 0:512], ys[:].bitcast(F32)[0:SLOT, j % JG, 0:512], ALU.subtract)                    .then_inc(S["yl_dve"], 1)

            def add_scattered(g, m):
                dve.wait_ge(S["scatter_done"], 6 * g + m + 1)
                dve.wait_ge(S["acc_done"], 6 * g + m + 1)
                a = acc[:, m // 2, m % 2 * 512:(m % 2 + 1) * 512]
                V.tensor_tensor(a, a, ps[:, 6 + m % 2, :], ALU.add).then_inc(S["acc_done"], 1)

            def pick_slots(cols_):
                i = slotrow.rearrange("p (j s) -> p j s", j=JG).unsqueeze(1).to_broadcast([P, NT, JG, SLOT])
                k = cols_.unsqueeze(3).to_broadcast([P, NT, JG, SLOT])
                return i, k

            def tokens(g, c):
                dve.wait_ge(S["gather_done"], NC * (g + 1) + c + 1)
                V.tensor_copy(xs[(half + 1) % 2][:, :, c], ps[:, 7, :].rearrange("p (z j s) -> p j z s", z=2, j=JG)).then_inc(S["xs_dve"], 1)

            def gates(n):
                dve.wait_ge(S["place_mm"], n)
                V.tensor_reduce(gslot[HI, :], ps[0:SLOT, 5, 0:4 * JG].rearrange("p (j k) -> p j k", k=4)[:, :, 0:3],
                                AX.X, ALU.add).then_inc(S["b5_sb"], 1)

            pick4 = pick[:].rearrange("p t (j s) -> p t j s", j=JG)
            i, k = pick_slots(posj[:, :, 0:JG])
            V.tensor_tensor(pick4, i, k, ALU.is_equal).then_inc(S["pick_ready"], 1)
            V.tensor_tensor(pickb[:], i, k, ALU.is_equal).then_inc(S["pickb_ready"], 1)
            low_gu(0, 0, 0)
            low_gu(0, 0, 2)
            for c in range(1, NC, 2):
                dve.wait_ge(S["gather_done"], c + 1)
                V.tensor_copy(xs[0][:, :, c], ps[:, 7, :].rearrange("p (z j s) -> p j z s", z=2, j=JG)).then_inc(S["xs_dve"], 1)
            gates(1)
            i, k = pick_slots(posj[:, :, JG:2 * JG])
            dve.wait_ge(S["gather_done"], NC)
            V.tensor_tensor(pick4, i, k, ALU.is_equal).then_inc(S["pick_ready"], 1)
            low_gu(0, 1, 0)
            low_gu(0, 1, 2)
            sum_up(0, 0)
            dve.wait_ge(S["b5_sb"], 1)
            gated(0, 0)
            split_dn(0, 0)
            n_rounds = dve.value_load(jobs[0:1, NJP:NJP + 1], min_val=NE // (2 * JG), max_val=NJ // (2 * JG))
            with dve.Fori(0, n_rounds) as r:
                for half in range(2):
                    g = 2 * r + half
                    for j in range(1, JG + 1):
                        low_a(g, j - 1)
                        if j == 1:
                            low_y(g, j - 2)
                        low_gu(g, j + 1, 0)
                        if j > 1:
                            low_y(g, j - 2)
                        low_gu(g, j + 1, 2)
                        sum_up(g, j)
                        if j == JG:
                            dve.wait_ge(S["b5_sb"], 5 * g + 6)
                        if j in (2, 3):
                            tokens(g, 4 * j - 7)
                        gated(g, j)
                        if j == 1:
                            add_scattered(g, 0)
                            add_scattered(g, 1)
                            add_scattered(g, 2)
                        split_dn(g, j)
                        if j in (2, 3):
                            tokens(g, 4 * j - 5)
                        if j == 1:
                            add_scattered(g, 3)
                        sum_y(g, j - 1)
                        if j == 1:
                            for m in range(4, 6):
                                add_scattered(g, m)
                        if j == 3:
                            i, k = pick_slots(posj[:, :, bass.ds(g * JG + JG, JG)])
                            dve.wait_ge(S["place_mm"], 5 * g + 5)
                            V.tensor_tensor(pickb[:], i, k, ALU.is_equal).then_inc(S["pickb_ready"], 1)
                            dve.wait_ge(S["a_ready"], JG * g + JG + 1)
                            gates(5 * g + 6)
                        if j == JG:
                            i, k = pick_slots(posj[:, :, bass.ds(g * JG + 2 * JG, JG)])
                            dve.wait_ge(S["gather_done"], NC * g + 2 * NC)
                            V.tensor_tensor(pick4, i, k, ALU.is_equal).then_inc(S["pick_ready"], 1)
            low_y(2 * n_rounds, -1)
            for m in range(6):
                add_scattered(2 * n_rounds, m)
            dve.wait_ge(S["acc_done"], 12 * n_rounds + 12)
            dve.wait_ge(S["tail_in"], 48)
            for t in range(NT):
                own(V.tensor_tensor(acc[:, t], acc[:, t], gt2[:, min(t, 1)], ALU.mult))
                V.tensor_tensor(x1b[:, t], x1b[:, t], acc[:, t], ALU.add).then_inc(S["y_ready"], 1)

        @block.gpsimd
        def _(pool):
            G = nc.gpsimd
            pool.wait_ge(S["cache_in"], 32)
            pool.wait_ge(S["proj_sb"], proj_no["mla2"] + 1)
            for t in range(NT):
                i = G.tensor_copy(krope[:, t, :], mla[:, t, QL + KL:])
                i.then_inc(S["pool_chain"], 1)
            pool.wait_ge(S["pool_chain"], NT)
            for t in range(4):
                i = G.tensor_copy(key[:, t, :, NOPE:], krope[:, t, :].unsqueeze(1).to_broadcast([P, MH, ROPE]))
                i.then_inc(S["pool_chain"], 1)
            pool.wait_ge(S["pool_chain"], NT + 4)
            pool.sem_inc(S["krope_ready"], 1)
            pool.wait_ge(S["qe_ready"], 1)
            G.memset(stateP[:], 0.0).then_inc(S["zero_ready"], 1)
            pool.wait_ge(S["g1_ready"], 1)
            pool.wait_ge(S["proj_sb"], proj_no["g2"] + 1)
            G.tensor_tensor(g_sb[:], g_sb[:], gexp[:], ALU.mult).then_inc(S["pool_chain"], 1)
            pool.wait_ge(S["pool_chain"], NT + 5)
            gw = g_sb[:].rearrange("p t (h w) -> p (t h) w", h=GH)
            G.tensor_tensor(gw, gw, row("g_gla_out").unsqueeze(1).to_broadcast([P, NT * GH, GDV]), ALU.mult)\
                .then_inc(S["mix_ready"], 1)
            pool.wait_ge(S["proj_sb"], proj_no["b211"] + 1)
            pool.wait_ge(S["g2_in"], 16)
            G.tensor_tensor(mul2[:], mul2[:], g2row[:].unsqueeze(1).to_broadcast([P, 2, D]), ALU.mult).then_inc(S["mod_rows"], 1)
            for t in range(NT):
                pool.wait_ge(S["h2h_ready"], t + 1)
                G.tensor_tensor(h2l[:, t], h2[:, t].rearrange("p (j c) -> p c j", c=NC), h2h[:].bitcast(F32)[:, t], ALU.subtract)\
                    .then_inc(S["h2l_ready"], 1)
            pool.wait_ge(S["h2l_ready"], NT)
            pool.sem_inc(S["h2s_ready"], 1)

            pool.wait_ge(S["shared_done"], 1)
            pool.sem_inc(S["lo_gu_pool"], 2)
            pool.sem_inc(S["lo_d5"], 2)

            def low_gu(g, j):
                for u in (1, 3):
                    pool.wait_ge(S["hi_gu"], 4 * (JG * g + j) + u + 1)
                    three = lambda w: w.rearrange("p (m c) -> p m c", m=2)
                    G.tensor_tensor(three(wl[u][:]), raw_gu[j % 2][:, :, 2 * u:2 * u + 2, :].rearrange("p m c n -> p m (c n)"),
                                    three(wh[u][:].bitcast(F32)), ALU.subtract).then_inc(S["lo_gu_pool"], 1)

            def low_dn(g, j):
                pool.wait_ge(S["hi_d5"], JG * g + j + 1)
                G.tensor_tensor(wl[5][:], raw_dn[j % 2][:, 1], wh[5][:].bitcast(F32), ALU.subtract).then_inc(S["lo_d5"], 1)

            def low_y(g, j):
                pool.wait_ge(S["lo_d5"], JG * g + j + 4)
                pool.wait_ge(S["yh_done"], JG * g + j + 2)
                G.tensor_tensor(ys[HI, j % JG, 512:], yt[:, 512:], ys[:].bitcast(F32)[0:SLOT, j % JG, 512:], ALU.subtract)                    .then_inc(S["yl_pool"], 1)
                pool.wait_ge(S["yl_pool"], JG * g + j + 2)

            low_gu(0, 0)
            pool.wait_ge(S["x1_out"], 16 * NT)
            G.memset(ys[:].bitcast(F32), 0.0).then_inc(S["zeroed"], 1)
            low_gu(0, 1)
            low_dn(0, 0)
            n_rounds = pool.value_load(jobs[0:1, NJP:NJP + 1], min_val=NE // (2 * JG), max_val=NJ // (2 * JG))
            with pool.Fori(0, n_rounds) as r:
                for half in range(2):
                    g = 2 * r + half
                    for j in range(1, JG + 1):
                        low_y(g, j - 2)
                        low_gu(g, j + 1)
                        low_dn(g, j)
            low_y(2 * n_rounds, -1)


_OUTS = [("y_prompt", (1, P, D)), ("y_sample", (1, 2 * P, D)), ("new_fwd", (1, 1, GH, GDK, GDV)),
         ("new_bwd", (1, 1, GH, GDK, GDV)), ("new_ckv", (1, 1, P, KL)), ("new_krope", (1, 1, P, ROPE))]
_WHOLE = ("x_prompt", "x_sample", "state_gla_fwd", "state_gla_bwd", "cache_mla_ckv", "cache_mla_krope", "w_ada", "b_ada",
          "g_norm2", "w_in", "w_uq", "w_ukv", "w_out", "w_router", "w_exp_gate", "w_exp_up", "w_exp_down", "w_sh_gate",
          "w_sh_up", "w_sh_down")


def kernel(**inputs):
    import numpy as _np
    import concourse.bacc as _bacc
    from concourse import mybir as _mybir
    from concourse.bass_utils import run_bass_kernel_spmd as _run

    a = {n: _np.ascontiguousarray(v) for n, v in inputs.items()}
    arrays = {n: a[n] for n in _WHOLE}
    pc = lambda v: v.reshape(P, NC)
    arrays["c_cols"] = _np.ascontiguousarray(_np.concatenate(
        [pc(a["c_ctx"]), pc(a["c"][0]), pc(a["g_norm1"][0]), pc(a["b_ada"][0, 0:D]), pc(a["b_ada"][0, D:2 * D]),
         a["b_gk_fwd"][0].reshape(2, P).T, a["b_gk_bwd"][0].reshape(2, P).T], 1))
    arrays["c_rows"] = _np.concatenate([a[n][0] for n in ("g_gla_out", "g_q_lora", "g_kv_lora", "g_qk_q", "g_qk_k",
                                                          "b_router")])[None]
    gates = _np.zeros((32, 2, 2, P), _np.float32)
    gates[0:16, 0] = a["w_gk_fwd"][0].reshape(16, 2, P)
    gates[16:32, 1] = a["w_gk_bwd"][0].reshape(16, 2, P)
    arrays["c_wgk"] = gates
    const = shape_constants()
    part = lambda n: const[:, CW[n][0]:CW[n][0] + CW[n][1]]
    kept = ("ident", "strict", "ones", "slot")
    arrays["c_keep"] = _np.ascontiguousarray(_np.concatenate([part(n) for n in kept], 1))
    arrays["c_trunk"] = _np.ascontiguousarray(_np.concatenate([part(n) for n in CW if n not in kept], 1))

    nc = _bacc.Bacc("TRN2", target_bir_lowering=False, num_devices=1)
    A = {n: nc.dram_tensor(f"in_{n}", v.shape, _mybir.dt.from_np(v.dtype), kind="ExternalInput").ap()
         for n, v in arrays.items()}
    O = {n: nc.dram_tensor(f"out_{n}", s, _mybir.dt.float32, kind="ExternalOutput").ap() for n, s in _OUTS}
    build(nc, A, O)
    r = _run(nc, [{f"in_{n}": v for n, v in arrays.items()}], core_ids=[0])
    return tuple(r.results[0][f"out_{n}"] for n, _ in _OUTS)
```
